# Optimizing a Trainium2 kernel written in Bass

```python
import math
import jax, jax.numpy as jnp
from jax import lax
import numpy as np

D_MODEL = 1024
BATCH = 1
SEQ = 256
DEPTH = 2

GRID_W = 64
CTX_LEN = 256
HEAD_DIM = 64
A_Q_HEADS = 8
A_KV_HEADS = 2
B_HEADS = 4
B_KEY_DIM = 128
B_VAL_DIM = 128
HGRN_CHUNK = 32
C_HEADS = 16
NA_ROWS = 8
NA_COLS = 16
D_FF = 2816
CONV_W = 3

ROPE_THETA = 10000.0
Q_BLOCK = 128
EPS = 1e-6
ATTN_SCALE = HEAD_DIM ** -0.5
HGRN_SCALE = B_KEY_DIM ** -0.5

N_EVEN = (DEPTH + 1) // 2
N_ODD = DEPTH // 2
A_Q_W = A_Q_HEADS * HEAD_DIM
A_KV_W = A_KV_HEADS * HEAD_DIM
B_K_W = B_HEADS * B_KEY_DIM
B_V_W = B_HEADS * B_VAL_DIM
EVEN_IN_W = A_Q_W + 2 * A_KV_W + 3 * B_K_W + 2 * B_V_W
EVEN_SPLITS = (A_Q_W, A_Q_W + A_KV_W, A_Q_W + 2 * A_KV_W, A_Q_W + 2 * A_KV_W + B_K_W,
               A_Q_W + 2 * A_KV_W + 2 * B_K_W, A_Q_W + 2 * A_KV_W + 3 * B_K_W,
               A_Q_W + 2 * A_KV_W + 3 * B_K_W + B_V_W)
EVEN_OUT_W = A_Q_W + B_V_W
C_W = C_HEADS * HEAD_DIM


def rms_norm(x, w):
    xf = x.astype(jnp.float32)
    y = xf * lax.rsqrt(jnp.mean(xf * xf, axis=-1, keepdims=True) + EPS)
    return (y * w.astype(jnp.float32)).astype(x.dtype)

def axial_rope_tables(n_tokens):
    t = jnp.arange(n_tokens)
    row = (t // GRID_W).astype(jnp.float32)
    col = (t % GRID_W).astype(jnp.float32)
    n_freq = HEAD_DIM // 4
    inv_freq = ROPE_THETA ** (-jnp.arange(n_freq, dtype=jnp.float32) / n_freq)
    ang = jnp.concatenate([row[:, None] * inv_freq, col[:, None] * inv_freq], axis=-1)
    return jnp.cos(ang), jnp.sin(ang)

def apply_rope(x, cos, sin):
    x1, x2 = jnp.split(x, 2, axis=-1)
    c = cos[None, :, None, :].astype(x.dtype)
    s = sin[None, :, None, :].astype(x.dtype)
    return jnp.concatenate([x1 * c - x2 * s, x1 * s + x2 * c], axis=-1)

def gqa_axial_attention(q_lat, k_lat, v_lat, q_ctx, k_ctx, v_ctx, q_norm_w, k_norm_w, with_ctx_out):
    B_, L = q_lat.shape[:2]
    n_ctx = q_ctx.shape[1]
    group = A_Q_HEADS // A_KV_HEADS
    q_lat, q_ctx = rms_norm(q_lat, q_norm_w), rms_norm(q_ctx, q_norm_w)
    k_lat, k_ctx = rms_norm(k_lat, k_norm_w), rms_norm(k_ctx, k_norm_w)
    cos, sin = axial_rope_tables(L)
    q_lat = apply_rope(q_lat, cos, sin)
    k_lat = apply_rope(k_lat, cos, sin)
    k_all = jnp.concatenate([k_ctx, k_lat], axis=1)
    v_all = jnp.concatenate([v_ctx, v_lat], axis=1)

    def attend(q, k, v):
        s = jnp.einsum("bqhgd,bkhd->bhgqk", q, k).astype(jnp.float32) * ATTN_SCALE
        p = jax.nn.softmax(s, axis=-1).astype(v.dtype)
        return jnp.einsum("bhgqk,bkhd->bqhgd", p, v)

    n_blk = L // Q_BLOCK
    q_blocks = q_lat.reshape(B_, n_blk, Q_BLOCK, A_KV_HEADS, group, HEAD_DIM).transpose(1, 0, 2, 3, 4, 5)
    o = lax.map(lambda qb: attend(qb, k_all, v_all), q_blocks)
    o_lat = o.transpose(1, 0, 2, 3, 4, 5).reshape(B_, L, A_Q_W)
    o_ctx = None
    if with_ctx_out:
        o_ctx = attend(q_ctx.reshape(B_, n_ctx, A_KV_HEADS, group, HEAD_DIM), k_ctx, v_ctx).reshape(B_, n_ctx, A_Q_W)
    return o_lat, o_ctx

def forget_gate(f_raw, lb):
    z = f_raw.astype(jnp.float32)
    log_f = jnp.logaddexp(jnp.log(lb), jnp.log1p(-lb) + jax.nn.log_sigmoid(z))
    k = (1.0 - lb) * jax.nn.sigmoid(-z)
    return k, log_f

def hgrn2_chunk_scan(q, k, log_f, v, s0):
    B_, L, H, dk = q.shape
    dv = v.shape[-1]
    n = L // HGRN_CHUNK

    def to_chunks(a):
        return a.reshape(B_, n, HGRN_CHUNK, H, a.shape[-1]).transpose(1, 0, 3, 2, 4)

    tri = jnp.tril(jnp.ones((HGRN_CHUNK, HGRN_CHUNK), dtype=bool))[None, None, :, :, None]

    def step(S, inp):
        qc, kc, gc, vc = inp
        b = jnp.cumsum(gc, axis=2)
        diff = b[:, :, :, None, :] - b[:, :, None, :, :]
        decay = jnp.exp(jnp.where(tri, diff, -jnp.inf))
        scores = jnp.einsum("bhtd,bhtsd,bhsd->bhts", qc, decay, kc)
        o = jnp.einsum("bhts,bhsv->bhtv", scores, vc) + jnp.einsum("bhtd,bhdv->bhtv", qc * jnp.exp(b), S)
        b_last = b[:, :, -1:, :]
        S_new = jnp.exp(b_last[:, :, 0, :])[..., None] * S + jnp.einsum("bhsd,bhsv->bhdv", kc * jnp.exp(b_last - b), vc)
        return S_new, o

    S, o = lax.scan(step, s0, (to_chunks(q), to_chunks(k), to_chunks(log_f), to_chunks(v)))
    o = o.transpose(1, 0, 3, 2, 4).reshape(B_, L, H, dv).astype(v.dtype)
    return o, S

def hgrn2_bidirectional(q_lat, f_lat, i_lat, q_ctx, f_ctx, i_ctx, lb):
    B_ = q_lat.shape[0]
    s0 = jnp.zeros((B_, B_HEADS, B_KEY_DIM, B_VAL_DIM), jnp.float32)
    o_lat, o_ctx = None, None
    for d in range(2):
        flip = (lambda a: a) if d == 0 else (lambda a: a[:, ::-1])
        k_l, lf_l = forget_gate(f_lat[d], lb[d])
        k_c, lf_c = forget_gate(f_ctx[d], lb[d])
        oc, s_ctx = hgrn2_chunk_scan(flip(q_ctx), flip(k_c), flip(lf_c), flip(i_ctx), s0)
        ol, _ = hgrn2_chunk_scan(flip(q_lat), flip(k_l), flip(lf_l), flip(i_lat), s_ctx)
        o_lat = flip(ol) if o_lat is None else o_lat + flip(ol)
        o_ctx = flip(oc) if o_ctx is None else o_ctx + flip(oc)
    return o_lat, o_ctx

def even_mixer(h_lat, h_ctx, w_in, w_out, q_norm_w, k_norm_w, lb, out_norm_w, with_ctx_out):
    def project(h):
        B_, n = h.shape[:2]
        aq, ak, av, bq, bff, bfb, bi, bg = jnp.split(h @ w_in, EVEN_SPLITS, axis=-1)
        bshape = (B_, n, B_HEADS, B_KEY_DIM)
        return (aq.reshape(B_, n, A_Q_HEADS, HEAD_DIM), ak.reshape(B_, n, A_KV_HEADS, HEAD_DIM),
                av.reshape(B_, n, A_KV_HEADS, HEAD_DIM), (jax.nn.silu(bq) * HGRN_SCALE).reshape(bshape),
                (bff.reshape(bshape), bfb.reshape(bshape)), bi.reshape(B_, n, B_HEADS, B_VAL_DIM), bg)

    aq_l, ak_l, av_l, bq_l, bf_l, bi_l, bg_l = project(h_lat)
    aq_c, ak_c, av_c, bq_c, bf_c, bi_c, bg_c = project(h_ctx)
    oa_lat, oa_ctx = gqa_axial_attention(aq_l, ak_l, av_l, aq_c, ak_c, av_c, q_norm_w, k_norm_w, with_ctx_out)
    ob_lat, ob_ctx = hgrn2_bidirectional(bq_l, bf_l, bi_l, bq_c, bf_c, bi_c, lb)

    def readout(o, g):
        B_, n = o.shape[:2]
        return (rms_norm(o, out_norm_w).reshape(B_, n, B_V_W) * jax.nn.silu(g)).astype(g.dtype)

    y_lat = jnp.concatenate([oa_lat, readout(ob_lat, bg_l)], axis=-1) @ w_out
    y_ctx = None
    if with_ctx_out:
        y_ctx = jnp.concatenate([oa_ctx, readout(ob_ctx, bg_c)], axis=-1) @ w_out
    return y_lat, y_ctx

def odd_mixer(h_lat, h_ctx, w_qkv, w_out, rpb, with_ctx_out):
    B_, L, _ = h_lat.shape
    n_ctx = h_ctx.shape[1]
    rows = L // GRID_W
    wr = min(NA_ROWS, rows)
    qkv = (h_lat @ w_qkv).reshape(B_, rows, GRID_W, 3, C_HEADS, HEAD_DIM)
    q, k, v = qkv[:, :, :, 0], qkv[:, :, :, 1], qkv[:, :, :, 2]
    qkv_c = (h_ctx @ w_qkv).reshape(B_, n_ctx, 3, C_HEADS, HEAD_DIM)
    q_c, k_c, v_c = qkv_c[:, :, 0], qkv_c[:, :, 1], qkv_c[:, :, 2]

    r_start = jnp.clip(jnp.arange(rows) - wr // 2, 0, rows - wr)
    c_start = jnp.clip(jnp.arange(GRID_W) - NA_COLS // 2, 0, GRID_W - NA_COLS)
    c_idx = c_start[:, None] + jnp.arange(NA_COLS)
    dx = c_idx - jnp.arange(GRID_W)[:, None] + (NA_COLS - 1)

    def row_block(inp):
        r, q_r = inp
        r0 = r_start[r]
        k_band = lax.dynamic_slice_in_dim(k, r0, wr, axis=1)
        v_band = lax.dynamic_slice_in_dim(v, r0, wr, axis=1)
        k_win = k_band[:, :, c_idx]
        v_win = v_band[:, :, c_idx]
        dy = r0 + jnp.arange(wr) - r + (NA_ROWS - 1)
        bias = rpb[:, dy[:, None, None], dx[None, :, :]].transpose(0, 2, 1, 3)
        s_loc = jnp.einsum("bqhd,brqjhd->bhqrj", q_r, k_win).astype(jnp.float32) * ATTN_SCALE
        s_loc = (s_loc + bias[None].astype(jnp.float32)).reshape(B_, C_HEADS, GRID_W, wr * NA_COLS)
        s_ctx = jnp.einsum("bqhd,bchd->bhqc", q_r, k_c).astype(jnp.float32) * ATTN_SCALE
        p = jax.nn.softmax(jnp.concatenate([s_loc, s_ctx], axis=-1), axis=-1).astype(v.dtype)
        p_loc = p[..., :wr * NA_COLS].reshape(B_, C_HEADS, GRID_W, wr, NA_COLS)
        p_ctx = p[..., wr * NA_COLS:]
        return jnp.einsum("bhqrj,brqjhd->bqhd", p_loc, v_win) + jnp.einsum("bhqc,bchd->bqhd", p_ctx, v_c)

    o = lax.map(row_block, (jnp.arange(rows), q.transpose(1, 0, 2, 3, 4)))
    y_lat = o.transpose(1, 0, 2, 3, 4).reshape(B_, L, C_W) @ w_out
    y_ctx = None
    if with_ctx_out:
        s = jnp.einsum("bqhd,bkhd->bhqk", q_c, k_c).astype(jnp.float32) * ATTN_SCALE
        p = jax.nn.softmax(s, axis=-1).astype(v_c.dtype)
        y_ctx = jnp.einsum("bhqk,bkhd->bqhd", p, v_c).reshape(B_, n_ctx, C_W) @ w_out
    return y_lat, y_ctx

def conv_ffn(h, w_up, conv_w, conv_b, w_down):
    u = h @ w_up
    u = lax.conv_general_dilated(u, conv_w[:, None, :], window_strides=(1,),
                                 padding=[(CONV_W // 2, CONV_W // 2)],
                                 dimension_numbers=("NWC", "WIO", "NWC"),
                                 feature_group_count=u.shape[-1]) + conv_b
    a, g = jnp.split(u, 2, axis=-1)
    return (jax.nn.silu(g) * a) @ w_down

def first_inputs(seed: int = 0) -> dict:
    key = jax.random.key(seed)
    ks = jax.random.split(key, 24)

    def nrm(k, shape, s):
        return jax.random.normal(k, shape, jnp.float32) * s

    return {
        "x": nrm(ks[0], (BATCH, SEQ, D_MODEL), 1.0),
        "c": nrm(ks[1], (BATCH, D_MODEL), 1.0),
        "ctx": nrm(ks[2], (BATCH, CTX_LEN, D_MODEL), 1.0),
        "c_ctx": nrm(ks[3], (D_MODEL,), 1.0),
        "w_mod": nrm(ks[4], (DEPTH, D_MODEL, 6 * D_MODEL), D_MODEL ** -0.5),
        "b_mod": nrm(ks[5], (DEPTH, 6 * D_MODEL), 0.02),
        "norm_pre_mix": 1.0 + nrm(ks[6], (DEPTH, D_MODEL), 0.1),
        "norm_post_mix": 1.0 + nrm(ks[7], (DEPTH, D_MODEL), 0.1),
        "norm_pre_ffn": 1.0 + nrm(ks[8], (DEPTH, D_MODEL), 0.1),
        "norm_post_ffn": 1.0 + nrm(ks[9], (DEPTH, D_MODEL), 0.1),
        "even_w_in": nrm(ks[10], (N_EVEN, D_MODEL, EVEN_IN_W), D_MODEL ** -0.5),
        "even_w_out": nrm(ks[11], (N_EVEN, EVEN_OUT_W, D_MODEL), EVEN_OUT_W ** -0.5),
        "even_q_norm": 1.0 + nrm(ks[12], (N_EVEN, HEAD_DIM), 0.1),
        "even_k_norm": 1.0 + nrm(ks[13], (N_EVEN, HEAD_DIM), 0.1),
        "hgrn_lb_logits": nrm(ks[14], (N_EVEN, 2, B_K_W), 1.0),
        "hgrn_out_norm": 1.0 + nrm(ks[15], (N_EVEN, B_VAL_DIM), 0.1),
        "odd_w_qkv": nrm(ks[16], (N_ODD, D_MODEL, 3 * C_W), D_MODEL ** -0.5),
        "odd_w_out": nrm(ks[17], (N_ODD, C_W, D_MODEL), C_W ** -0.5),
        "odd_rpb": nrm(ks[18], (N_ODD, C_HEADS, 2 * NA_ROWS - 1, 2 * NA_COLS - 1), 0.1),
        "ffn_w_up": nrm(ks[19], (DEPTH, D_MODEL, 2 * D_FF), D_MODEL ** -0.5),
        "ffn_conv_w": nrm(ks[20], (DEPTH, CONV_W, 2 * D_FF), CONV_W ** -0.5),
        "ffn_conv_b": nrm(ks[21], (DEPTH, 2 * D_FF), 0.02),
        "ffn_w_down": nrm(ks[22], (DEPTH, D_FF, D_MODEL), D_FF ** -0.5),
    }

def first_block(x, c, ctx, c_ctx, w_mod, b_mod, norm_pre_mix, norm_post_mix, norm_pre_ffn, norm_post_ffn,
              even_w_in, even_w_out, even_q_norm, even_k_norm, hgrn_lb_logits, hgrn_out_norm,
              odd_w_qkv, odd_w_out, odd_rpb, ffn_w_up, ffn_conv_w, ffn_conv_b, ffn_w_down):
    p_lb = jax.nn.softmax(hgrn_lb_logits.astype(jnp.float32), axis=0)
    lb_all = jnp.concatenate([jnp.zeros_like(p_lb[:1]), jnp.cumsum(p_lb[1:], axis=0)], axis=0)
    lb_all = lb_all.reshape(N_EVEN, 2, B_HEADS, B_KEY_DIM)

    for l in range(DEPTH):
        with_ctx_out = l < DEPTH - 1
        mod_lat = (jax.nn.silu(c) @ w_mod[l] + b_mod[l])[:, None, :]
        mod_ctx = (jax.nn.silu(c_ctx) @ w_mod[l] + b_mod[l])[None, None, :]
        sh1, sc1, g1, sh2, sc2, g2 = jnp.split(mod_lat, 6, axis=-1)
        sh1c, sc1c, g1c, sh2c, sc2c, g2c = jnp.split(mod_ctx, 6, axis=-1)

        h_lat = rms_norm(x, norm_pre_mix[l]) * (1.0 + sc1) + sh1
        h_ctx = rms_norm(ctx, norm_pre_mix[l]) * (1.0 + sc1c) + sh1c
        if l % 2 == 0:
            e = l // 2
            y_lat, y_ctx = even_mixer(h_lat, h_ctx, even_w_in[e], even_w_out[e], even_q_norm[e], even_k_norm[e],
                                      lb_all[e], hgrn_out_norm[e], with_ctx_out)
        else:
            o = l // 2
            y_lat, y_ctx = odd_mixer(h_lat, h_ctx, odd_w_qkv[o], odd_w_out[o], odd_rpb[o], with_ctx_out)
        x = x + g1 * rms_norm(y_lat, norm_post_mix[l])

        h_lat = rms_norm(x, norm_pre_ffn[l]) * (1.0 + sc2) + sh2
        x = x + g2 * rms_norm(conv_ffn(h_lat, ffn_w_up[l], ffn_conv_w[l], ffn_conv_b[l], ffn_w_down[l]), norm_post_ffn[l])
        if with_ctx_out:
            ctx = ctx + g1c * rms_norm(y_ctx, norm_post_mix[l])
            h_ctx = rms_norm(ctx, norm_pre_ffn[l]) * (1.0 + sc2c) + sh2c
            ctx = ctx + g2c * rms_norm(conv_ffn(h_ctx, ffn_w_up[l], ffn_conv_w[l], ffn_conv_b[l], ffn_w_down[l]), norm_post_ffn[l])
    return x


MOBA_HEAD_DIM = 128
MOBA_HEADS = D_MODEL // (2 * MOBA_HEAD_DIM)
MOBA_BLOCK = 256
MOBA_TOPK = 3
MOBA_QBLOCK = 32
GLA_DV = 128
GLA_HEADS = D_MODEL // (2 * GLA_DV)
GLA_DK = GLA_DV // 2
GLA_GATE_RANK = 16
GLA_GATE_NORM = 16.0
GLA_CHUNK = 64
GDN_DK = 128
GDN_DV = 128
GDN_HEADS = D_MODEL // GDN_DV
GDN_CONV = 4
GDN_CHUNK = 64
RPE_BUCKETS = 32
RPE_MAX_DIST = 2048
N_EXPERTS = 64
TOP_K = 6
N_GROUPS = 8
TOPK_GROUPS = 4
D_EXPERT = 256
D_SHARED = 256
ROUTED_SCALE = 2.5
MOE_BLOCK = 128
DEEPNORM_ALPHA = float((2 * DEPTH) ** 0.25)
DEEPNORM_BETA = float((8 * DEPTH) ** -0.25)
LN_EPS = 1e-5
NORM_EPS = 1e-6
N_EVEN_2 = (DEPTH + 1) // 2
N_ODD_2 = DEPTH // 2

MOBA_W = MOBA_HEADS * MOBA_HEAD_DIM
GLA_QK_W = GLA_HEADS * GLA_DK
GLA_V_W = GLA_HEADS * GLA_DV
EVEN_SPLITS_2 = (MOBA_W, MOBA_W, MOBA_W, GLA_QK_W, GLA_QK_W, GLA_V_W, GLA_V_W, GLA_GATE_RANK)
EVEN_IN = sum(EVEN_SPLITS_2)
EVEN_MIX = MOBA_W + GLA_V_W
GDN_QK_W = GDN_HEADS * GDN_DK
GDN_V_W = GDN_HEADS * GDN_DV
GDN_QKV_W = 2 * GDN_QK_W + GDN_V_W
ODD_SPLITS = (GDN_QK_W, GDN_QK_W, GDN_V_W, GDN_V_W, GDN_HEADS, GDN_HEADS)
ODD_IN = sum(ODD_SPLITS)
ODD_MIX = GDN_V_W


F32 = jnp.float32

def _split(t, sizes):
    return jnp.split(t, np.cumsum(sizes)[:-1].tolist(), axis=-1)

def layer_norm(x, g, b):
    xf = x.astype(F32)
    mu = jnp.mean(xf, -1, keepdims=True)
    var = jnp.mean(jnp.square(xf - mu), -1, keepdims=True)
    return ((xf - mu) * lax.rsqrt(var + LN_EPS)).astype(x.dtype) * g + b

def l2norm(t):
    tf = t.astype(F32)
    return tf * lax.rsqrt(jnp.sum(tf * tf, -1, keepdims=True) + NORM_EPS)

def gated_rmsnorm(o, gate, w):
    of = o.astype(F32)
    of = of * lax.rsqrt(jnp.mean(of * of, -1, keepdims=True) + NORM_EPS)
    return of * w.astype(F32) * jax.nn.silu(gate.astype(F32))

def rpe_bucket(dist):
    exact = RPE_BUCKETS // 2
    d = jnp.maximum(dist, 0)
    logd = jnp.log(jnp.maximum(d, 1).astype(F32) / exact)
    large = exact + (logd / math.log(RPE_MAX_DIST / exact) * (RPE_BUCKETS - exact)).astype(jnp.int32)
    large = jnp.minimum(large, RPE_BUCKETS - 1)
    return jnp.where(d < exact, d, large)

def causal_dwconv(x, w):
    k = w.shape[0]
    return lax.conv_general_dilated(x, w[:, None, :], window_strides=(1,), padding=[(k - 1, 0)],
                                    dimension_numbers=('NWC', 'WIO', 'NWC'),
                                    feature_group_count=x.shape[-1])

def moba_attention(q, k, v, rpe_bias):
    B, S, H, Dh = q.shape
    nkb = -(-S // MOBA_BLOCK)
    nqb = S // MOBA_QBLOCK
    kk = min(MOBA_TOPK, nkb)
    pad = nkb * MOBA_BLOCK - S

    def blocks(t):
        t = jnp.pad(t, ((0, 0), (0, pad), (0, 0), (0, 0)))
        return t.reshape(B, nkb, MOBA_BLOCK, H, Dh).transpose(0, 3, 1, 2, 4)

    kb, vb = blocks(k), blocks(v)
    k_mean = jnp.mean(kb.astype(F32), axis=3)
    qb = q.reshape(B, nqb, MOBA_QBLOCK, H, Dh).transpose(1, 0, 3, 2, 4)
    rpe_hb = rpe_bias.T.astype(F32)
    scale = Dh ** -0.5
    b_idx = jnp.arange(B)[:, None, None, None]
    h_idx = jnp.arange(H)[None, :, None, None]
    offs = jnp.arange(MOBA_BLOCK)

    def one_block(args):
        qi, qblk = args
        q0 = qi * MOBA_QBLOCK
        qpos = q0 + jnp.arange(MOBA_QBLOCK)
        cur = q0 // MOBA_BLOCK
        gate = jnp.einsum('bhqd,bhnd->bhqn', qblk.astype(F32), k_mean)
        gate = jnp.where(jnp.arange(nkb) < cur, gate, -jnp.inf)
        _, sel = lax.top_k(gate, kk)
        valid = jnp.arange(kk) < cur
        k_sel = kb[b_idx, h_idx, sel]
        v_sel = vb[b_idx, h_idx, sel]
        kpos = sel[..., None] * MOBA_BLOCK + offs
        bias_sel = rpe_hb[h_idx[..., None], rpe_bucket(qpos[:, None, None] - kpos)]
        l_sel = jnp.einsum('bhqd,bhqrtd->bhqrt', qblk, k_sel).astype(F32) * scale + bias_sel
        l_sel = jnp.where(valid[:, None], l_sel, -jnp.inf)
        k_own = lax.dynamic_index_in_dim(kb, cur, axis=2, keepdims=False)
        v_own = lax.dynamic_index_in_dim(vb, cur, axis=2, keepdims=False)
        dist = qpos[:, None] - (cur * MOBA_BLOCK + offs)[None, :]
        l_own = jnp.einsum('bhqd,bhtd->bhqt', qblk, k_own).astype(F32) * scale + rpe_hb[:, rpe_bucket(dist)]
        l_own = jnp.where(dist >= 0, l_own, -jnp.inf)
        logits = jnp.concatenate([l_sel.reshape(B, H, MOBA_QBLOCK, kk * MOBA_BLOCK), l_own], axis=-1)
        p = jax.nn.softmax(logits, axis=-1).astype(v.dtype)
        p_sel = p[..., :kk * MOBA_BLOCK].reshape(B, H, MOBA_QBLOCK, kk, MOBA_BLOCK)
        p_own = p[..., kk * MOBA_BLOCK:]
        return (jnp.einsum('bhqrt,bhqrtd->bhqd', p_sel, v_sel)
                + jnp.einsum('bhqt,bhtd->bhqd', p_own, v_own))

    out = lax.map(one_block, (jnp.arange(nqb), qb))
    return out.transpose(1, 0, 3, 2, 4).reshape(B, S, H, Dh)

def gla_chunked(q, k, v, g):
    B, S, H, DK = q.shape
    DV = v.shape[-1]
    n = S // GLA_CHUNK

    def chunks(t):
        return t.astype(F32).reshape(B, n, GLA_CHUNK, H, t.shape[-1]).transpose(1, 0, 3, 2, 4)

    qc = chunks(q) * DK ** -0.5
    kc, vc, gc = chunks(k), chunks(v), chunks(g)
    b = jnp.cumsum(gc, axis=3)
    b_last = b[:, :, :, -1:, :]
    q_e = qc * jnp.exp(b)
    k_e = kc * jnp.exp(-b)
    k_end = kc * jnp.exp(b_last - b)
    causal = jnp.tril(jnp.ones((GLA_CHUNK, GLA_CHUNK), F32))
    o_intra = jnp.einsum('nbhij,nbhjv->nbhiv', jnp.einsum('nbhid,nbhjd->nbhij', q_e, k_e) * causal, vc)

    def step(state, xs):
        q_i, k_i, v_i, d_i = xs
        o_i = jnp.einsum('bhid,bhdv->bhiv', q_i, state)
        state = state * d_i[..., None] + jnp.einsum('bhjd,bhjv->bhdv', k_i, v_i)
        return state, o_i

    s0 = jnp.zeros((B, H, DK, DV), F32)
    _, o_inter = lax.scan(step, s0, (q_e, k_end, vc, jnp.exp(b_last[:, :, :, 0, :])))
    return (o_intra + o_inter).transpose(1, 0, 3, 2, 4).reshape(B, S, H, DV)

def gated_delta_chunked(q, k, v, g, beta):
    B, S, H, DK = q.shape
    DV = v.shape[-1]
    C = GDN_CHUNK
    n = S // C

    def chunks(t):
        return t.astype(F32).reshape(B, n, C, H, t.shape[-1]).transpose(1, 0, 3, 2, 4)

    qc = chunks(q) * DK ** -0.5
    kc, vc = chunks(k), chunks(v)
    gc = jnp.cumsum(chunks(g[..., None])[..., 0], axis=-1)
    bc = chunks(beta[..., None])
    incl = jnp.tril(jnp.ones((C, C), bool))
    strict = jnp.tril(jnp.ones((C, C), bool), -1)
    diff = gc[..., :, None] - gc[..., None, :]
    decay = jnp.where(incl, jnp.exp(jnp.where(incl, diff, 0.0)), 0.0)
    k_beta = kc * bc
    v_beta = vc * bc
    a = jnp.where(strict, jnp.einsum('nbhid,nbhjd->nbhij', k_beta, kc) * decay, 0.0)
    eye = jnp.eye(C, dtype=F32)
    t_mat = lax.linalg.triangular_solve(a + eye, jnp.broadcast_to(eye, a.shape), left_side=True,
                                        lower=True, unit_diagonal=True)
    w_val = t_mat @ v_beta
    k_cum = t_mat @ (k_beta * jnp.exp(gc)[..., None])
    attn = jnp.einsum('nbhid,nbhjd->nbhij', qc, kc) * decay
    q_g = qc * jnp.exp(gc)[..., None]
    g_last = gc[..., -1:]
    k_end = kc * jnp.exp(g_last - gc)[..., None]
    d_last = jnp.exp(g_last[..., 0])

    def step(state, xs):
        q_i, kc_i, w_i, at_i, ke_i, dl_i = xs
        v_new = w_i - jnp.einsum('bhcd,bhdv->bhcv', kc_i, state)
        o_i = jnp.einsum('bhcd,bhdv->bhcv', q_i, state) + jnp.einsum('bhij,bhjv->bhiv', at_i, v_new)
        state = state * dl_i[..., None, None] + jnp.einsum('bhcd,bhcv->bhdv', ke_i, v_new)
        return state, o_i

    s0 = jnp.zeros((B, H, DK, DV), F32)
    _, o = lax.scan(step, s0, (q_g, k_cum, w_val, attn, k_end, d_last))
    return o.transpose(1, 0, 3, 2, 4).reshape(B, S, H, DV)

def moba_gla_mixer(h, rpe_bias, w_in, gk_w2, gk_b, o_norm, w_out):
    B, S, _ = h.shape
    mq, mk, mv, gq, gk, gv, gg, glr = _split(h @ w_in, EVEN_SPLITS_2)
    o_a = moba_attention(mq.reshape(B, S, MOBA_HEADS, MOBA_HEAD_DIM),
                         mk.reshape(B, S, MOBA_HEADS, MOBA_HEAD_DIM),
                         mv.reshape(B, S, MOBA_HEADS, MOBA_HEAD_DIM), rpe_bias)
    log_gate = jax.nn.log_sigmoid((glr @ gk_w2 + gk_b).astype(F32)) / GLA_GATE_NORM
    o_b = gla_chunked(gq.reshape(B, S, GLA_HEADS, GLA_DK), gk.reshape(B, S, GLA_HEADS, GLA_DK),
                      gv.reshape(B, S, GLA_HEADS, GLA_DV), log_gate.reshape(B, S, GLA_HEADS, GLA_DK))
    o_b = gated_rmsnorm(o_b, gg.reshape(B, S, GLA_HEADS, GLA_DV), o_norm).astype(h.dtype)
    mixed = jnp.concatenate([o_a.reshape(B, S, MOBA_W), o_b.reshape(B, S, GLA_V_W)], axis=-1)
    return mixed @ w_out

def gated_deltanet_mixer(h, w_in, conv_w, a_log, dt_bias, o_norm, w_out):
    B, S, _ = h.shape
    proj = h @ w_in
    qkv = jax.nn.silu(causal_dwconv(proj[..., :GDN_QKV_W], conv_w))
    q, k, v = _split(qkv, (GDN_QK_W, GDN_QK_W, GDN_V_W))
    gate, b_raw, a_raw = _split(proj[..., GDN_QKV_W:], (GDN_V_W, GDN_HEADS, GDN_HEADS))
    q = l2norm(q.reshape(B, S, GDN_HEADS, GDN_DK))
    k = l2norm(k.reshape(B, S, GDN_HEADS, GDN_DK))
    beta = jax.nn.sigmoid(b_raw.astype(F32))
    g = -jnp.exp(a_log.astype(F32)) * jax.nn.softplus(a_raw.astype(F32) + dt_bias.astype(F32))
    o = gated_delta_chunked(q, k, v.reshape(B, S, GDN_HEADS, GDN_DV), g, beta)
    o = gated_rmsnorm(o, gate.reshape(B, S, GDN_HEADS, GDN_DV), o_norm).astype(h.dtype)
    return o.reshape(B, S, GDN_V_W) @ w_out

def routed_experts(xf, topi, topw, w_gate, w_up, w_down):
    T, D = xf.shape
    M = T * TOP_K
    eid = topi.reshape(M)
    tok = jnp.arange(M, dtype=jnp.int32) // TOP_K
    wts = topw.reshape(M)
    order = jnp.argsort(eid)
    eid_s, tok_s, w_s = eid[order], tok[order], wts[order]
    counts = jnp.bincount(eid, length=N_EXPERTS)
    padded = (counts + MOE_BLOCK - 1) // MOE_BLOCK * MOE_BLOCK
    pad_end = jnp.cumsum(padded)
    pad_start = pad_end - padded
    start = jnp.cumsum(counts) - counts
    dest = pad_start[eid_s] + jnp.arange(M) - start[eid_s]
    nblk = (M + N_EXPERTS * (MOE_BLOCK - 1) + MOE_BLOCK - 1) // MOE_BLOCK
    P = nblk * MOE_BLOCK
    row_tok = jnp.zeros((P,), jnp.int32).at[dest].set(tok_s)
    row_w = jnp.zeros((P,), F32).at[dest].set(w_s)
    blk_exp = jnp.minimum(jnp.searchsorted(pad_end, jnp.arange(nblk) * MOE_BLOCK, side='right'),
                          N_EXPERTS - 1)

    def step(acc, xs):
        e, rt, rw = xs
        xb = xf[rt]
        hb = jax.nn.silu(xb @ w_gate[e]) * (xb @ w_up[e])
        yb = (hb @ w_down[e]).astype(F32) * rw[:, None]
        return acc.at[rt].add(yb), None

    out, _ = lax.scan(step, jnp.zeros((T, D), F32),
                      (blk_exp, row_tok.reshape(nblk, MOE_BLOCK), row_w.reshape(nblk, MOE_BLOCK)))
    return out.astype(xf.dtype)

def moe_ffn(h, router_w, router_b, w_gate, w_up, w_down, sh_gate, sh_up, sh_down):
    B, S, D = h.shape
    xf = h.reshape(B * S, D)
    scores = jax.nn.sigmoid((xf @ router_w).astype(F32))
    sel_scores = scores + router_b.astype(F32)
    grp = sel_scores.reshape(-1, N_GROUPS, N_EXPERTS // N_GROUPS)
    grp_score = jnp.sum(lax.top_k(grp, 2)[0], axis=-1)
    _, top_g = lax.top_k(grp_score, TOPK_GROUPS)
    gmask = jnp.any(top_g[..., None] == jnp.arange(N_GROUPS), axis=1)
    emask = jnp.repeat(gmask, N_EXPERTS // N_GROUPS, axis=1)
    _, topi = lax.top_k(jnp.where(emask, sel_scores, -jnp.inf), TOP_K)
    topw = jnp.take_along_axis(scores, topi, axis=1)
    topw = topw / (jnp.sum(topw, -1, keepdims=True) + 1e-20) * ROUTED_SCALE
    routed = routed_experts(xf, topi, topw, w_gate, w_up, w_down)
    shared = (jax.nn.silu(xf @ sh_gate) * (xf @ sh_up)) @ sh_down
    return (routed + shared).reshape(B, S, D)

def second_inputs(seed: int = 0) -> dict:
    key = jax.random.key(seed)
    ks = iter(jax.random.split(key, 32))

    def nrm(shape, s):
        return jax.random.normal(next(ks), shape, F32) * s

    D = D_MODEL
    u_a = jax.random.uniform(next(ks), (N_ODD_2, GDN_HEADS), F32, 1.0, 16.0)
    u_dt = jax.random.uniform(next(ks), (N_ODD_2, GDN_HEADS), F32)
    dt = jnp.exp(u_dt * (math.log(0.1) - math.log(0.001)) + math.log(0.001))
    return {
        "x": nrm((BATCH, SEQ, D), 1.0),
        "c": nrm((BATCH, D), 1.0),
        "rpe_bias": nrm((RPE_BUCKETS, MOBA_HEADS), 0.5),
        "ada_w": nrm((DEPTH, D, 6 * D), 0.5 * D ** -0.5),
        "ada_b": nrm((DEPTH, 6 * D), 0.02),
        "ln_mix_g": 1.0 + nrm((DEPTH, D), 0.02),
        "ln_mix_b": nrm((DEPTH, D), 0.02),
        "ln_ffn_g": 1.0 + nrm((DEPTH, D), 0.02),
        "ln_ffn_b": nrm((DEPTH, D), 0.02),
        "ev_w_in": nrm((N_EVEN_2, D, EVEN_IN), D ** -0.5),
        "ev_gk_w2": nrm((N_EVEN_2, GLA_GATE_RANK, GLA_QK_W), GLA_GATE_RANK ** -0.5),
        "ev_gk_b": nrm((N_EVEN_2, GLA_QK_W), 0.1),
        "ev_norm": 1.0 + nrm((N_EVEN_2, GLA_DV), 0.02),
        "ev_w_out": nrm((N_EVEN_2, EVEN_MIX, D), EVEN_MIX ** -0.5 * DEEPNORM_BETA),
        "od_w_in": nrm((N_ODD_2, D, ODD_IN), D ** -0.5),
        "od_conv_w": nrm((N_ODD_2, GDN_CONV, GDN_QKV_W), GDN_CONV ** -0.5),
        "od_a_log": jnp.log(u_a),
        "od_dt_bias": dt + jnp.log(-jnp.expm1(-dt)),
        "od_norm": 1.0 + nrm((N_ODD_2, GDN_DV), 0.02),
        "od_w_out": nrm((N_ODD_2, ODD_MIX, D), ODD_MIX ** -0.5 * DEEPNORM_BETA),
        "moe_router_w": nrm((DEPTH, D, N_EXPERTS), D ** -0.5),
        "moe_router_b": nrm((DEPTH, N_EXPERTS), 0.01),
        "moe_w_gate": nrm((DEPTH, N_EXPERTS, D, D_EXPERT), D ** -0.5),
        "moe_w_up": nrm((DEPTH, N_EXPERTS, D, D_EXPERT), D ** -0.5),
        "moe_w_down": nrm((DEPTH, N_EXPERTS, D_EXPERT, D), D_EXPERT ** -0.5 * DEEPNORM_BETA),
        "sh_w_gate": nrm((DEPTH, D, D_SHARED), D ** -0.5),
        "sh_w_up": nrm((DEPTH, D, D_SHARED), D ** -0.5),
        "sh_w_down": nrm((DEPTH, D_SHARED, D), D_SHARED ** -0.5 * DEEPNORM_BETA),
    }

def second_block(x, c, rpe_bias, ada_w, ada_b, ln_mix_g, ln_mix_b, ln_ffn_g, ln_ffn_b,
              ev_w_in, ev_gk_w2, ev_gk_b, ev_norm, ev_w_out,
              od_w_in, od_conv_w, od_a_log, od_dt_bias, od_norm, od_w_out,
              moe_router_w, moe_router_b, moe_w_gate, moe_w_up, moe_w_down,
              sh_w_gate, sh_w_up, sh_w_down):
    c_act = jax.nn.silu(c)
    for layer in range(DEPTH):
        mod = c_act @ ada_w[layer] + ada_b[layer]
        sh1, sc1, g1, sh2, sc2, g2 = jnp.split(mod[:, None, :], 6, axis=-1)
        h = x * (1.0 + sc1) + sh1
        i = layer // 2
        if layer % 2 == 0:
            y = moba_gla_mixer(h, rpe_bias, ev_w_in[i], ev_gk_w2[i], ev_gk_b[i], ev_norm[i], ev_w_out[i])
        else:
            y = gated_deltanet_mixer(h, od_w_in[i], od_conv_w[i], od_a_log[i], od_dt_bias[i],
                                     od_norm[i], od_w_out[i])
        x = layer_norm(DEEPNORM_ALPHA * x + g1 * y, ln_mix_g[layer], ln_mix_b[layer])
        h = x * (1.0 + sc2) + sh2
        y = moe_ffn(h, moe_router_w[layer], moe_router_b[layer], moe_w_gate[layer], moe_w_up[layer],
                    moe_w_down[layer], sh_w_gate[layer], sh_w_up[layer], sh_w_down[layer])
        x = layer_norm(DEEPNORM_ALPHA * x + g2 * y, ln_ffn_g[layer], ln_ffn_b[layer])
    return x


def setup_inputs(seed=0):
    out = dict(first_inputs(seed))
    for name, value in second_inputs(seed + 1).items():
        if name != "x":
            out[name + "_2"] = value
    return out


def reference(
    x, c, ctx, c_ctx, w_mod, b_mod, norm_pre_mix, norm_post_mix, norm_pre_ffn, norm_post_ffn,
    even_w_in, even_w_out, even_q_norm, even_k_norm, hgrn_lb_logits, hgrn_out_norm, odd_w_qkv,
    odd_w_out, odd_rpb, ffn_w_up, ffn_conv_w, ffn_conv_b, ffn_w_down, c_2, rpe_bias_2, ada_w_2,
    ada_b_2, ln_mix_g_2, ln_mix_b_2, ln_ffn_g_2, ln_ffn_b_2, ev_w_in_2, ev_gk_w2_2, ev_gk_b_2,
    ev_norm_2, ev_w_out_2, od_w_in_2, od_conv_w_2, od_a_log_2, od_dt_bias_2, od_norm_2,
    od_w_out_2, moe_router_w_2, moe_router_b_2, moe_w_gate_2, moe_w_up_2, moe_w_down_2,
    sh_w_gate_2, sh_w_up_2, sh_w_down_2,
):
    x = first_block(
        x, c, ctx, c_ctx, w_mod, b_mod, norm_pre_mix, norm_post_mix, norm_pre_ffn,
        norm_post_ffn, even_w_in, even_w_out, even_q_norm, even_k_norm, hgrn_lb_logits,
        hgrn_out_norm, odd_w_qkv, odd_w_out, odd_rpb, ffn_w_up, ffn_conv_w, ffn_conv_b,
        ffn_w_down,
    )
    return second_block(
        x, c_2, rpe_bias_2, ada_w_2, ada_b_2, ln_mix_g_2, ln_mix_b_2, ln_ffn_g_2, ln_ffn_b_2,
        ev_w_in_2, ev_gk_w2_2, ev_gk_b_2, ev_norm_2, ev_w_out_2, od_w_in_2, od_conv_w_2,
        od_a_log_2, od_dt_bias_2, od_norm_2, od_w_out_2, moe_router_w_2, moe_router_b_2,
        moe_w_gate_2, moe_w_up_2, moe_w_down_2, sh_w_gate_2, sh_w_up_2, sh_w_down_2,
    )


_drawn_inputs = setup_inputs


def setup_inputs(seed=0):
    import zlib

    import numpy as np

    out = dict(_drawn_inputs(seed))
    spreads = {}
    factors = {'even_q_norm': 3.833,
     'even_k_norm': 3.525,
     'odd_rpb': 4.573,
     'ffn_conv_b': 2.834,
     'rpe_bias_2': 3.447,
     'ev_gk_b_2': 8.0,
     'ev_norm_2': 27.238,
     'od_a_log_2': 3.941,
     'od_norm_2': 31.352}
    for name, (base, spread) in spreads.items():
        noise = np.random.default_rng([zlib.crc32(name.encode()), seed]).standard_normal(out[name].shape)
        drawn = base * np.exp(spread * noise) if base else spread * noise
        out[name] = __import__('jax').numpy.asarray(drawn.astype(out[name].dtype))
    for name, factor in factors.items():
        out[name] = (out[name] * factor).astype(out[name].dtype)
    return out
```

```python
from contextlib import ExitStack

import numpy as np
import concourse.bass as bass
from concourse import mybir

F32 = mybir.dt.float32
ALU = mybir.AluOpType
ACT = mybir.ActivationFunctionType
AX = mybir.AxisListType.X
MUL, ADD, SUB, MAX, MIN = ALU.mult, ALU.add, ALU.subtract, ALU.max, ALU.min

RING = 5
SLOT = 4096
ARENA = 22100
EPS = 1e-6
ALPHA = float(4 ** 0.25)
NEXP = 64

COLS = {}
_n = 0
for _name, _w in (("c", 8), ("c_ctx", 8), ("c_2", 8), ("npm", 16), ("nqm", 16), ("npf", 16), ("nqf", 16),
                  ("bmod", 96), ("adab", 96), ("lmg", 16), ("lmb", 16), ("lfg", 16), ("lfb", 16),
                  ("cw", 2 * 3 * 44), ("cb", 2 * 44), ("ocw", 4 * 24)):
    COLS[_name] = _n
    _n += _w
NCOL = _n
ROWS = {}
_n = 0
for _name, _w in (("qn", 64), ("kn", 64), ("on", 128), ("gkb", 256), ("evn", 128), ("odn", 128),
                  ("alog", 8), ("dtb", 8), ("rb", 128)):
    ROWS[_name] = _n
    _n += _w
NROW = _n


class Queues:

    def __init__(self, nc, ctx):
        self.nc, self.ctx = nc, ctx
        self.q = {e: [] for e in "pvags"}
        self.sem = {e: ctx.enter_context(nc.semaphore("done_" + e)) for e in "pvag"}
        self.n = {e: 0 for e in "pvag"}
        self.seen = {e: {} for e in "pvags"}
        self.chained = "vag"

    def new_sem(self, name):
        self.sem[name] = self.ctx.enter_context(self.nc.semaphore(name))
        self.n[name] = 0
        return name

    def wait(self, e, toks):
        for t in toks:
            if t is None:
                continue
            if isinstance(t, list):
                self.wait(e, t)
                continue
            s, v = t
            if v == 0:
                continue
            if self.seen[e].get(s, 0) >= v:
                continue
            self.seen[e][s] = v
            self.q[e].append(lambda eng, s=self.sem[s], v=v: eng.wait_ge(s, v))

    def op(self, e, f, *w):
        self.wait(e, w)
        if e in self.chained:
            self.wait(e, [(e, self.n[e])])
        self.n[e] += 1
        self.q[e].append(lambda eng, s=self.sem[e]: f(eng).then_inc(s, 1))
        return (e, self.n[e])

    def quiet(self, e, f, *w):
        self.wait(e, w)
        self.q[e].append(lambda eng: f(eng))

    def dma(self, e, sem, out, in_, *w):
        self.wait(e, w)
        self.n[sem] += 16
        self.q[e].append(lambda eng, s=self.sem[sem]: eng.dma_start(out, in_).then_inc(s, 16))
        return (sem, self.n[sem])

    def now(self, e):
        return (e, self.n[e])


def program(nc, A, out):
    with ExitStack() as ctx:
        Q = Queues(nc, ctx)
        op, quiet = Q.op, Q.quiet

        def sb(name, shape):
            return ctx.enter_context(nc.sbuf_tensor(name, shape, F32))

        ring = sb("ring", [128, RING, SLOT])
        X = sb("X", [128, 4, 1024])
        HT = sb("HT", [128, 8, 512])
        arena = sb("arena", [128, ARENA])
        ident = sb("ident", [128, 128])
        ones = sb("ones", [128, 128])
        colp = sb("colp", [128, NCOL])
        rowp = sb("rowp", [128, NROW])
        mod = sb("mod", [128, 48, 2])
        csil = sb("csil", [128, 8, 4])
        st = sb("st", [128, 256])
        ps = [ctx.enter_context(nc.psum_tensor(f"ps{i}", [128, 512], F32)) for i in range(8)]
        free = [None] * 8
        bank_at = [0]

        for i in range(RING):
            Q.new_sem(f"w{i}")
        for i in range(4):
            Q.new_sem(f"b{i}")
        Q.new_sem("small")
        Q.new_sem("outs")

        top = [0]

        def carve(*shape):
            n = int(np.prod(shape))
            a = top[0]
            top[0] += n
            assert top[0] <= ARENA, top[0]
            v = arena[:, a:a + n]
            if len(shape) == 2:
                return v.rearrange("p (a b) -> p a b", b=shape[1])
            if len(shape) == 3:
                return v.rearrange("p (a b c) -> p a b c", b=shape[1], c=shape[2])
            return v

        st_top = [0]

        def cstat(n):
            a = st_top[0]
            st_top[0] += n
            assert st_top[0] <= 256
            return st[:, a:a + n]

        small_open = [None]

        def fence():
            toks = [Q.now(e) for e in "pvag"] + [Q.now("small")]
            for e in "pvag":
                Q.wait(e, toks)
            st_top[0] = 0
            for i in range(8):
                free[i] = None

        def load(dst, src, *w):
            return Q.dma("g", "small", dst, src, *w)

        jobs = [0]
        released = {}

        def weights(*parts):
            i = jobs[0]
            jobs[0] += 1
            s = i % RING
            if i >= RING:
                Q.wait("s", [released.pop(i - RING)])
            tok = None
            for dst, src in parts:
                tok = Q.dma("s", f"w{s}", dst(ring[:, s, :]), src)
            return i, ring[:, s, :], tok

        def wtile(src, kc, n):
            i, slot, tok = weights((lambda sl: sl[:, 0:kc * n].rearrange("p (k n) -> p k n", n=n),
                                    src.rearrange("(k p) n -> p k n", p=128)))
            return i, slot[:, 0:kc * n].rearrange("p (k n) -> p k n", n=n), tok

        def release(i):
            released[i] = Q.now("p")

        def bank(banks=range(8)):
            banks = list(banks)
            b = banks[bank_at[0] % len(banks)]
            bank_at[0] += 1
            return b

        def mm(o, l, r, start, stop, *w):
            quiet("p", lambda e: e.matmul(o, l, r, start=start, stop=stop), *w)

        def mmi(o, l, r, start, stop, *w):
            return op("p", lambda e: e.matmul(o, l, r, start=start, stop=stop), *w)

        def tr(o, i, *w):
            k = i.shape[0]
            return op("p", lambda e: e.transpose(o, i, ident[0:k, 0:k]), *w)

        def vtt(o, a, b, f, *w, e="v"):
            return op(e, lambda g: g.tensor_tensor(o, a, b, f), *w)

        def vts(o, a, s1, s2, f1, f2, *w, e="v"):
            if f2 is None:
                return op(e, lambda g: g.tensor_scalar(o, a, s1, None, f1), *w)
            return op(e, lambda g: g.tensor_scalar(o, a, s1, s2, f1, f2), *w)

        def stt(o, a, s, b, f1, f2, *w):
            return op("v", lambda g: g.scalar_tensor_tensor(out=o, in0=a, scalar=s, in1=b, op0=f1, op1=f2), *w)

        def red(o, a, f, *w):
            return op("v", lambda g: g.tensor_reduce(o, a, AX, f), *w)

        def recip(o, a, *w):
            return op("v", lambda g: g.reciprocal(o, a), *w)

        def vcopy(o, a, *w, e="v"):
            return op(e, lambda g: g.tensor_copy(o, a), *w)

        def act(o, a, f, *w, scale=1.0, bias=0.0, accum=None):
            if accum is None:
                return op("a", lambda g: g.activation(o, a, f, scale=scale, bias=bias), *w)
            return op("a", lambda g: g.activation(o, a, f, scale=scale, bias=bias, accum_out=accum), *w)

        def copy(e, o, a, *w):
            if e == "a":
                return act(o, a, ACT.Copy, *w)
            return vcopy(o, a, *w, e=e)

        def bc(ap, n, at):
            shape = list(ap.shape)
            return ap.unsqueeze(at).broadcast_to(shape[:at] + [n] + shape[at:])

        def col(name, i, n):
            return colp[:, COLS[name] + i:COLS[name] + i + n]

        def row(name, n, i=0):
            return rowp[:, ROWS[name] + i:ROWS[name] + i + n]

        def rstd_of(ss, n, scale, eps, *w):
            t = vts(ss, ss, scale, eps, MUL, ADD, *w)
            t = act(ss, ss, ACT.Ln, t)
            return act(ss, ss, ACT.Exp, t, scale=-0.5)

        tI = load(ident[:, :], A["cst"][:, 0:128])
        load(colp[:, :], A["colp"])
        load(rowp[:, :], A["rowp"][0:1, :].broadcast_to([128, NROW]))
        xv = A["x"].rearrange("a (t p) d -> p (a t) d", p=128)
        cv = A["ctx"].rearrange("a (t p) d -> p (a t) d", p=128)
        load(X[:, 0:2, :], xv)
        tI = load(X[:, 2:4, :], cv)
        op("v", lambda g: g.memset(ones[:, :], 1.0))
        for i, nm in enumerate(("c", "c_ctx", "c_2", "c_2")):
            act(csil[:, :, i], col(nm, 0, 8), ACT.Silu, tI)
        fence()

        def modulate(src, bname, l, which):
            b = bank()
            bk = ps[b]
            for j in range(12):
                i, wt, tw = wtile(src[:, 512 * j:512 * j + 512], 8, 512)
                for m in range(4):
                    o = bk[:, (j * 4 + m) * 2:(j * 4 + m) * 2 + 2]
                    for k in range(8):
                        f = mmi if k == 7 else mm
                        t = f(o, wt[:, k, m * 128:m * 128 + 128], csil[:, k, which:which + 2], k == 0, k == 7, tw)
                release(i)
            vtt(mod[:, :, :], bk[:, 0:96].rearrange("p (a b) -> p a b", b=2), bc(col(bname, 48 * l, 48), 2, 2), ADD, t)
            fence()

        def scaled(dst, j, which, wname, l):
            return stt(dst, mod[:, 8 * j:8 * j + 8, which], 1.0, col(wname, 8 * l, 8), ADD, MUL)

        def spread(dst, c, dg, *w):
            t = vtt(dg, bc(ident[:, :], 8, 1), bc(c, 128, 2), MUL, *w)
            for h in range(2):
                b = bank()
                tm = mmi(ps[b][:, :], ones[:, :], dg[:, 4 * h:4 * h + 4, :], True, True, t, free[b])
                t2 = free[b] = copy("va"[h], dst[:, 512 * h:512 * h + 512], ps[b][:, :], tm)
                if h == 0:
                    t0 = t2
            return [t0, t2]

        def transposed(tiles, norm, sc, sh):
            tmp = carve(2, 1024)
            ss = cstat(4)
            used = [None, None]
            if norm:
                for i, t in enumerate(tiles):
                    used[i % 2] = act(tmp[:, i % 2, :], X[:, t, :], ACT.Square, accum=ss[:, t:t + 1])
                tr_ = rstd_of(ss[:, tiles[0]:tiles[-1] + 1], len(tiles), 1.0 / 1024, EPS, Q.now("a"))
                used = [tr_, tr_]
            for i, t in enumerate(tiles):
                if norm:
                    tx = vts(tmp[:, i % 2, :], X[:, t, :], ss[:, t:t + 1], None, MUL, None, used[i % 2])
                    src = tmp[:, i % 2, :]
                else:
                    tx, src = None, X[:, t, :]
                for h in range(2):
                    b = bank()
                    for c in range(4):
                        k = 4 * h + c
                        tt_ = tr(ps[b][:, 128 * c:128 * c + 128], src[:, 128 * k:128 * k + 128], tx, free[b])
                    last = []
                    for c in range(4):
                        k = 4 * h + c
                        o, a = HT[:, k, 128 * t:128 * t + 128], ps[b][:, 128 * c:128 * c + 128]
                        if h == 0:
                            z = vts(o, a, sc(t)[:, k:k + 1], sh(t)[:, k:k + 1], MUL, ADD, tt_)
                        else:
                            z = act(o, a, ACT.Identity, tt_, scale=sc(t)[:, k:k + 1], bias=sh(t)[:, k:k + 1])
                    free[b] = z
                used[i % 2] = tt_
            fence()

        def lin_tok(wt, tw, c0, n, lhs, kc, tiles, evac, banks=range(8)):
            for t in tiles:
                b = bank(banks)
                for k in range(kc):
                    f = mmi if k == kc - 1 else mm
                    tm = f(ps[b][:, 0:n], lhs(k, t), wt[:, k, c0:c0 + n], k == 0, k == kc - 1, tw, free[b])
                free[b] = evac(t, ps[b][:, 0:n], tm)

        def lin_col(wt, tw, c0, m, rhs, kc, ntok, evac, banks=range(8)):
            b = bank(banks)
            for k in range(kc):
                f = mmi if k == kc - 1 else mm
                tm = f(ps[b][0:m, 0:ntok], wt[:, k, c0:c0 + m], rhs(k), k == 0, k == kc - 1, tw, free[b])
            free[b] = evac(ps[b][0:m, 0:ntok], tm)

        ht_tok = lambda k, t: HT[:, k, 128 * t:128 * t + 128]
        flip = [0]

        def ev(dst):
            def f(t, p, tok):
                flip[0] ^= 1
                return copy("va"[flip[0]], dst(t), p, tok)
            return f

        def evc(dst):
            def f(p, tok):
                flip[0] ^= 1
                return copy("va"[flip[0]], dst, p, tok)
            return f

        def attention(items, scale, nbuf=4):
            P = carve(nbuf, 512)
            PT = carve(2, 4 * 256)
            mx, nm, sm, ri = (cstat(nbuf) for _ in range(4))
            pfree = [None] * nbuf
            ptfree = [None, None]
            S = {}
            seq = [(i, qt) for i in range(len(items)) for qt in range(2)]

            def first(n):
                i, qt = seq[n]
                it = items[i]
                r = n % nbuf
                b = bank((0, 1, 2))
                nk = it["nk"]
                o = ps[b][:, 0:nk]
                t = mmi(o, it["q"](qt), it["k"], True, True, free[b])
                src = o
                tb = []
                if it["bias"] is not None:
                    bv, btok, lo, hi = it["bias"](qt)
                    t = stt(P[:, r, lo:hi], o[:, lo:hi], scale, bv, MUL, ADD, t, btok, pfree[r])
                    if hi < nk:
                        t2 = vts(P[:, r, hi:nk], o[:, hi:nk], scale, None, MUL, None)
                        t = [t, t2]
                    free[b] = t[1] if isinstance(t, list) else t
                    it["bias_done"](t)
                    src = P[:, r, 0:nk]
                t = red(mx[:, r:r + 1], src, MAX, t, pfree[r])
                sc = 1.0 if it["bias"] is not None else scale
                t = vts(nm[:, r:r + 1], mx[:, r:r + 1], -sc, None, MUL, None, t)
                t = act(P[:, r, 0:nk], src, ACT.Exp, t, pfree[r], scale=sc, bias=nm[:, r:r + 1], accum=sm[:, r:r + 1])
                if it["bias"] is None:
                    free[b] = t
                S[n] = t

            def second(n):
                i, qt = seq[n]
                it = items[i]
                r = n % nbuf
                nk = it["nk"]
                t = recip(ri[:, r:r + 1], sm[:, r:r + 1], S[n])
                t = vts(P[:, r, 0:nk], P[:, r, 0:nk], ri[:, r:r + 1], None, MUL, None, t)
                b = bank((3, 4, 5))
                for kt in range(nk // 128):
                    tt_ = tr(ps[b][:, 128 * kt:128 * kt + 128], P[:, r, 128 * kt:128 * kt + 128], t, free[b])
                pfree[r] = tt_
                ptv = PT[:, i % 2, 0:nk * 2].rearrange("p (k q c) -> p k q c", q=2, c=128)
                t = copy("a", ptv[:, :, qt, :], ps[b][:, 0:nk].rearrange("p (k c) -> p k c", c=128), tt_, ptfree[i % 2])
                free[b] = t
                if qt == 1:
                    S["pt", i] = t

            def third(i):
                it = items[i]
                nkt = it["nk"] // 128
                nd, base = it["nd"], it["base"]
                ptv = PT[:, i % 2, 0:nkt * 256].rearrange("p (k q) -> p k q", q=256)
                b = bank((6, 7))
                o = ps[b][base:base + nd, 0:256]
                for kt in range(nkt):
                    f = mmi if kt == nkt - 1 else mm
                    t = f(o, it["v"](kt), ptv[:, kt, :], kt == 0, kt == nkt - 1, S["pt", i], free[b])
                ptfree[i % 2] = t
                free[b] = copy("v", it["out"], o, t)

            N = len(seq)
            for n in range(N + 4):
                if n < N:
                    first(n)
                if 2 <= n < N + 2:
                    second(n - 2)
                if n >= 4 and (n - 4) % 2 == 1:
                    third((n - 4) // 2)

        def heads_rstd(src, nh, hd, scale, eps, tmp, ss, *w):
            t = act(tmp, src, ACT.Square, *w)
            t = red(ss, tmp.rearrange("p (h d) -> p h d", d=hd), ADD, t)
            return rstd_of(ss, nh, scale, eps, t)

        def even_mixer():
            W, WO = A["even_w_in"][0], A["even_w_out"][0]
            G_ = carve(4, 512)
            V = carve(4, 512)
            Z = [carve(4, 512), carve(4, 512)]
            QB = carve(4, 512)
            keep = top[0]
            AA = carve(4, 768)
            hcol = lambda k: HT[:, k, :]
            i, wt, tw = wtile(W[:, 0:512], 8, 512)
            lin_tok(wt, tw, 0, 512, ht_tok, 8, range(4), lambda t, p, tok: copy(
                "va"[t % 2], AA[:, t, 0:512].rearrange("p (h w d) -> p w h d", w=2, d=64),
                p.rearrange("p (w h d) -> p w h d", w=2, d=64), tok))
            release(i)
            i, wt, tw = wtile(W[:, 512:768], 8, 256)
            lin_tok(wt, tw, 0, 256, ht_tok, 8, range(4), ev(lambda t: AA[:, t, 512:768]))
            release(i)
            i, wt, tw = wtile(W[:, 768:1280], 8, 512)
            for h in range(4):
                def e(p, tok, h=h):
                    t = act(QB[:, h, :], p, ACT.Silu, tok)
                    vts(QB[:, h, :], QB[:, h, :], 128 ** -0.5, None, MUL, None, t)
                    return t
                lin_col(wt, tw, 128 * h, 128, hcol, 8, 512, e)
            release(i)
            for dst, c in ((Z[0], 1280), (Z[1], 1792), (V, 2304), (G_, 2816)):
                i, wt, tw = wtile(W[:, c:c + 512], 8, 512)
                if dst is G_:
                    lin_tok(wt, tw, 0, 512, ht_tok, 8, range(4), lambda t, p, tok: act(G_[:, t, :], p, ACT.Silu, tok))
                else:
                    lin_tok(wt, tw, 0, 512, ht_tok, 8, range(4), ev(lambda t, dst=dst: dst[:, t, :]))
                release(i)
            fence()
            OT = HT
            SQ = carve(640)
            ROT = carve(2, 320)
            cs = carve(2, 64)
            ss = cstat(40)
            tcs = load(cs, A["rope"].rearrange("(t p) c -> p t c", p=128))
            for t in range(4):
                tq = heads_rstd(AA[:, t, 0:640], 10, 64, 1.0 / 64, EPS, SQ, ss[:, 10 * t:10 * t + 10], Q.now("v"))
                hv = AA[:, t, 0:640].rearrange("p (h d) -> p h d", d=64)
                tq = vtt(hv, hv, bc(ss[:, 10 * t:10 * t + 10], 64, 2), MUL, tq)
                tq = [vtt(hv[:, 0:8, :], hv[:, 0:8, :], bc(row("qn", 64), 8, 1), MUL, tq),
                      vtt(hv[:, 8:10, :], hv[:, 8:10, :], bc(row("kn", 64), 2, 1), MUL, tq)]
                if t < 2:
                    x1, x2 = hv[:, :, 0:32], hv[:, :, 32:64]
                    c_, s_ = bc(cs[:, t, 0:32], 10, 1), bc(cs[:, t, 32:64], 10, 1)
                    r0, r1 = (ROT[:, j, :].rearrange("p (h d) -> p h d", d=32) for j in range(2))
                    ta = vtt(r0, x1, s_, MUL, tq, tcs)
                    tb = vtt(r1, x2, s_, MUL, tq)
                    t1 = vtt(x1, x1, c_, MUL, ta)
                    t1 = vtt(x1, x1, r1, SUB, t1, tb)
                    t2 = vtt(x2, x2, c_, MUL, tb)
                    tq = vtt(x2, x2, r0, ADD, t2, ta)
            QT = carve(4, 512)
            KT = carve(512)
            for t in range(4):
                b = bank()
                for h in range(4):
                    t_ = tr(ps[b][:, 128 * h:128 * h + 128], AA[:, t, 128 * h:128 * h + 128], Q.now("v"), free[b])
                free[b] = copy("v", QT[:, :, 128 * t:128 * t + 128], ps[b][:, :].rearrange("p (h c) -> p h c", c=128), t_)
                b = bank()
                t_ = tr(ps[b][:, 0:128], AA[:, t, 512:640], free[b])
                free[b] = copy("a", KT[:, 128 * t:128 * t + 128], ps[b][:, 0:128], t_)
            fence()
            items = []
            for h in range(8):
                kv, pr = h // 4, h % 4
                B0 = 64 * kv
                for grp in range(2):
                    k0 = 0 if grp == 0 else 256
                    t0 = 2 * grp
                    items.append(dict(
                        q=lambda qt, B0=B0, pr=pr, t0=t0: QT[B0:B0 + 64, pr, 128 * (t0 + qt):128 * (t0 + qt) + 128],
                        k=KT[B0:B0 + 64, k0:512], nk=512 - k0, bias=None,
                        v=lambda kt, k0=k0, kv=kv: AA[:, k0 // 128 + kt, 640 + 64 * kv:704 + 64 * kv],
                        nd=64, base=64 * (h % 2),
                        out=OT[64 * (h % 2):64 * (h % 2) + 64, h // 2, 256 * grp:256 * grp + 256]))
            attention(items, 0.125)
            fence()
            top[0] = keep
            GG = carve(4, 512)
            KTT = carve(4, 512)
            O = carve(4, 512)
            CM = carve(9, 128)
            CK = carve(8, 128)
            E = HT[:, 4:8, :].rearrange("p (h j) (l c) -> p h (j l) c", h=2, c=128)
            QF = carve(2, 128)
            S = carve(512)
            KL = carve(512)
            AM = carve(8, 128)
            AT = carve(2, 128)
            for d in range(2):
                z = Z[d]
                fl = lambda a: a.rearrange("p a b -> p (a b)")
                tc = load(CM, A["hgc"][d, :, 0:1152].rearrange("p (a b) -> p a b", b=128))
                tc = load(CK, A["hgc"][d, :, 1152:2176].rearrange("p (a b) -> p a b", b=128))
                t = act(fl(GG), fl(z), ACT.Abs)
                t = act(fl(GG), fl(GG), ACT.Exp, t, scale=-1.0)
                t = act(fl(GG), fl(GG), ACT.Ln, t, bias=1.0)
                t = stt(fl(GG), fl(z), 0.0, fl(GG), MIN, SUB, t)
                t = vtt(fl(z), fl(GG), fl(z), SUB, t)
                t = act(fl(z), fl(z), ACT.Exp, t)
                for c in range(4):
                    b = bank()
                    for h in range(4):
                        t_ = tr(ps[b][:, 128 * h:128 * h + 128], z[:, c, 128 * h:128 * h + 128], t, free[b])
                    free[b] = copy("a", KTT[:, :, 128 * c:128 * c + 128],
                                   ps[b][:, :].rearrange("p (h c) -> p h c", c=128), t_)
                tkt = Q.now("a")
                qtwo, ktwo, last = (1, 0, 127) if d == 0 else (0, 1, 0)
                order = (2, 3, 0, 1) if d == 0 else (3, 2, 1, 0)
                ts = None
                tkl = None
                for n, c in enumerate(order):
                    if n < 3:
                        b = bank((0, 1))
                        t = mmi(ps[b][:, :], CM[:, 8, :], GG[:, c, :], True, True, tc, Q.now("v"), free[b])
                        t = free[b] = act(KL, ps[b][:, :], ACT.Exp, t, tkl)
                        tkl = vtt(KL, KL, z[:, c, :], MUL, t)
                    bo = 6 + n % 2
                    for hp in range(2):
                        te, tx = [None, None], [None, None]
                        for hh in range(2):
                            h = 2 * hp + hh
                            for j in range(2):
                                b = 2 + (2 * hh + j) % 2
                                t = mmi(ps[b][:, :], GG[:, c, 128 * h:128 * h + 128], CM[:, 4 * j:4 * j + 4, :],
                                        True, True, tc, free[b])
                                te[hh] = free[b] = act(E[:, hh, 4 * j:4 * j + 4, :],
                                                       ps[b][:, :].rearrange("p (a b) -> p a b", b=128), ACT.Exp, t, ts)
                        qv = QB[:, 2 * hp:2 * hp + 2, 128 * c:128 * c + 128]
                        kv = KTT[:, 2 * hp:2 * hp + 2, 128 * c:128 * c + 128]
                        tqf = vtt(QF, E[:, :, 7, :], qv, MUL, te[0], te[1], tkt, ts)
                        for lv in range(7):
                            m = 64 >> lv
                            ev_ = E[:, :, lv, :].rearrange("p h (b w m) -> p h b w m", w=2, m=m)
                            q5 = qv.rearrange("p h (b w m) -> p h b w m", w=2, m=m)
                            k5 = kv.rearrange("p h (b w m) -> p h b w m", w=2, m=m)
                            vtt(ev_[:, :, :, qtwo, :], ev_[:, :, :, qtwo, :], q5[:, :, :, qtwo, :], MUL)
                            tx = vtt(ev_[:, :, :, ktwo, :], ev_[:, :, :, ktwo, :], k5[:, :, :, ktwo, :], MUL)
                        for hh in range(2):
                            h = 2 * hp + hh
                            for j in range(2):
                                b = 4 + j
                                for a in range(4):
                                    lv = 4 * j + a
                                    l_, r_ = (E[:, hh, lv, :], E[:, hh, lv, :]) if lv < 7 else (kv[:, hh, :], qv[:, hh, :])
                                    t = mmi(ps[b][:, 128 * a:128 * a + 128], l_, r_, True, True, tx, free[b])
                                t = free[b] = vtt(AM[:, 4 * j:4 * j + 4, :], ps[b][:, :].rearrange("p (a b) -> p a b", b=128),
                                                  CK[:, 4 * j:4 * j + 4, :], MUL, t)
                            t = red(AT[:, hh, :], AM.rearrange("p l t -> p t l"), ADD, t, Q.now("p"))
                            oo = ps[bo][:, 128 * h:128 * h + 128]
                            vv = V[:, c, 128 * h:128 * h + 128]
                            if n == 0:
                                ts = mmi(oo, AT[:, hh, :], vv, True, True, t, free[bo])
                            else:
                                mm(oo, AT[:, hh, :], vv, True, False, t, free[bo])
                                ts = mmi(oo, QF[:, hh, :], S[:, 128 * h:128 * h + 128], False, True, tqf)
                            if n < 3:
                                b = bank((0, 1))
                                t = mmi(ps[b][:, 0:128], KL[:, 128 * h:128 * h + 128], vv, True, True, tkl, free[b])
                                sl = S[:, 128 * h:128 * h + 128]
                                if n == 0:
                                    free[b] = copy("v", sl, ps[b][:, 0:128], t, ts)
                                else:
                                    free[b] = stt(sl, sl, E[:, hh, 7, last:last + 1], ps[b][:, 0:128], MUL, ADD, t, ts)
                                ts = free[b]
                    if n < 3:
                        tkl = Q.now("p")
                    if d == 0:
                        free[bo] = copy("v", O[:, c, :], ps[bo][:, :], Q.now("p"))
                    else:
                        free[bo] = vtt(O[:, c, :], O[:, c, :], ps[bo][:, :], ADD, Q.now("p"))
                fence()
            ss = cstat(16)
            SQ = GG
            for t in range(4):
                tq = heads_rstd(O[:, t, :], 4, 128, 1.0 / 128, EPS, SQ[:, t, :], ss[:, 4 * t:4 * t + 4])
                ov = O[:, t, :].rearrange("p (h d) -> p h d", d=128)
                tq = vtt(ov, ov, bc(ss[:, 4 * t:4 * t + 4], 128, 2), MUL, tq)
                tq = vtt(ov, ov, bc(row("on", 128), 4, 1), MUL, tq)
                tq = vtt(O[:, t, :], O[:, t, :], G_[:, t, :], MUL, tq)
                b = bank()
                for h in range(4):
                    t_ = tr(ps[b][:, 128 * h:128 * h + 128], O[:, t, 128 * h:128 * h + 128], tq, free[b])
                free[b] = copy("a", OT[:, 4:8, 128 * t:128 * t + 128], ps[b][:, :].rearrange("p (h c) -> p h c", c=128), t_)
            fence()
            top[0] = 0
            project_out(WO, OT, range(4))

        Yh = [None]

        def project_out(WO, OT, tiles):
            Y = Yh[0] = carve(4, 1024)
            for h in range(2):
                i, wt, tw = wtile(WO[:, 512 * h:512 * h + 512], 8, 512)
                lin_tok(wt, tw, 0, 512, lambda k, t: OT[:, k, 128 * t:128 * t + 128], 8, tiles,
                        ev(lambda t: Y[:, t, 512 * h:512 * h + 512]))
                release(i)
            fence()

        def residual_rms(j, wname, l, tiles):
            Y = Yh[0]
            R = carve(2, 1024)
            DG = carve(8, 128)
            SQ = carve(1024)
            cc = cstat(16)
            ss = cstat(4)
            tg = []
            for w in range(2 if len(tiles) == 4 else 1):
                t = vtt(cc[:, 8 * w:8 * w + 8], mod[:, 8 * j:8 * j + 8, w], col(wname, 8 * l, 8), MUL)
                tg += spread(R[:, w, :], cc[:, 8 * w:8 * w + 8], DG, t, Q.now("p"))
            for t in tiles:
                act(SQ, Y[:, t, :], ACT.Square, Q.now("a"), accum=ss[:, t:t + 1])
            tq = rstd_of(ss[:, 0:len(tiles)], len(tiles), 1.0 / 1024, EPS, Q.now("a"))
            for t in tiles:
                a = stt(Y[:, t, :], Y[:, t, :], ss[:, t:t + 1], R[:, t // 2, :], MUL, MUL, tq, tg)
                vtt(X[:, t, :], X[:, t, :], Y[:, t, :], ADD, a)
            fence()

        def conv_ffn(l, tiles):
            NT = 128 * len(tiles)
            ns = len(tiles) // 2
            WU, WD = A["ffn_w_up"][l], A["ffn_w_down"][l]
            HID = carve(22, NT)
            CB = carve(4, NT)
            cbf = [None] * 4
            for j in range(11):
                c = 256 * j
                i, slot, tw = weights(
                    (lambda sl: sl.rearrange("p (k n) -> p k n", n=512)[:, :, 0:256],
                     WU[:, c:c + 256].rearrange("(k p) n -> p k n", p=128)),
                    (lambda sl: sl.rearrange("p (k n) -> p k n", n=512)[:, :, 256:512],
                     WU[:, 2816 + c:2816 + c + 256].rearrange("(k p) n -> p k n", p=128)))
                wt = slot.rearrange("p (k n) -> p k n", n=512)
                for s in range(2):
                    m = 2 * j + s
                    done = []
                    for g in range(2):
                        ch = 22 * g + m
                        r = 2 * (m % 2) + g

                        def e(p, tok, ch=ch, r=r):
                            w0, w1, w2 = (col("cw", (3 * l + k) * 44 + ch, 1) for k in range(3))
                            cb = CB[:, r, :]
                            t = act(cb, p, ACT.Identity, tok, cbf[r], scale=w1, bias=col("cb", 44 * l + ch, 1))
                            cv = cb.rearrange("p (s t) -> p s t", s=ns)
                            pv = p.rearrange("p (s t) -> p s t", s=ns)
                            t = stt(cv[:, :, 1:256], pv[:, :, 0:255], w0, cv[:, :, 1:256], MUL, ADD, t)
                            t = stt(cv[:, :, 0:255], pv[:, :, 1:256], w2, cv[:, :, 0:255], MUL, ADD, t)
                            done.append(t)
                            return t
                        lin_col(wt, tw, 256 * g + 128 * s, 128, lambda k: HT[:, k, 0:NT], 8, NT, e)
                    ra, rg = 2 * (m % 2), 2 * (m % 2) + 1
                    t = act(CB[:, rg, :], CB[:, rg, :], ACT.Silu, done[1])
                    t = vtt(HID[:, m, :], CB[:, rg, :], CB[:, ra, :], MUL, t, done[0], e="g")
                    cbf[ra] = cbf[rg] = t
                release(i)
            fence()
            top[0] = 22 * NT
            Y = Yh[0] = carve(4, 1024)
            for h in range(2):
                bs = [4 * h + t for t in tiles]
                for q in range(3):
                    kc = (8, 8, 6)[q]
                    i, wt, tw = wtile(WD[1024 * q:1024 * q + 128 * kc, 512 * h:512 * h + 512], kc, 512)
                    for t in tiles:
                        for k in range(kc):
                            f = mmi if k == kc - 1 else mm
                            tm = f(ps[bs[t]][:, :], HID[:, 8 * q + k, 128 * t:128 * t + 128], wt[:, k, :],
                                   q == 0 and k == 0, q == 2 and k == kc - 1, tw)
                        if q == 2:
                            copy("va"[t % 2], Y[:, t, 512 * h:512 * h + 512], ps[bs[t]][:, :], tm)
                    release(i)
            fence()
            if len(tiles) == 4:
                top[0] = 0

        def odd_mixer():
            W, WO = A["odd_w_qkv"][0], A["odd_w_out"][0]
            QT = carve(8, 256)
            KT = carve(8, 512)
            V = carve(4, 1024)
            BI = carve(4, 512)
            for j in range(2):
                i, wt, tw = wtile(W[:, 512 * j:512 * j + 512], 8, 512)
                for m in range(4):
                    lin_col(wt, tw, 128 * m, 128, lambda k: HT[:, k, 0:256], 8, 256, evc(QT[:, 4 * j + m, :]))
                release(i)
            for j in range(2):
                i, wt, tw = wtile(W[:, 1024 + 512 * j:1536 + 512 * j], 8, 512)
                for m in range(4):
                    lin_col(wt, tw, 128 * m, 128, lambda k: HT[:, k, :], 8, 512, evc(KT[:, 4 * j + m, :]))
                release(i)
            for j in range(2):
                i, wt, tw = wtile(W[:, 2048 + 512 * j:2560 + 512 * j], 8, 512)
                lin_tok(wt, tw, 0, 512, ht_tok, 8, range(4), ev(lambda t, j=j: V[:, t, 512 * j:512 * j + 512]))
                release(i)
            fence()
            OT = HT
            attention(biased(BI, A["bias1"], 16, lambda h, qt: QT[64 * (h % 2):64 * (h % 2) + 64, h // 2, 128 * qt:128 * qt + 128],
                             lambda h: KT[64 * (h % 2):64 * (h % 2) + 64, h // 2, :], 512,
                             lambda h, kt: V[:, kt, 64 * h:64 * h + 64], 64,
                             lambda h: 64 * (h % 2), lambda h: OT[64 * (h % 2):64 * (h % 2) + 64, h // 2, 0:256]), 0.125)
            fence()
            top[0] = 0
            project_out(WO, OT, range(2))

        def biased(BI, src, nh, q, k, nk, v, nd, base, outf):
            gone = {}
            got = {}

            def fetch(h):
                got[h] = Q.dma("g", f"b{h % 4}", BI[:, h % 4, :].rearrange("p (q k) -> p q k", k=256),
                              src[h].rearrange("(q p) k -> p q k", p=128), gone.get(h - 4))

            for h in range(min(4, nh)):
                fetch(h)

            def bias(h, qt):
                if qt == 0 and 1 <= h and h + 3 < nh and h >= 1 and (h + 3) not in got:
                    fetch(h + 3)
                return BI[:, h % 4, 256 * qt:256 * qt + 256], got[h], 0, 256

            items = []
            for h in range(nh):
                items.append(dict(q=lambda qt, h=h: q(h, qt), k=k(h), nk=nk, bias=lambda qt, h=h: bias(h, qt),
                                  bias_done=lambda t, h=h: gone.__setitem__(h, t),
                                  v=lambda kt, h=h: v(h, kt), nd=nd, base=base(h), out=outf(h)))
            return items

        def residual_ln(j, gname, bname, l):
            Y = Yh[0]
            R = carve(3, 1024)
            DG = carve(8, 128)
            sm, ss = cstat(4), cstat(4)
            t1 = spread(R[:, 0, :], mod[:, 8 * j:8 * j + 8, 0], DG)
            t2 = spread(R[:, 1, :], col(gname, 8 * l, 8), DG, t1, Q.now("p"))
            t3 = spread(R[:, 2, :], col(bname, 8 * l, 8), DG, t2, Q.now("p"))
            for t in range(2):
                a = vtt(Y[:, t, :], Y[:, t, :], R[:, 0, :], MUL, t1)
                a = stt(X[:, t, :], X[:, t, :], ALPHA, Y[:, t, :], MUL, ADD, a)
                a = act(Y[:, t, :], X[:, t, :], ACT.Identity, a, accum=sm[:, t:t + 1])
                a = vts(sm[:, 2 + t:3 + t], sm[:, t:t + 1], 1.0 / 1024, None, MUL, None, a)
                a = vts(X[:, t, :], X[:, t, :], sm[:, 2 + t:3 + t], None, SUB, None, a)
                a = act(Y[:, t, :], X[:, t, :], ACT.Square, a, accum=ss[:, t:t + 1])
                a = rstd_of(ss[:, t:t + 1], 1, 1.0 / 1024, 1e-5, a)
                a = stt(X[:, t, :], X[:, t, :], ss[:, t:t + 1], R[:, 1, :], MUL, MUL, a, t2)
                vtt(X[:, t, :], X[:, t, :], R[:, 2, :], ADD, a, t3)
            fence()

        def moba_gla():
            W, WO = A["ev_w_in_2"][0], A["ev_w_out_2"][0]
            QM, KM = carve(4, 256), carve(4, 256)
            VM, GV, GG = carve(2, 512), carve(2, 512), carve(2, 512)
            GQ, GKD, GK = carve(2, 256), carve(2, 256), carve(2, 256)
            LR = carve(256)
            W2 = carve(256)
            GD = carve(2, 128)
            G = carve(2, 256)
            tw2 = load(W2[0:16, :], A["ev_gk_w2_2"][0])
            tgd = load(GD, A["gdc"][:, 0:256].rearrange("p (a b) -> p a b", b=128))
            h2 = lambda k: HT[:, k, 0:256]
            for dst, c in ((QM, 0), (KM, 512)):
                i, wt, tw = wtile(W[:, c:c + 512], 8, 512)
                for m in range(4):
                    lin_col(wt, tw, 128 * m, 128, h2, 8, 256, evc(dst[:, m, :]))
                release(i)
            i, wt, tw = wtile(W[:, 1024:1536], 8, 512)
            lin_tok(wt, tw, 0, 512, ht_tok, 8, range(2), ev(lambda t: VM[:, t, :]))
            release(i)
            i, wt, tw = wtile(W[:, 1536:2048], 8, 512)
            for m in range(4):
                lin_col(wt, tw, 128 * m, 128, h2, 8, 256, evc((GQ, GKD)[m // 2][:, m % 2, :]))
            lin_tok(wt, tw, 256, 256, ht_tok, 8, range(2), ev(lambda t: GK[:, t, :]))
            release(i)
            i, wt, tw = wtile(W[:, 2048:2560], 8, 512)
            lin_tok(wt, tw, 0, 512, ht_tok, 8, range(2), ev(lambda t: GV[:, t, :]))
            release(i)
            i, wt, tw = wtile(W[:, 2560:3072], 8, 512)
            lin_tok(wt, tw, 0, 512, ht_tok, 8, range(2), lambda t, p, tok: act(GG[:, t, :], p, ACT.Silu, tok))
            release(i)
            i, wt, tw = wtile(W[:, 3072:3088], 8, 16)
            lin_col(wt, tw, 0, 16, h2, 8, 256, lambda p, tok: vcopy(LR[0:16, :], p, tok))
            release(i)
            fence()
            OT = HT
            for t in range(2):
                b = bank()
                tm = mmi(ps[b][:, 0:256], LR[0:16, 128 * t:128 * t + 128], W2[0:16, :], True, True, tw2)
                vtt(G[:, t, :], ps[b][:, 0:256], row("gkb", 256), ADD, tm)
            L_ = carve(2, 256)
            fl = lambda a: a.rearrange("p a b -> p (a b)")
            t = act(fl(L_), fl(G), ACT.Abs, Q.now("v"))
            t = act(fl(L_), fl(L_), ACT.Exp, t, scale=-1.0)
            t = act(fl(L_), fl(L_), ACT.Ln, t, bias=1.0)
            t = stt(fl(G), fl(G), 0.0, fl(L_), MIN, SUB, t)
            tg = vts(fl(G), fl(G), 1.0 / 16, None, MUL, None, t)
            fence()
            EB, EN, QE, KE = (carve(2, 128) for _ in range(4))
            KEND = carve(256)
            AT = carve(4, 64)
            S = carve(2, 128)
            O = carve(2, 512)
            MIN_, MREV = GD[:, 0, :], GD[:, 1, :]
            for t in range(2):
                for j in range(2):
                    b = bank((0, 1))
                    tm = mmi(ps[b][:, 0:128], G[:, t, 128 * j:128 * j + 128], MIN_, True, True, free[b])
                    act(EB[:, j, :], ps[b][:, 0:128], ACT.Exp, tm, Q.now("v"), Q.now("p"))
                    free[b] = act(EN[:, j, :], ps[b][:, 0:128], ACT.Exp, scale=-1.0)
                te = Q.now("a")
                for j in range(2):
                    stt(QE[:, j, :], GQ[:, j, 128 * t:128 * t + 128], 0.125, EB[:, j, :], MUL, MUL, te, Q.now("p"))
                    tk = vtt(KE[:, j, :], GKD[:, j, 128 * t:128 * t + 128], EN[:, j, :], MUL)
                b = bank((0, 1))
                tm = mmi(ps[b][:, 0:256], MREV, G[:, t, :], True, True, free[b])
                free[b] = a = act(KEND, ps[b][:, 0:256], ACT.Exp, tm)
                tke = vtt(KEND, KEND, GK[:, t, :], MUL, a)
                for c in range(2):
                    r0 = 64 * c
                    rr = slice(r0, r0 + 64)
                    for hh in range(2):
                        for j in range(2):
                            tm = mmi(ps[2 + hh][rr, 64 * j:64 * j + 64], KE[64 * hh:64 * hh + 64, j, rr],
                                     QE[64 * hh:64 * hh + 64, j, rr], True, True, tk, free[2 + hh])
                        free[2 + hh] = ta = vtt(
                            AT[rr, :, :].rearrange("p (j w) t -> p j w t", w=2)[:, :, hh, :],
                            ps[2 + hh][rr, 0:128].rearrange("p (j t) -> p j t", t=64),
                            bc(GD[rr, 0, rr], 2, 1), MUL, tm, Q.now("p"))
                    bo = 4 + c
                    for h in range(4):
                        tm = mmi(ps[bo][rr, 128 * h:128 * h + 128], AT[rr, h, :], GV[rr, t, 128 * h:128 * h + 128],
                                 True, True, ta, free[bo])
                    free[bo] = vcopy(O[rr, t, :], ps[bo][rr, :], tm)
                    first = t == 0 and c == 0
                    if not first:
                        for hh in range(2):
                            for j in range(2):
                                tm = mmi(ps[6 + hh][rr, 128 * j:128 * j + 128], QE[64 * hh:64 * hh + 64, j, rr],
                                         S[64 * hh:64 * hh + 64, j, :], True, True, ts, free[6 + hh])
                            ov = O[rr, t, :].rearrange("p (j w d) -> p j w d", w=2, d=128)[:, :, hh, :]
                            free[6 + hh] = vtt(ov, ov, ps[6 + hh][rr, 0:256].rearrange("p (j d) -> p j d", d=128), ADD, tm)
                    if t == 0 or c == 0:
                        b = bank((0, 1))
                        for h in range(4):
                            hh, j = h % 2, h // 2
                            tm = mmi(ps[b][64 * hh:64 * hh + 64, 128 * j:128 * j + 128], KEND[rr, 64 * h:64 * h + 64],
                                     GV[rr, t, 128 * h:128 * h + 128], True, True, tke, free[b])
                        for j in range(2):
                            if first:
                                ts = vcopy(S[:, j, :], ps[b][:, 128 * j:128 * j + 128], tm)
                            else:
                                ts = stt(S[:, j, :], S[:, j, :], EB[:, j, r0 + 63:r0 + 64],
                                         ps[b][:, 128 * j:128 * j + 128], MUL, ADD, tm)
                        free[b] = ts
            readout(O, 4, GG, "evn", OT, 4, range(2))
            BI = carve(4, 512)
            attention(biased(BI, A["bias2"], 4, lambda h, qt: QM[:, h, 128 * qt:128 * qt + 128], lambda h: KM[:, h, :],
                             256, lambda h, kt: VM[:, kt, 128 * h:128 * h + 128], 128, lambda h: 0,
                             lambda h: OT[:, h, 0:256]), 128 ** -0.5)
            fence()
            top[0] = 0
            project_out(WO, OT, range(2))

        def readout(O, nh, G, wname, OT, c0, tiles):
            ss = cstat(nh * 2)
            SQ = carve(nh * 128)
            for t in tiles:
                tq = heads_rstd(O[:, t, :], nh, 128, 1.0 / 128, EPS, SQ, ss[:, nh * t:nh * t + nh], Q.now("v"))
                ov = O[:, t, :].rearrange("p (h d) -> p h d", d=128)
                tq = vtt(ov, ov, bc(ss[:, nh * t:nh * t + nh], 128, 2), MUL, tq)
                tq = vtt(ov, ov, bc(row(wname, 128), nh, 1), MUL, tq)
                tq = vtt(O[:, t, :], O[:, t, :], G[:, t, :], MUL, tq)
                for q in range(nh // 4):
                    b = bank()
                    for h in range(4):
                        x0 = 512 * q + 128 * h
                        t_ = tr(ps[b][:, 128 * h:128 * h + 128], O[:, t, x0:x0 + 128], tq, free[b])
                    free[b] = copy("a", OT[:, c0 + 4 * q:c0 + 4 * q + 4, 128 * t:128 * t + 128],
                                   ps[b][:, :].rearrange("p (h c) -> p h c", c=128), t_)
            fence()

        def deltanet():
            W, WO = A["od_w_in_2"][0], A["od_w_out_2"][0]
            QKV = [carve(8, 256) for _ in range(3)]
            QC, KC, VC = QKV
            GATE = carve(2, 1024)
            BA = carve(2, 16)
            GD = carve(14, 128)
            tgd = load(GD, A["gdc"].rearrange("p (a b) -> p a b", b=128))
            h2 = lambda k: HT[:, k, 0:256]
            for j in range(6):
                i, wt, tw = wtile(W[:, 512 * j:512 * j + 512], 8, 512)
                for m in range(4):
                    ch = 4 * j + m

                    def e(p, tok, ch=ch):
                        d = QKV[ch // 8][:, ch % 8, :]
                        w = [col("ocw", 24 * k + ch, 1) for k in range(4)]
                        t = act(d, p, ACT.Identity, tok, scale=w[3])
                        for s in (1, 2, 3):
                            t = stt(d[:, s:256], p[:, 0:256 - s], w[3 - s], d[:, s:256], MUL, ADD, t)
                        act(d, d, ACT.Silu, t)
                        return t
                    lin_col(wt, tw, 128 * m, 128, h2, 8, 256, e)
                release(i)
            for j in range(2):
                i, wt, tw = wtile(W[:, 3072 + 512 * j:3584 + 512 * j], 8, 512)
                lin_tok(wt, tw, 0, 512, ht_tok, 8, range(2),
                        lambda t, p, tok, j=j: act(GATE[:, t, 512 * j:512 * j + 512], p, ACT.Silu, tok))
                release(i)
            i, wt, tw = wtile(W[:, 4096:4112], 8, 16)
            lin_tok(wt, tw, 0, 16, ht_tok, 8, range(2), lambda t, p, tok: vcopy(BA[:, t, :], p, tok))
            release(i)
            fence()
            VT = HT[:, 0:4, :].rearrange("p (t a) b -> p t (a b)", t=2)
            KT = HT[:, 4:8, :].rearrange("p (t a) b -> p t (a b)", t=2)
            O = VT
            fl = lambda a: a.rearrange("p a b -> p (a b)")
            MINC, MREV = GD[:, 0, :], GD[:, 1, :]
            BE, G, T1 = (cstat(16).rearrange("p (t h) -> p t h", h=8) for _ in range(3))
            GC, EGE, EGC, BG = (cstat(16).rearrange("p (t h) -> p t h", h=8) for _ in range(4))
            EA = cstat(8)
            t = act(BE, BA[:, :, 0:8], ACT.Exp, scale=-1.0)
            t = vts(BE, BE, 1.0, None, ADD, None, t)
            t = recip(fl(BE), fl(BE), t)
            t = vtt(G, BA[:, :, 8:16], bc(row("dtb", 8), 2, 1), ADD)
            t = act(T1, G, ACT.Abs, t)
            t = act(T1, T1, ACT.Exp, t, scale=-1.0)
            t = act(T1, T1, ACT.Ln, t, bias=1.0)
            t = stt(fl(G), fl(G), 0.0, fl(T1), MAX, ADD, t)
            t = act(EA, row("alog", 8), ACT.Exp, t)
            t = vtt(G, G, bc(EA, 2, 1), MUL, t)
            t = vts(G, G, -1.0, None, MUL, None, t)
            for tt_ in range(2):
                b = bank()
                tm = mmi(ps[b][:, 0:8], MINC, G[:, tt_, :], True, True, t)
                vcopy(GC[:, tt_, :], ps[b][:, 0:8], tm)
                act(EGC[:, tt_, :], ps[b][:, 0:8], ACT.Exp, Q.now("v"))
                b = bank()
                tm = mmi(ps[b][:, 0:8], MREV, G[:, tt_, :], True, True)
                act(EGE[:, tt_, :], ps[b][:, 0:8], ACT.Exp, tm)
            vtt(BG, BE, EGC, MUL, Q.now("a"))
            SQ, RN = carve(512), carve(512)
            for D in (QC, KC):
                for j in range(4):
                    dv = fl(D)[:, 512 * j:512 * j + 512]
                    t = act(SQ, dv, ACT.Square, Q.now("p"))
                    b = bank()
                    tm = mmi(ps[b][:, :], ones[:, :], SQ, True, True, t)
                    t = vts(RN, ps[b][:, :], EPS, None, ADD, None, tm)
                    t = act(RN, RN, ACT.Ln, t)
                    t = act(RN, RN, ACT.Exp, t, scale=-0.5)
                    vtt(dv, dv, RN, MUL, t)
            fence()
            for D, dst in ((KC, KT), (VC, VT)):
                for t in range(2):
                    for q in range(2):
                        b = bank()
                        for h in range(4):
                            tm = tr(ps[b][:, 128 * h:128 * h + 128], D[:, 4 * q + h, 128 * t:128 * t + 128], free[b])
                        free[b] = copy("va"[q], dst[:, t, 512 * q:512 * q + 512], ps[b][:, :], tm)
            fence()
            top[0] -= 1024
            vc = fl(VC)
            EGR, ET, AA, AAT = (vc[:, 512 * i:512 * i + 512].rearrange("p (h c) -> p h c", c=128) for i in range(4))
            E, T, U, W1, B_, ATT, KBG, VB, WV, KCT, QG, KEND, S = (carve(4, 128) for _ in range(13))
            scale = 128 ** -0.5
            b4 = lambda m: bc(m, 4, 1)
            v4 = lambda p: p.rearrange("p (h c) -> p h c", c=128)

            def each(l_, r_, *w, banks=range(8)):
                b = bank(banks)
                for h in range(4):
                    tm = mmi(ps[b][:, 128 * h:128 * h + 128], l_(h), r_(h), True, True, free[b], *w)
                return b, tm

            for gq in range(2):
                h0 = 4 * gq
                for t in range(2):
                    tk = slice(128 * t, 128 * t + 128)
                    ts_ = vcopy(B_, bc(G[:, t, h0:h0 + 4], 128, 2), Q.now("p"))
                    b, tm = each(lambda h: B_[:, h, :], lambda h: MINC, ts_)
                    te = act(fl(EGR), ps[b][:, :], ACT.Exp, tm, Q.now("v"))
                    for h in range(4):
                        pv = ps[b][:, 128 * h:128 * h + 128]
                        g1 = GC[:, t, h0 + h:h0 + h + 1]
                        vts(ET[:, h, :], pv, g1, 0.0, SUB, MIN, tm, te)
                        td = vts(E[:, h, :], pv, g1, 0.0, SUB, MAX)
                    free[b] = td
                    a1 = act(fl(ET), fl(ET), ACT.Exp, td)
                    a2 = act(fl(E), fl(E), ACT.Exp, scale=-1.0)
                    vtt(ET, ET, b4(MINC), MUL, a1, e="g")
                    tE = vtt(E, E, b4(MREV), MUL, a2, e="g")
                    stt(QG, QC[:, h0:h0 + 4, tk], scale, EGR, MUL, MUL, a1, Q.now("p"))
                    b, tm = each(lambda h: KC[:, h0 + h, tk], lambda h: KC[:, h0 + h, tk])
                    for h in range(4):
                        ta = stt(AA[:, h, :], ps[b][:, 128 * h:128 * h + 128], BE[:, t, h0 + h:h0 + h + 1], E[:, h, :],
                                 MUL, MUL, tm, tE)
                    free[b] = ta
                    b, tm = each(lambda h: KC[:, h0 + h, tk], lambda h: QC[:, h0 + h, tk])
                    free[b] = stt(fl(ATT), ps[b][:, :], scale, fl(ET), MUL, MUL, tm, tE)
                    b = bank()
                    for h in range(4):
                        tm = tr(ps[b][:, 128 * h:128 * h + 128], AA[:, h, :], ta, free[b])
                    free[b] = tt_ = copy("a", fl(AAT), ps[b][:, :], tm)
                    x = vtt(T, AA, b4(GD[:, 2, :]), MUL, ta)
                    x = vtt(T, b4(ident[:, :]), T, SUB, x)
                    y = vtt(U, AAT, b4(GD[:, 8, :]), MUL, tt_)
                    tU = vtt(U, b4(ident[:, :]), U, SUB, y)
                    for lv in range(1, 6):
                        z = vtt(B_, AAT, b4(GD[:, 8 + lv, :]), MUL, Q.now("p"))
                        b, tm = each(lambda h: B_[:, h, :], lambda h: T[:, h, :], z, tU)
                        free[b] = w1 = copy("a", fl(W1), ps[b][:, :], tm)
                        b2, tm2 = each(lambda h: W1[:, h, :], lambda h: U[:, h, :], w1)
                        if lv < 5:
                            b, tm = each(lambda h: U[:, h, :], lambda h: W1[:, h, :])
                            free[b] = vtt(fl(T), fl(T), ps[b][:, :], SUB, tm)
                        free[b2] = tU = vtt(fl(U), fl(U), ps[b2][:, :], SUB, tm2, Q.now("p"))
                    ktv = v4(KT[:, t, 512 * gq:512 * gq + 512])
                    vtv = v4(VT[:, t, 512 * gq:512 * gq + 512])
                    hb = lambda a: bc(a[:, t, h0:h0 + 4], 128, 2)
                    vtt(VB, vtv, hb(BE), MUL, Q.now("p"))
                    vtt(KBG, ktv, hb(BG), MUL)
                    x = vtt(KEND, ktv, hb(EGE), MUL)
                    b, tm = each(lambda h: U[:, h, :], lambda h: VB[:, h, :], x)
                    free[b] = copy("v", fl(WV), ps[b][:, :], tm)
                    b, tm = each(lambda h: KBG[:, h, :], lambda h: U[:, h, :])
                    free[b] = tw_ = copy("v", fl(KCT), ps[b][:, :], tm)
                    for c in range(2):
                        r = slice(64 * c, 64 * c + 64)
                        first = t == 0 and c == 0
                        if not first:
                            b = bank()
                            for h in range(4):
                                tm = mmi(ps[b][r, 128 * h:128 * h + 128], KCT[:, h, r], S[:, h, :], True, True, tw_, ts, free[b])
                            free[b] = tw_ = vtt(fl(WV)[r, :], fl(WV)[r, :], ps[b][r, :], SUB, tm)
                        b = bank()
                        for h in range(4):
                            o = ps[b][r, 128 * h:128 * h + 128]
                            if not first:
                                mm(o, QG[:, h, r], S[:, h, :], True, False, free[b])
                            tm = mmi(o, ATT[:, h, r], WV[:, h, :], first, True, tw_, free[b])
                        free[b] = copy("v", O[r, t, 512 * gq:512 * gq + 512], ps[b][r, :], tm)
                        if t == 0 or c == 0:
                            b = bank()
                            for h in range(4):
                                tm = mmi(ps[b][:, 128 * h:128 * h + 128], KEND[r, h, :], WV[r, h, :], True, True, tw_, free[b])
                            if first:
                                ts = copy("v", fl(S), ps[b][:, :], tm)
                            else:
                                for h in range(4):
                                    ts = stt(S[:, h, :], S[:, h, :], EGR[:, h, 64 * c + 63:64 * c + 64],
                                             ps[b][:, 128 * h:128 * h + 128], MUL, ADD, tm)
                            free[b] = ts
            fence()
            OT = QC
            readout(O, 8, GATE, "odn", OT, 0, range(2))
            top[0] = 2048
            project_out(WO, OT, range(2))
            return

        def moe(l):
            CWB = carve(NEXP, 256)
            SG = carve(2, 512)
            HI = carve(2, 512)
            lo = top[0]
            SC, SEL, MS, GT, EQ, CU = (carve(2, 64) for _ in range(6))
            M8 = carve(2, 64)
            GS, GM, G8 = carve(2, 8), carve(2, 8), carve(2, 8)
            sv = cstat(16)
            i, wt, tw = wtile(A["moe_router_w_2"][l], 8, 64)
            lin_tok(wt, tw, 0, 64, ht_tok, 8, range(2), lambda t, p, tok: act(SC[:, t, :], p, ACT.Exp, tok, scale=-1.0),
                    banks=(0, 1))
            release(i)
            fl = lambda a: a.rearrange("p a b -> p (a b)")
            t_ = vts(fl(SC), fl(SC), 1.0, None, ADD, None, Q.now("a"))
            t_ = recip(fl(SC), fl(SC), t_)
            vtt(SEL, SC, bc(row("rb", 64, 64 * l), 2, 1), ADD, t_)

            def choose(mask, v, k, v8, gt, eq, cu, s):
                op("v", lambda g: g.max(v8, v))
                thr = v8[:, k - 1:k]
                vts(gt, v, thr, None, ALU.is_gt, None)
                vts(eq, v, thr, None, ALU.is_equal, None)
                red(s[:, 0:1], gt, ADD)
                vts(s[:, 1:2], s[:, 0:1], -1.0, float(k), MUL, ADD)
                op("v", lambda g: g.tensor_tensor_scan(cu, ones[:, 0:v.shape[1]], eq, 0.0, MUL, ADD))
                stt(eq, cu, s[:, 1:2], eq, ALU.is_le, MUL)
                return vtt(mask, gt, eq, ADD)

            for t in range(2):
                m8 = M8[:, t, :].rearrange("p (g k) -> p g k", k=8)
                for g in range(8):
                    op("v", lambda e, t=t, g=g, m8=m8: e.max(m8[:, g, :], SEL[:, t, 8 * g:8 * g + 8]))
                vtt(GS[:, t, :], m8[:, :, 0], m8[:, :, 1], ADD)
                choose(GM[:, t, :], GS[:, t, :], 4, G8[:, t, :], GT[:, t, 0:8], EQ[:, t, 0:8], CU[:, t, 0:8], sv[:, 0:2])
                gb = bc(GM[:, t, :], 8, 2)
                e8 = lambda a: a[:, t, :].rearrange("p (g k) -> p g k", k=8)
                vtt(e8(MS), e8(SEL), gb, MUL)
                vts(GS[:, t, :], GM[:, t, :], -1.0, 1e30, ADD, MUL)
                vtt(e8(MS), e8(MS), bc(GS[:, t, :], 8, 2), ADD)
                choose(MS[:, t, :], MS[:, t, :], 6, G8[:, t, :], GT[:, t, :], EQ[:, t, :], CU[:, t, :], sv[:, 0:2])
                vtt(MS[:, t, :], MS[:, t, :], SC[:, t, :], MUL)
                red(sv[:, 2:3], MS[:, t, :], ADD)
                vts(sv[:, 2:3], sv[:, 2:3], 1e-20, None, ADD, None)
                recip(sv[:, 3:4], sv[:, 2:3])
                tq = vts(MS[:, t, :], MS[:, t, :], sv[:, 3:4], 2.5, MUL, MUL)
            tw_ = tq

            def route():
                tm = tr(ps[2][0:64, 0:128], MS[:, 0, :], tw_)
                tm = tr(ps[2][0:64, 128:256], MS[:, 1, :])
                t = free[2] = vcopy(CTB[0:64, :], ps[2][0:64, 0:256], tm)
                t = Q.dma("g", "small", A["cws"][l], CTB[0:64, :], t)
                Q.wait("g", [t])
                src = A["cws"][l:l + 1, :, :].rearrange("a e t -> a (e t)").broadcast_to([128, NEXP * 256])
                return Q.dma("g", "small", fl(CWB), src)

            CTB = carve(256)
            gu = {}
            hid = {}
            hifree = [None, None]
            h2 = lambda k: HT[:, k, 0:256]

            def up(n):
                if n == 0:
                    wg, wu = A["sh_w_gate_2"][l], A["sh_w_up_2"][l]
                else:
                    wg, wu = A["moe_w_gate_2"][l, n - 1], A["moe_w_up_2"][l, n - 1]
                half = lambda i: (lambda sl: sl[:, 2048 * i:2048 * i + 2048].rearrange("p (k n) -> p k n", n=256))
                i, slot, tw = weights((half(0), wg.rearrange("(k p) n -> p k n", p=128)),
                                      (half(1), wu.rearrange("(k p) n -> p k n", p=128)))
                tok = []
                r = n % 2
                for g in range(2):
                    wt = half(g)(slot)
                    b = 2 * r + g
                    for m in range(2):
                        for k in range(8):
                            f = mmi if k == 7 else mm
                            tm = f(ps[b][:, 256 * m:256 * m + 256], wt[:, k, 128 * m:128 * m + 128], h2(k),
                                   k == 0, k == 7, tw, free[b])
                    tok.append(tm)
                release(i)
                a = act(SG[:, r, :], ps[2 * r][:, :], ACT.Silu, tok[0], hid.get(n - 2))
                free[2 * r] = a
                if n == 0:
                    t = vtt(HI[:, r, :], SG[:, r, :], ps[1][:, :], MUL, a, tok[1])
                    free[1] = t
                else:
                    t = vtt(SG[:, r, :], SG[:, r, :], ps[2 * r + 1][:, :], MUL, a, tok[1])
                    free[2 * r + 1] = t
                    t = vtt(HI[:, r, :].rearrange("p (f t) -> p f t", t=256),
                            SG[:, r, :].rearrange("p (f t) -> p f t", t=256), bc(CWB[:, n - 1, :], 2, 1), MUL,
                            t, routed, hifree[r], e="g")
                hid[n] = t

            down_at = {}

            def down(n):
                if n == 0:
                    i, slot, tw = weights((lambda sl: sl[:, 0:2048].rearrange("p (k n) -> p k n", n=1024),
                                           A["sh_w_down_2"][l].rearrange("(k p) n -> p k n", p=128)))
                    off = 0
                elif n % 2 == 1:
                    wd = A["moe_w_down_2"][l, n - 1:n + 1]
                    i, slot, tw = weights((lambda sl: sl.rearrange("p (e k n) -> p (e k) n", k=2, n=1024),
                                           wd.rearrange("e (k p) n -> p (e k) n", p=128)))
                    down_at[n + 1] = (i, slot, tw)
                    off = 0
                else:
                    i, slot, tw = down_at[n]
                    off = 2
                wt = slot.rearrange("p (k n) -> p k n", n=1024)
                r = n % 2
                hv = HI[:, r, :].rearrange("p (f t) -> p f t", t=256)
                for t in range(2):
                    for h in range(2):
                        for f in range(2):
                            fn = mmi if f == 1 else mm
                            tm = fn(ps[4 + 2 * t + h][:, :], hv[:, f, 128 * t:128 * t + 128],
                                    wt[:, off + f, 512 * h:512 * h + 512], n == 0 and f == 0, n == NEXP and f == 1,
                                    tw, hid[n])
                hifree[r] = tm
                if n == 0 or n % 2 == 0:
                    release(i)
                return tm

            up(0)
            routed = route()
            for n in range(1, NEXP + 1):
                up(n)
                down(n - 1)
            tm = down(NEXP)
            fence()
            top[0] = 0
            Y = Yh[0] = carve(4, 1024)
            for t in range(2):
                for h in range(2):
                    copy("va"[h], Y[:, t, 512 * h:512 * h + 512], ps[4 + 2 * t + h][:, :], tm)
            fence()

        def second_layer(l):
            top[0] = 0
            modulate(A["ada_w_2"][l], "adab", l, 2)
            for half in range(2):
                top[0] = 0
                cs_ = cstat(8)
                t = vts(cs_, mod[:, 24 * half + 8:24 * half + 16, 0], 1.0, None, ADD, None)
                Q.wait("a", [t])
                transposed(range(2), False, lambda t: cs_, lambda t: mod[:, 24 * half:24 * half + 8, 0])
                top[0] = 0
                if half == 0:
                    (moba_gla if l == 0 else deltanet)()
                    residual_ln(2, "lmg", "lmb", l)
                else:
                    moe(l)
                    residual_ln(5, "lfg", "lfb", l)

        for l in range(2):
            top[0] = 0
            modulate(A["w_mod"][l], "bmod", l, 0)
            tiles = range(4) if l == 0 else range(2)
            for half in range(2):
                top[0] = 0
                tl = range(4) if half == 0 else tiles
                cs_ = cstat(16)
                for w in range(2):
                    scaled(cs_[:, 8 * w:8 * w + 8], 3 * half + 1, w, ("npm", "npf")[half], l)
                Q.wait("v", [Q.now("v")])
                Q.wait("a", [Q.now("v")])
                transposed(tl, True, lambda t: cs_[:, 8 * (t // 2):8 * (t // 2) + 8],
                           lambda t: mod[:, 24 * half:24 * half + 8, t // 2])
                top[0] = 0
                if half == 0:
                    (even_mixer if l == 0 else odd_mixer)()
                    residual_rms(2, "nqm", l, tiles)
                else:
                    conv_ffn(l, tiles)
                    residual_rms(5, "nqf", l, tiles)
            if STAGE == l + 1:
                break

        if STAGE == 0:
            for l in range(2):
                second_layer(l)

        t = Q.dma("s", "outs", out.rearrange("a (t p) d -> p (a t) d", p=128), X[:, 0:2, :], Q.now("v"), Q.now("a"))
        Q.wait("s", [t])

        block = ctx.enter_context(nc.Block())

        @block.tensor
        def _(e):
            for f in Q.q["p"]:
                f(e)

        @block.vector
        def _(e):
            for f in Q.q["v"]:
                f(e)

        @block.scalar
        def _(e):
            for f in Q.q["a"]:
                f(e)

        @block.gpsimd
        def _(e):
            for f in Q.q["g"]:
                f(e)

        @block.sync
        def _(e):
            for f in Q.q["s"]:
                f(e)


STAGE = 0


def shape_constants():
    c = {"cst": np.eye(128, dtype=np.float32)}
    t = np.arange(256)
    inv = (np.float32(10000.0) ** (-np.arange(16, dtype=np.float32) / np.float32(16))).astype(np.float32)
    ang = np.concatenate([(t // 64).astype(np.float32)[:, None] * inv, (t % 64).astype(np.float32)[:, None] * inv], 1)
    c["rope"] = np.concatenate([np.cos(ang), np.sin(ang)], 1).astype(np.float32)
    h = np.zeros((2, 128, 17, 128), np.float32)
    i = np.arange(128)
    s, p = i[:, None], i[None, :]
    for lv in range(7):
        m = 64 >> lv
        blk, right = p // (2 * m), (p // m) % 2
        mid = blk * 2 * m + m
        h[0, :, lv] = np.where(right == 1, (s >= mid) & (s <= p), (s > p) & (s < mid))
        sb_, tb_ = s // (2 * m), p // (2 * m)
        h[0, :, 9 + lv] = (sb_ == tb_) & ((s // m) % 2 == 0) & ((p // m) % 2 == 1)
    h[0, :, 7] = s <= p
    h[0, :, 8] = s > p
    h[0, :, 16] = s == p
    h[1] = h[0][::-1, :, ::-1]
    c["hgc"] = h.reshape(2, 128, 17 * 128)
    return c


def more_constants(c):
    i = np.arange(128)
    s, p = i[:, None], i[None, :]
    g = np.zeros((128, 14, 128), np.float32)
    same = (s // 64) == (p // 64)
    g[:, 0] = same & (s <= p)
    g[:, 1] = same & (s > p)
    for lv in range(6):
        m = 1 << lv
        low = (s // (2 * m) == p // (2 * m)) & ((s // m) % 2 == 1) & ((p // m) % 2 == 0)
        g[:, 2 + lv] = low
        g[:, 8 + lv] = low.T
    c["gdc"] = g.reshape(128, 14 * 128)


def bucket_of(d):
    d = np.maximum(d, 0)
    logd = np.log(np.maximum(d, 1).astype(np.float32) / np.float32(16)).astype(np.float32)
    large = 16 + (logd / np.float32(np.log(2048 / 16)) * np.float32(16)).astype(np.int32)
    return np.where(d < 16, d, np.minimum(large, 31))


def more_arrays(A, I):
    more_constants(A)
    t = np.arange(256)
    dist = t[:, None] - t[None, :]
    own = dist >= 0
    b2 = np.full((4, 256, 256), -1e30, np.float32)
    b2[:, own] = I["rpe_bias_2"].T[:, bucket_of(dist)[own]]
    A["bias2"] = b2
    for name in ("ada_w_2", "ev_w_in_2", "ev_gk_w2_2", "ev_w_out_2", "od_w_in_2", "od_w_out_2", "moe_router_w_2",
                 "moe_w_gate_2", "moe_w_up_2", "moe_w_down_2", "sh_w_gate_2", "sh_w_up_2", "sh_w_down_2"):
        A[name] = I[name]


def kernel(**inputs):
    import concourse.bacc as _bacc
    from concourse.bass_utils import run_bass_kernel_spmd as _run

    I = {k: np.asarray(v) for k, v in inputs.items()}
    A = shape_constants()

    def cols(a):
        a = np.asarray(a, np.float32).reshape(-1, 128)
        return a.T

    A["colp"] = np.ascontiguousarray(np.concatenate([
        cols(I["c"]), cols(I["c_ctx"]), cols(I["c_2"]), cols(I["norm_pre_mix"]), cols(I["norm_post_mix"]),
        cols(I["norm_pre_ffn"]), cols(I["norm_post_ffn"]), cols(I["b_mod"]), cols(I["ada_b_2"]),
        cols(I["ln_mix_g_2"]), cols(I["ln_mix_b_2"]), cols(I["ln_ffn_g_2"]), cols(I["ln_ffn_b_2"]),
        cols(I["ffn_conv_w"]), cols(I["ffn_conv_b"]), cols(I["od_conv_w_2"])], 1))
    A["rowp"] = np.concatenate([I[k].reshape(1, -1) for k in (
        "even_q_norm", "even_k_norm", "hgrn_out_norm", "ev_gk_b_2", "ev_norm_2", "od_norm_2",
        "od_a_log_2", "od_dt_bias_2", "moe_router_b_2")], 1)
    t = np.arange(256)
    r, cc = t // 64, t % 64
    dy = r[None, :] - r[:, None] + 7
    dx = cc[None, :] - cc[:, None] + 15
    c0 = np.clip(cc - 8, 0, 48)[:, None]
    inside = (cc[None, :] >= c0) & (cc[None, :] < c0 + 16)
    b1 = np.full((16, 256, 256), -1e30, np.float32)
    b1[:, inside] = I["odd_rpb"][0][:, dy[inside], dx[inside]]
    A["bias1"] = b1
    for name in ("x", "ctx", "w_mod", "even_w_in", "even_w_out", "odd_w_qkv", "odd_w_out", "ffn_w_up", "ffn_w_down"):
        A[name] = I[name]
    if STAGE == 0:
        more_arrays(A, I)

    nc = _bacc.Bacc("TRN2", target_bir_lowering=False, num_devices=1)
    arrays, aps = {}, {}
    for name, a in A.items():
        a = np.ascontiguousarray(a)
        arrays[f"in_{name}"] = a
        aps[name] = nc.dram_tensor(f"in_{name}", a.shape, mybir.dt.from_np(a.dtype), kind="ExternalInput").ap()
    if STAGE == 0:
        aps["cws"] = nc.dram_tensor("cws", [2, 64, 256], F32, kind="Internal").ap()
    o = nc.dram_tensor("out_0", [1, 256, 1024], F32, kind="ExternalOutput").ap()
    program(nc, aps, o)
    r = _run(nc, [arrays], core_ids=[0])
    return r.results[0]["out_0"]
```

```python
from contextlib import ExitStack

import numpy as np
import concourse.bass as bass
from concourse import mybir

F32 = mybir.dt.float32
ALU = mybir.AluOpType
ACT = mybir.ActivationFunctionType
AX = mybir.AxisListType.X
MUL, ADD, SUB, MAX, MIN = ALU.mult, ALU.add, ALU.subtract, ALU.max, ALU.min

RING = 5
SLOT = 4096
ARENA = 21000
CAP = 64
EPS = 1e-6
ALPHA = float(4 ** 0.25)
NEXP = 64

COLS = {}
_n = 0
for _name, _w in (("c", 8), ("c_ctx", 8), ("c_2", 8), ("npm", 16), ("nqm", 16), ("npf", 16), ("nqf", 16),
                  ("bmod", 96), ("adab", 96), ("lmg", 16), ("lmb", 16), ("lfg", 16), ("lfb", 16),
                  ("cw", 2 * 3 * 44), ("cb", 2 * 44), ("ocw", 4 * 24)):
    COLS[_name] = _n
    _n += _w
NCOL = _n
ROWS = {}
_n = 0
for _name, _w in (("qn", 64), ("kn", 64), ("on", 128), ("gkb", 256), ("evn", 128), ("odn", 128),
                  ("alog", 8), ("dtb", 8), ("rb", 128)):
    ROWS[_name] = _n
    _n += _w
NROW = _n


class Queues:

    def __init__(self, nc, ctx):
        self.nc, self.ctx = nc, ctx
        self.q = {e: [] for e in "pvags"}
        self.sem = {e: ctx.enter_context(nc.semaphore("done_" + e)) for e in "pvag"}
        self.n = {e: 0 for e in "pvag"}
        self.seen = {e: {} for e in "pvags"}
        self.chained = "vag"
        self.pe_count = 0

    def new_sem(self, name):
        self.sem[name] = self.ctx.enter_context(self.nc.semaphore(name))
        self.n[name] = 0
        return name

    def wait(self, e, toks):
        for t in toks:
            if t is None:
                continue
            if isinstance(t, list):
                self.wait(e, t)
                continue
            s, v = t
            if v == 0:
                continue
            if self.seen[e].get(s, 0) >= v:
                continue
            self.seen[e][s] = v
            self.q[e].append(lambda eng, s=self.sem[s], v=v: eng.wait_ge(s, v))

    def op(self, e, f, *w):
        self.wait(e, w)
        if e in self.chained:
            self.wait(e, [(e, self.n[e])])
        self.n[e] += 1
        self.pe_count += e == "p"
        self.q[e].append(lambda eng, s=self.sem[e]: f(eng).then_inc(s, 1))
        return (e, self.n[e])

    def quiet(self, e, f, *w):
        self.wait(e, w)
        self.pe_count += e == "p"
        self.q[e].append(lambda eng: f(eng))

    def dma(self, e, sem, out, in_, *w):
        self.wait(e, w)
        self.n[sem] += 16
        self.q[e].append(lambda eng, s=self.sem[sem]: eng.dma_start(out, in_).then_inc(s, 16))
        return (sem, self.n[sem])

    def now(self, e):
        return (e, self.n[e])

    def enter_if(self, flag, tok, name):
        self.wait("s", [tok])
        saved = (self.q, self.sem, self.n, self.seen)
        self.q = {e: [] for e in "pvags"}
        self.sem = {k: self.ctx.enter_context(self.nc.semaphore(f"{name}_{k}")) for k in self.sem}
        self.n = {k: 0 for k in self.sem}
        self.seen = {e: {} for e in "pvags"}
        self.flag = flag
        self.pe_saved = self.pe_count
        return saved

    def wait_outer(self, e, saved, tok):
        s, v = saved[1][tok[0]], tok[1]
        self.q[e].append(lambda eng: eng.wait_ge(s, v))

    def leave_if(self, saved):
        body, flag = self.q, self.flag
        self.pe_count = self.pe_saved
        self.q, self.sem, self.n, self.seen = saved

        def run(eng, inner):
            v = eng.value_load(flag, min_val=0, max_val=1 << 20)
            with eng.If(v > 0):
                for f in inner:
                    f(eng)

        for e in "pvags":
            self.q[e].append(lambda eng, inner=body[e]: run(eng, inner))

    def enter_branch(self):
        saved = (self.q, dict(self.n), {e: dict(x) for e, x in self.seen.items()})
        self.q = {e: [] for e in "pvags"}
        return saved

    def leave_branch(self, saved, flag):
        body = self.q
        self.q, before, self.seen = saved
        more = {e: [] for e in "pvags"}
        for k, v in self.n.items():
            if v > before[k]:
                more[k if k in "pvag" else "s"].append((self.sem[k], v - before[k]))

        def run(eng, inner, adds):
            v = eng.value_load(flag, min_val=0, max_val=1 << 20)
            with eng.If(v > 0):
                for f in inner:
                    f(eng)
            with eng.Else():
                for s, n in adds:
                    eng.sem_inc(s, n)

        for e in "pvags":
            self.q[e].append(lambda eng, inner=body[e], adds=more[e]: run(eng, inner, adds))


def program(nc, A, out):
    with ExitStack() as ctx:
        Q = Queues(nc, ctx)
        op, quiet = Q.op, Q.quiet

        def sb(name, shape):
            return ctx.enter_context(nc.sbuf_tensor(name, shape, F32))

        ring = sb("ring", [128, RING, SLOT])
        X = sb("X", [128, 4, 1024])
        HT = sb("HT", [128, 8, 512])
        arena = sb("arena", [128, ARENA])
        ident = sb("ident", [128, 128])
        ones = sb("ones", [128, 128])
        colp = sb("colp", [128, NCOL])
        rowp = sb("rowp", [128, NROW])
        mods = sb("mods", [128, 4, 96])
        RF = sb("RF", [128, 512])
        sel4 = sb("sel4", [128, 4])
        flag = ctx.enter_context(nc.sbuf_tensor("flag", [128, 146], mybir.dt.int32))
        csil = sb("csil", [128, 8, 32])
        st = sb("st", [128, 256])
        ps = [ctx.enter_context(nc.psum_tensor(f"ps{i}", [128, 512], F32)) for i in range(8)]
        free = [None] * 8
        bank_at = [0]

        for i in range(RING):
            Q.new_sem(f"w{i}")
        for i in range(4):
            Q.new_sem(f"b{i}")
        Q.new_sem("small")
        Q.new_sem("outs")

        top = [0]

        def carve(*shape):
            n = int(np.prod(shape))
            a = top[0]
            top[0] += n
            assert top[0] <= ARENA, top[0]
            v = arena[:, a:a + n]
            if len(shape) == 2:
                return v.rearrange("p (a b) -> p a b", b=shape[1])
            if len(shape) == 3:
                return v.rearrange("p (a b c) -> p a b c", b=shape[1], c=shape[2])
            return v

        st_top = [0]

        def cstat(n):
            a = st_top[0]
            st_top[0] += n
            assert st_top[0] <= 256
            return st[:, a:a + n]

        small_open = [None]

        def fence(name=""):
            MARKS.append((name, Q.pe_count))
            toks = [Q.now(e) for e in "pvag"] + [Q.now("small")]
            for e in "pvag":
                Q.wait(e, toks)
            st_top[0] = 0
            for i in range(8):
                free[i] = None

        def load(dst, src, *w):
            return Q.dma("g", "small", dst, src, *w)

        jobs = [0]
        released = {}

        def weights(*parts):
            i = jobs[0]
            jobs[0] += 1
            s = i % RING
            if i - RING in released:
                Q.wait("s", [released.pop(i - RING)])
            tok = None
            for dst, src in parts:
                tok = Q.dma("s", f"w{s}", dst(ring[:, s, :]), src)
            return i, ring[:, s, :], tok

        def wtile(src, kc, n):
            i, slot, tok = weights((lambda sl: sl[:, 0:kc * n].rearrange("p (k n) -> p k n", n=n),
                                    src.rearrange("(k p) n -> p k n", p=128)))
            return i, slot[:, 0:kc * n].rearrange("p (k n) -> p k n", n=n), tok

        def release(i):
            released[i] = Q.now("p")

        def bank(banks=range(8)):
            banks = list(banks)
            b = banks[bank_at[0] % len(banks)]
            bank_at[0] += 1
            return b

        def mm(o, l, r, start, stop, *w):
            quiet("p", lambda e: e.matmul(o, l, r, start=start, stop=stop), *w)

        def mmi(o, l, r, start, stop, *w):
            return op("p", lambda e: e.matmul(o, l, r, start=start, stop=stop), *w)

        def tr(o, i, *w):
            k = i.shape[0]
            return op("p", lambda e: e.transpose(o, i, ident[0:k, 0:k]), *w)

        def vtt(o, a, b, f, *w, e="v"):
            return op(e, lambda g: g.tensor_tensor(o, a, b, f), *w)

        def vts(o, a, s1, s2, f1, f2, *w, e="v"):
            if f2 is None:
                return op(e, lambda g: g.tensor_scalar(o, a, s1, None, f1), *w)
            return op(e, lambda g: g.tensor_scalar(o, a, s1, s2, f1, f2), *w)

        def stt(o, a, s, b, f1, f2, *w):
            return op("v", lambda g: g.scalar_tensor_tensor(out=o, in0=a, scalar=s, in1=b, op0=f1, op1=f2), *w)

        def red(o, a, f, *w):
            return op("v", lambda g: g.tensor_reduce(o, a, AX, f), *w)

        def recip(o, a, *w):
            return op("v", lambda g: g.reciprocal(o, a), *w)

        def vcopy(o, a, *w, e="v"):
            return op(e, lambda g: g.tensor_copy(o, a), *w)

        def act(o, a, f, *w, scale=1.0, bias=0.0, accum=None):
            if accum is None:
                return op("a", lambda g: g.activation(o, a, f, scale=scale, bias=bias), *w)
            return op("a", lambda g: g.activation(o, a, f, scale=scale, bias=bias, accum_out=accum), *w)

        def copy(e, o, a, *w):
            if e == "a":
                return act(o, a, ACT.Copy, *w)
            return vcopy(o, a, *w, e=e)

        def bc(ap, n, at):
            shape = list(ap.shape)
            return ap.unsqueeze(at).broadcast_to(shape[:at] + [n] + shape[at:])

        def col(name, i, n):
            return colp[:, COLS[name] + i:COLS[name] + i + n]

        def row(name, n, i=0):
            return rowp[:, ROWS[name] + i:ROWS[name] + i + n]

        def rstd_of(ss, n, scale, eps, *w):
            t = vts(ss, ss, scale, eps, MUL, ADD, *w)
            t = act(ss, ss, ACT.Ln, t)
            return act(ss, ss, ACT.Exp, t, scale=-0.5)

        Q.new_sem("first")
        tF = Q.dma("s", "first", colp[:, :], A["colp"])
        tF = Q.dma("s", "first", sel4[:, :], A["cst"][:, 320:324])
        tI = load(ident[:, :], A["cst"][:, 0:128])
        load(rowp[:, :], A["rowp"][0:1, :].broadcast_to([128, NROW]))
        xv = A["x"].rearrange("a (t p) d -> p (a t) d", p=128)
        cv = A["ctx"].rearrange("a (t p) d -> p (a t) d", p=128)
        load(X[:, 0:2, :], xv)
        tI = load(X[:, 2:4, :], cv)
        op("v", lambda g: g.memset(ones[:, :], 1.0))
        tZ = [tF, op("v", lambda g: g.memset(csil[:, :, :], 0.0))]
        for i, nm in enumerate(("c", "c_ctx", "c_2", "c_2")):
            act(csil[:, :, i], col(nm, 0, 8), ACT.Silu, tZ)
        for e in "pv":
            Q.wait(e, [tF, Q.now("a"), Q.now("v")])

        def mod_of(m):
            return mods[:, m, :].rearrange("p (a b) -> p a b", b=2)

        cur = [0]

        def M():
            return mod_of(cur[0])

        fill = {"left": [], "open": None, "rfree": None}

        def fill_start(m, j, b):
            src = A["w_mod"][m] if m < 2 else A["ada_w_2"][m - 2]
            i, wt, tw = wtile(src[:, 512 * j:512 * j + 512], 8, 512)
            for k in range(8):
                g = k % 4
                f = mmi if k == 7 else mm
                t = f(ps[b][32 * g:32 * g + 32, :], csil[:, k, :], wt[:, k, :], k < 4, k >= 4, tw, free[b])
            release(i)
            t = copy("a", RF[:, :], ps[b][:, :], t, fill["rfree"])
            free[b] = t
            fill["open"] = (m, j, b, t)

        def fill_end():
            m, j, b, t = fill["open"]
            w0 = 0 if m < 2 else 2
            for q in range(4):
                tm = mmi(ps[b][:, 2 * q:2 * q + 2], RF[:, 128 * q:128 * q + 128], sel4[:, w0:w0 + 2], True, True, t, free[b])
            fill["rfree"] = tm
            bias = col(("bmod", "adab")[m // 2], 48 * (m % 2) + 4 * j, 4)
            free[b] = vtt(mod_of(m)[:, 4 * j:4 * j + 4, :], ps[b][:, 0:8].rearrange("p (a b) -> p a b", b=2),
                          bc(bias, 2, 2), ADD, tm)
            fill["open"] = None

        def filler(b):
            if fill["open"]:
                fill_end()
            elif fill["left"]:
                fill_start(*fill["left"].pop(0), b)

        def fill_rest(b):
            while fill["left"] or fill["open"]:
                filler(b)

        def scaled(dst, j, which, wname, l):
            return stt(dst, M()[:, 8 * j:8 * j + 8, which], 1.0, col(wname, 8 * l, 8), ADD, MUL)

        def spread(dst, c, dg, *w):
            t = vtt(dg, bc(ident[:, :], 8, 1), bc(c, 128, 2), MUL, *w)
            for h in range(2):
                b = bank()
                tm = mmi(ps[b][:, :], ones[:, :], dg[:, 4 * h:4 * h + 4, :], True, True, t, free[b])
                t2 = free[b] = copy("va"[h], dst[:, 512 * h:512 * h + 512], ps[b][:, :], tm)
                if h == 0:
                    t0 = t2
            return [t0, t2]

        def transposed(tiles, norm, sc, sh):
            tmp = carve(2, 1024)
            ss = cstat(4)
            used = [None, None]
            if norm:
                for i, t in enumerate(tiles):
                    used[i % 2] = act(tmp[:, i % 2, :], X[:, t, :], ACT.Square, accum=ss[:, t:t + 1])
                tr_ = rstd_of(ss[:, tiles[0]:tiles[-1] + 1], len(tiles), 1.0 / 1024, EPS, Q.now("a"))
                used = [tr_, tr_]
            for i, t in enumerate(tiles):
                if norm:
                    tx = vts(tmp[:, i % 2, :], X[:, t, :], ss[:, t:t + 1], None, MUL, None, used[i % 2])
                    src = tmp[:, i % 2, :]
                else:
                    tx, src = None, X[:, t, :]
                for h in range(2):
                    b = bank()
                    for c in range(4):
                        k = 4 * h + c
                        tt_ = tr(ps[b][:, 128 * c:128 * c + 128], src[:, 128 * k:128 * k + 128], tx, free[b])
                    last = []
                    for c in range(4):
                        k = 4 * h + c
                        o, a = HT[:, k, 128 * t:128 * t + 128], ps[b][:, 128 * c:128 * c + 128]
                        if h == 0:
                            z = vts(o, a, sc(t)[:, k:k + 1], sh(t)[:, k:k + 1], MUL, ADD, tt_)
                        else:
                            z = act(o, a, ACT.Identity, tt_, scale=sc(t)[:, k:k + 1], bias=sh(t)[:, k:k + 1])
                    free[b] = z
                used[i % 2] = tt_
            fence("transposed")

        def lin_tok(wt, tw, c0, n, lhs, kc, tiles, evac, banks=range(8)):
            for t in tiles:
                b = bank(banks)
                for k in range(kc):
                    f = mmi if k == kc - 1 else mm
                    tm = f(ps[b][:, 0:n], lhs(k, t), wt[:, k, c0:c0 + n], k == 0, k == kc - 1, tw, free[b])
                free[b] = evac(t, ps[b][:, 0:n], tm)

        def lin_col(wt, tw, c0, m, rhs, kc, ntok, evac, banks=range(8)):
            b = bank(banks)
            for k in range(kc):
                f = mmi if k == kc - 1 else mm
                tm = f(ps[b][0:m, 0:ntok], wt[:, k, c0:c0 + m], rhs(k), k == 0, k == kc - 1, tw, free[b])
            free[b] = evac(ps[b][0:m, 0:ntok], tm)

        ht_tok = lambda k, t: HT[:, k, 128 * t:128 * t + 128]
        flip = [0]

        def ev(dst):
            def f(t, p, tok):
                flip[0] ^= 1
                return copy("va"[flip[0]], dst(t), p, tok)
            return f

        def evc(dst):
            def f(p, tok):
                flip[0] ^= 1
                return copy("va"[flip[0]], dst, p, tok)
            return f

        def attention(items, scale, nbuf=4):
            P = carve(nbuf, 512)
            PT = carve(2, 4 * 256)
            mx, nm, sm, ri = (cstat(nbuf) for _ in range(4))
            pfree = [None] * nbuf
            ptfree = [None, None]
            S = {}
            seq = [(i, qt) for i in range(len(items)) for qt in range(2)]

            def first(n):
                i, qt = seq[n]
                it = items[i]
                r = n % nbuf
                b = bank((0, 1))
                nk = it["nk"]
                o = ps[b][:, 0:nk]
                t = mmi(o, it["q"](qt), it["k"], True, True, free[b])
                src = o
                tb = []
                if it["bias"] is not None:
                    bv, btok, lo, hi = it["bias"](qt)
                    t = stt(P[:, r, lo:hi], o[:, lo:hi], scale, bv, MUL, ADD, t, btok, pfree[r])
                    if hi < nk:
                        t2 = vts(P[:, r, hi:nk], o[:, hi:nk], scale, None, MUL, None)
                        t = [t, t2]
                    free[b] = t[1] if isinstance(t, list) else t
                    it["bias_done"](t)
                    src = P[:, r, 0:nk]
                t = red(mx[:, r:r + 1], src, MAX, t, pfree[r])
                sc = 1.0 if it["bias"] is not None else scale
                t = vts(nm[:, r:r + 1], mx[:, r:r + 1], -sc, None, MUL, None, t)
                t = act(P[:, r, 0:nk], src, ACT.Exp, t, pfree[r], scale=sc, bias=nm[:, r:r + 1], accum=sm[:, r:r + 1])
                if it["bias"] is None:
                    free[b] = t
                S[n] = t

            def second(n):
                i, qt = seq[n]
                it = items[i]
                r = n % nbuf
                nk = it["nk"]
                t = recip(ri[:, r:r + 1], sm[:, r:r + 1], S[n])
                t = vts(P[:, r, 0:nk], P[:, r, 0:nk], ri[:, r:r + 1], None, MUL, None, t)
                b = bank((2, 3, 4))
                for kt in range(nk // 128):
                    tt_ = tr(ps[b][:, 128 * kt:128 * kt + 128], P[:, r, 128 * kt:128 * kt + 128], t, free[b])
                pfree[r] = tt_
                ptv = PT[:, i % 2, 0:nk * 2].rearrange("p (k q c) -> p k q c", q=2, c=128)
                t = copy("a", ptv[:, :, qt, :], ps[b][:, 0:nk].rearrange("p (k c) -> p k c", c=128), tt_, ptfree[i % 2])
                free[b] = t
                if qt == 1:
                    S["pt", i] = t

            def third(i):
                it = items[i]
                nkt = it["nk"] // 128
                nd, base = it["nd"], it["base"]
                ptv = PT[:, i % 2, 0:nkt * 256].rearrange("p (k q) -> p k q", q=256)
                b = bank((6, 7))
                o = ps[b][base:base + nd, 0:256]
                for kt in range(nkt):
                    f = mmi if kt == nkt - 1 else mm
                    t = f(o, it["v"](kt), ptv[:, kt, :], kt == 0, kt == nkt - 1, S["pt", i], free[b])
                ptfree[i % 2] = t
                free[b] = copy("v", it["out"], o, t)

            N = len(seq)
            for n in range(N + 4):
                if n < N:
                    first(n)
                filler(5)
                if 2 <= n < N + 2:
                    second(n - 2)
                if n >= 4 and (n - 4) % 2 == 1:
                    third((n - 4) // 2)

        def heads_rstd(src, nh, hd, scale, eps, tmp, ss, *w):
            t = act(tmp, src, ACT.Square, *w)
            t = red(ss, tmp.rearrange("p (h d) -> p h d", d=hd), ADD, t)
            return rstd_of(ss, nh, scale, eps, t)

        def even_mixer():
            W, WO = A["even_w_in"][0], A["even_w_out"][0]
            G_ = carve(4, 512)
            V = carve(4, 512)
            Z = [carve(4, 512), carve(4, 512)]
            QB = carve(4, 512)
            keep = top[0]
            AA = carve(4, 768)
            hcol = lambda k: HT[:, k, :]
            i, wt, tw = wtile(W[:, 0:512], 8, 512)
            lin_tok(wt, tw, 0, 512, ht_tok, 8, range(4), lambda t, p, tok: copy(
                "va"[t % 2], AA[:, t, 0:512].rearrange("p (h w d) -> p w h d", w=2, d=64),
                p.rearrange("p (w h d) -> p w h d", w=2, d=64), tok))
            release(i)
            i, wt, tw = wtile(W[:, 512:768], 8, 256)
            lin_tok(wt, tw, 0, 256, ht_tok, 8, range(4), ev(lambda t: AA[:, t, 512:768]))
            release(i)
            i, wt, tw = wtile(W[:, 768:1280], 8, 512)
            for h in range(4):
                def e(p, tok, h=h):
                    t = act(QB[:, h, :], p, ACT.Silu, tok)
                    vts(QB[:, h, :], QB[:, h, :], 128 ** -0.5, None, MUL, None, t)
                    return t
                lin_col(wt, tw, 128 * h, 128, hcol, 8, 512, e)
            release(i)
            for dst, c in ((Z[0], 1280), (Z[1], 1792), (V, 2304), (G_, 2816)):
                i, wt, tw = wtile(W[:, c:c + 512], 8, 512)
                if dst is G_:
                    lin_tok(wt, tw, 0, 512, ht_tok, 8, range(4), lambda t, p, tok: act(G_[:, t, :], p, ACT.Silu, tok))
                else:
                    lin_tok(wt, tw, 0, 512, ht_tok, 8, range(4), ev(lambda t, dst=dst: dst[:, t, :]))
                release(i)
            fence("e")
            OT = HT
            QT = carve(4, 512)
            KT = carve(512)
            work = top[0]
            SQ = carve(640)
            ROT = carve(2, 320)
            cs = carve(2, 64)
            ss = cstat(40)
            tcs = load(cs, A["rope"].rearrange("(t p) c -> p t c", p=128))
            for t in range(4):
                tq = heads_rstd(AA[:, t, 0:640], 10, 64, 1.0 / 64, EPS, SQ, ss[:, 10 * t:10 * t + 10], Q.now("v"))
                hv = AA[:, t, 0:640].rearrange("p (h d) -> p h d", d=64)
                tq = vtt(hv, hv, bc(ss[:, 10 * t:10 * t + 10], 64, 2), MUL, tq)
                tq = [vtt(hv[:, 0:8, :], hv[:, 0:8, :], bc(row("qn", 64), 8, 1), MUL, tq),
                      vtt(hv[:, 8:10, :], hv[:, 8:10, :], bc(row("kn", 64), 2, 1), MUL, tq)]
                if t < 2:
                    x1, x2 = hv[:, :, 0:32], hv[:, :, 32:64]
                    c_, s_ = bc(cs[:, t, 0:32], 10, 1), bc(cs[:, t, 32:64], 10, 1)
                    r0, r1 = (ROT[:, j, :].rearrange("p (h d) -> p h d", d=32) for j in range(2))
                    ta = vtt(r0, x1, s_, MUL, tq, tcs)
                    tb = vtt(r1, x2, s_, MUL, tq)
                    t1 = vtt(x1, x1, c_, MUL, ta)
                    t1 = vtt(x1, x1, r1, SUB, t1, tb)
                    t2 = vtt(x2, x2, c_, MUL, tb)
                    tq = vtt(x2, x2, r0, ADD, t2, ta)
            for t in range(4):
                b = bank()
                for h in range(4):
                    t_ = tr(ps[b][:, 128 * h:128 * h + 128], AA[:, t, 128 * h:128 * h + 128], Q.now("v"), free[b])
                free[b] = copy("v", QT[:, :, 128 * t:128 * t + 128], ps[b][:, :].rearrange("p (h c) -> p h c", c=128), t_)
                b = bank()
                t_ = tr(ps[b][:, 0:128], AA[:, t, 512:640], free[b])
                free[b] = copy("a", KT[:, 128 * t:128 * t + 128], ps[b][:, 0:128], t_)
            fence("e")
            top[0] = work
            items = []
            for h in range(8):
                kv, pr = h // 4, h % 4
                B0 = 64 * kv
                for grp in range(2):
                    k0 = 0 if grp == 0 else 256
                    t0 = 2 * grp
                    items.append(dict(
                        q=lambda qt, B0=B0, pr=pr, t0=t0: QT[B0:B0 + 64, pr, 128 * (t0 + qt):128 * (t0 + qt) + 128],
                        k=KT[B0:B0 + 64, k0:512], nk=512 - k0, bias=None,
                        v=lambda kt, k0=k0, kv=kv: AA[:, k0 // 128 + kt, 640 + 64 * kv:704 + 64 * kv],
                        nd=64, base=64 * (h % 2),
                        out=OT[64 * (h % 2):64 * (h % 2) + 64, h // 2, 256 * grp:256 * grp + 256]))
            attention(items, 0.125)
            fence("e")
            top[0] = keep
            GG = carve(4, 512)
            KTT = carve(4, 512)
            O = carve(4, 512)
            CM = carve(9, 128)
            CK = carve(8, 128)
            E = HT[:, 4:8, :].rearrange("p (h j) (l c) -> p h (j l) c", h=2, c=128)
            QF = carve(2, 128)
            S = carve(512)
            KL = carve(512)
            DL = carve(2)
            AT = carve(2, 128)
            for d in range(2):
                z = Z[d]
                fl = lambda a: a.rearrange("p a b -> p (a b)")
                tc = load(CM, A["hgc"][d, :, 0:1152].rearrange("p (a b) -> p a b", b=128))
                tc = load(CK, A["hgc"][d, :, 1152:2176].rearrange("p (a b) -> p a b", b=128))
                t = act(fl(GG), fl(z), ACT.Abs)
                t = act(fl(GG), fl(GG), ACT.Exp, t, scale=-1.0)
                t = act(fl(GG), fl(GG), ACT.Ln, t, bias=1.0)
                t = stt(fl(GG), fl(z), 0.0, fl(GG), MIN, SUB, t)
                t = vtt(fl(z), fl(GG), fl(z), SUB, t)
                t = act(fl(z), fl(z), ACT.Exp, t)
                for c in range(4):
                    b = bank()
                    for h in range(4):
                        t_ = tr(ps[b][:, 128 * h:128 * h + 128], z[:, c, 128 * h:128 * h + 128], t, free[b])
                    free[b] = copy("a", KTT[:, :, 128 * c:128 * c + 128],
                                   ps[b][:, :].rearrange("p (h c) -> p h c", c=128), t_)
                tkt = Q.now("a")
                qtwo, ktwo, last = (1, 0, 127) if d == 0 else (0, 1, 0)
                order = (2, 3, 0, 1) if d == 0 else (3, 2, 1, 0)
                units = [(n, order[n], h) for n in range(4) for h in range(4)]
                te, tx, tat, tqf = {}, {}, {}, {}
                spent, read = [None, None], [None, None]
                st_ = {"kl": None, "klr": None, "s": None}

                def decays(u):
                    n, c, h = units[u]
                    for j in range(2):
                        b = 2 + j
                        t = mmi(ps[b][:, :], GG[:, c, 128 * h:128 * h + 128], CM[:, 4 * j:4 * j + 4, :], True, True, tc,
                                Q.now("v") if u == 0 else None, free[b])
                        te[u] = free[b] = act(E[:, u % 2, 4 * j:4 * j + 4, :],
                                              ps[b][:, :].rearrange("p (a b) -> p a b", b=128), ACT.Exp, t, spent[u % 2])

                def factors(u):
                    n, c, h = units[u]
                    r = u % 2
                    qv, kv = QB[:, h, 128 * c:128 * c + 128], KTT[:, h, 128 * c:128 * c + 128]
                    vcopy(DL[:, r:r + 1], E[:, r, 7, last:last + 1], te[u])
                    tqf[u] = vtt(QF[:, r, :], E[:, r, 7, :], qv, MUL, te[u], tkt, read[r])
                    for lv in range(7):
                        m = 64 >> lv
                        w3 = lambda a: a.rearrange("p (b w m) -> p b w m", w=2, m=m)
                        e3 = w3(E[:, r, lv, :])
                        vtt(e3[:, :, qtwo, :], e3[:, :, qtwo, :], w3(qv)[:, :, qtwo, :], MUL)
                        tx[u] = vtt(e3[:, :, ktwo, :], e3[:, :, ktwo, :], w3(kv)[:, :, ktwo, :], MUL)

                def scores(u):
                    n, c, h = units[u]
                    r = u % 2
                    qv, kv = QB[:, h, 128 * c:128 * c + 128], KTT[:, h, 128 * c:128 * c + 128]
                    for j in range(2):
                        b = 4 + j
                        for a in range(4):
                            lv = 4 * j + a
                            l_, r_ = (E[:, r, lv, :], E[:, r, lv, :]) if lv < 7 else (kv, qv)
                            t = mmi(ps[b][:, 128 * a:128 * a + 128], l_, r_, True, True, tx[u], free[b])
                        t = free[b] = vtt(E[:, r, 4 * j:4 * j + 4, :], ps[b][:, :].rearrange("p (a b) -> p a b", b=128),
                                          CK[:, 4 * j:4 * j + 4, :], MUL, t)
                    tat[u] = spent[r] = red(AT[:, r, :], E[:, r, :, :].rearrange("p l t -> p t l"), ADD, t, read[r])

                def outputs(u):
                    n, c, h = units[u]
                    r = u % 2
                    bo = 6 + n % 2
                    if h == 0 and n < 3:
                        t = mmi(ps[0][:, :], CM[:, 8, :], GG[:, c, :], True, True, tc, free[0])
                        t = free[0] = act(KL, ps[0][:, :], ACT.Exp, t, st_["klr"])
                        st_["kl"] = vtt(KL, KL, z[:, c, :], MUL, t)
                    oo = ps[bo][:, 128 * h:128 * h + 128]
                    vv = V[:, c, 128 * h:128 * h + 128]
                    sl = S[:, 128 * h:128 * h + 128]
                    if n == 0:
                        t1 = mmi(oo, AT[:, r, :], vv, True, True, tat[u], free[bo])
                    else:
                        mm(oo, AT[:, r, :], vv, True, False, tat[u], free[bo])
                        t1 = mmi(oo, QF[:, r, :], sl, False, True, tqf[u], st_["s"])
                    read[r] = t1
                    if n < 3:
                        t = mmi(ps[0][:, 0:128], KL[:, 128 * h:128 * h + 128], vv, True, True, st_["kl"], free[0])
                        st_["klr"] = t
                        if n == 0:
                            free[0] = copy("v", sl, ps[0][:, 0:128], t, t1)
                        else:
                            free[0] = stt(sl, sl, DL[:, r:r + 1], ps[0][:, 0:128], MUL, ADD, t, t1)
                        st_["s"] = free[0]
                    if h == 3:
                        if d == 0:
                            free[bo] = copy("v", O[:, c, :], ps[bo][:, :], t1)
                        else:
                            free[bo] = vtt(O[:, c, :], O[:, c, :], ps[bo][:, :], ADD, t1)

                decays(0)
                for u in range(16):
                    if u < 15:
                        decays(u + 1)
                    factors(u)
                    filler(1)
                    if u >= 1:
                        outputs(u - 1)
                    filler(1)
                    scores(u)
                outputs(15)
                fence("hgrn")
            fill_rest(1)
            fence("mods")
            ss = cstat(16)
            SQ = GG
            for t in range(4):
                tq = heads_rstd(O[:, t, :], 4, 128, 1.0 / 128, EPS, SQ[:, t, :], ss[:, 4 * t:4 * t + 4])
                ov = O[:, t, :].rearrange("p (h d) -> p h d", d=128)
                tq = vtt(ov, ov, bc(ss[:, 4 * t:4 * t + 4], 128, 2), MUL, tq)
                tq = vtt(ov, ov, bc(row("on", 128), 4, 1), MUL, tq)
                tq = vtt(O[:, t, :], O[:, t, :], G_[:, t, :], MUL, tq)
                b = bank()
                for h in range(4):
                    t_ = tr(ps[b][:, 128 * h:128 * h + 128], O[:, t, 128 * h:128 * h + 128], tq, free[b])
                free[b] = copy("a", OT[:, 4:8, 128 * t:128 * t + 128], ps[b][:, :].rearrange("p (h c) -> p h c", c=128), t_)
            fence("e")
            top[0] = 0
            project_out(WO, OT, range(4))

        Yh = [None]

        def project_out(WO, OT, tiles):
            Y = Yh[0] = carve(4, 1024)
            for h in range(2):
                i, wt, tw = wtile(WO[:, 512 * h:512 * h + 512], 8, 512)
                lin_tok(wt, tw, 0, 512, lambda k, t: OT[:, k, 128 * t:128 * t + 128], 8, tiles,
                        ev(lambda t: Y[:, t, 512 * h:512 * h + 512]))
                release(i)
            fence("project_out")

        def residual_rms(j, wname, l, tiles):
            Y = Yh[0]
            R = carve(2, 1024)
            DG = carve(8, 128)
            SQ = carve(1024)
            cc = cstat(16)
            ss = cstat(4)
            tg = []
            for w in range(2 if len(tiles) == 4 else 1):
                t = vtt(cc[:, 8 * w:8 * w + 8], M()[:, 8 * j:8 * j + 8, w], col(wname, 8 * l, 8), MUL)
                tg += spread(R[:, w, :], cc[:, 8 * w:8 * w + 8], DG, t, Q.now("p"))
            for t in tiles:
                act(SQ, Y[:, t, :], ACT.Square, Q.now("a"), accum=ss[:, t:t + 1])
            tq = rstd_of(ss[:, 0:len(tiles)], len(tiles), 1.0 / 1024, EPS, Q.now("a"))
            for t in tiles:
                a = stt(Y[:, t, :], Y[:, t, :], ss[:, t:t + 1], R[:, t // 2, :], MUL, MUL, tq, tg)
                vtt(X[:, t, :], X[:, t, :], Y[:, t, :], ADD, a)
            fence("residual_rms")

        def conv_ffn(l, tiles):
            NT = 128 * len(tiles)
            ns = len(tiles) // 2
            WU, WD = A["ffn_w_up"][l], A["ffn_w_down"][l]
            HID = carve(22, NT)
            CB = carve(4, NT)
            cbf = [None] * 4
            for j in range(11):
                c = 256 * j
                i, slot, tw = weights(
                    (lambda sl: sl.rearrange("p (k n) -> p k n", n=512)[:, :, 0:256],
                     WU[:, c:c + 256].rearrange("(k p) n -> p k n", p=128)),
                    (lambda sl: sl.rearrange("p (k n) -> p k n", n=512)[:, :, 256:512],
                     WU[:, 2816 + c:2816 + c + 256].rearrange("(k p) n -> p k n", p=128)))
                wt = slot.rearrange("p (k n) -> p k n", n=512)
                for s in range(2):
                    m = 2 * j + s
                    done = []
                    for g in range(2):
                        ch = 22 * g + m
                        r = 2 * (m % 2) + g

                        def e(p, tok, ch=ch, r=r):
                            w0, w1, w2 = (col("cw", (3 * l + k) * 44 + ch, 1) for k in range(3))
                            cb = CB[:, r, :]
                            t = act(cb, p, ACT.Identity, tok, cbf[r], scale=w1, bias=col("cb", 44 * l + ch, 1))
                            cv = cb.rearrange("p (s t) -> p s t", s=ns)
                            pv = p.rearrange("p (s t) -> p s t", s=ns)
                            t = stt(cv[:, :, 1:256], pv[:, :, 0:255], w0, cv[:, :, 1:256], MUL, ADD, t)
                            t = stt(cv[:, :, 0:255], pv[:, :, 1:256], w2, cv[:, :, 0:255], MUL, ADD, t)
                            done.append(t)
                            return t
                        lin_col(wt, tw, 256 * g + 128 * s, 128, lambda k: HT[:, k, 0:NT], 8, NT, e)
                    ra, rg = 2 * (m % 2), 2 * (m % 2) + 1
                    t = act(CB[:, rg, :], CB[:, rg, :], ACT.Silu, done[1])
                    t = vtt(HID[:, m, :], CB[:, rg, :], CB[:, ra, :], MUL, t, done[0], e="g")
                    cbf[ra] = cbf[rg] = t
                release(i)
            fence("e")
            top[0] = 22 * NT
            Y = Yh[0] = carve(4, 1024)
            for h in range(2):
                bs = [4 * h + t for t in tiles]
                for q in range(3):
                    kc = (8, 8, 6)[q]
                    i, wt, tw = wtile(WD[1024 * q:1024 * q + 128 * kc, 512 * h:512 * h + 512], kc, 512)
                    for t in tiles:
                        for k in range(kc):
                            f = mmi if k == kc - 1 else mm
                            tm = f(ps[bs[t]][:, :], HID[:, 8 * q + k, 128 * t:128 * t + 128], wt[:, k, :],
                                   q == 0 and k == 0, q == 2 and k == kc - 1, tw)
                        if q == 2:
                            copy("va"[t % 2], Y[:, t, 512 * h:512 * h + 512], ps[bs[t]][:, :], tm)
                    release(i)
            fence("e")
            if len(tiles) == 4:
                top[0] = 0

        def odd_mixer():
            W, WO = A["odd_w_qkv"][0], A["odd_w_out"][0]
            QT = carve(8, 256)
            KT = carve(8, 512)
            V = carve(4, 1024)
            BI = carve(4, 512)
            for j in range(2):
                i, wt, tw = wtile(W[:, 512 * j:512 * j + 512], 8, 512)
                for m in range(4):
                    lin_col(wt, tw, 128 * m, 128, lambda k: HT[:, k, 0:256], 8, 256, evc(QT[:, 4 * j + m, :]))
                release(i)
            for j in range(2):
                i, wt, tw = wtile(W[:, 1024 + 512 * j:1536 + 512 * j], 8, 512)
                for m in range(4):
                    lin_col(wt, tw, 128 * m, 128, lambda k: HT[:, k, :], 8, 512, evc(KT[:, 4 * j + m, :]))
                release(i)
            for j in range(2):
                i, wt, tw = wtile(W[:, 2048 + 512 * j:2560 + 512 * j], 8, 512)
                lin_tok(wt, tw, 0, 512, ht_tok, 8, range(4), ev(lambda t, j=j: V[:, t, 512 * j:512 * j + 512]))
                release(i)
            fence("odd_mixer")
            OT = HT
            attention(biased(BI, A["bias1"], 16, lambda h, qt: QT[64 * (h % 2):64 * (h % 2) + 64, h // 2, 128 * qt:128 * qt + 128],
                             lambda h: KT[64 * (h % 2):64 * (h % 2) + 64, h // 2, :], 512,
                             lambda h, kt: V[:, kt, 64 * h:64 * h + 64], 64,
                             lambda h: 64 * (h % 2), lambda h: OT[64 * (h % 2):64 * (h % 2) + 64, h // 2, 0:256]), 0.125)
            fence("odd_mixer")
            top[0] = 0
            project_out(WO, OT, range(2))

        def biased(BI, src, nh, q, k, nk, v, nd, base, outf):
            gone = {}
            got = {}

            def fetch(h):
                got[h] = Q.dma("g", f"b{h % 4}", BI[:, h % 4, :].rearrange("p (q k) -> p q k", k=256),
                              src[h].rearrange("(q p) k -> p q k", p=128), gone.get(h - 4))

            for h in range(min(4, nh)):
                fetch(h)

            def bias(h, qt):
                if qt == 0 and 1 <= h and h + 3 < nh and h >= 1 and (h + 3) not in got:
                    fetch(h + 3)
                return BI[:, h % 4, 256 * qt:256 * qt + 256], got[h], 0, 256

            items = []
            for h in range(nh):
                items.append(dict(q=lambda qt, h=h: q(h, qt), k=k(h), nk=nk, bias=lambda qt, h=h: bias(h, qt),
                                  bias_done=lambda t, h=h: gone.__setitem__(h, t),
                                  v=lambda kt, h=h: v(h, kt), nd=nd, base=base(h), out=outf(h)))
            return items

        def residual_ln(j, gname, bname, l):
            Y = Yh[0]
            R = carve(3, 1024)
            DG = carve(8, 128)
            sm, ss = cstat(4), cstat(4)
            t1 = spread(R[:, 0, :], M()[:, 8 * j:8 * j + 8, 0], DG)
            t2 = spread(R[:, 1, :], col(gname, 8 * l, 8), DG, t1, Q.now("p"))
            t3 = spread(R[:, 2, :], col(bname, 8 * l, 8), DG, t2, Q.now("p"))
            for t in range(2):
                a = vtt(Y[:, t, :], Y[:, t, :], R[:, 0, :], MUL, t1)
                a = stt(X[:, t, :], X[:, t, :], ALPHA, Y[:, t, :], MUL, ADD, a)
                a = act(Y[:, t, :], X[:, t, :], ACT.Identity, a, accum=sm[:, t:t + 1])
                a = vts(sm[:, 2 + t:3 + t], sm[:, t:t + 1], 1.0 / 1024, None, MUL, None, a)
                a = vts(X[:, t, :], X[:, t, :], sm[:, 2 + t:3 + t], None, SUB, None, a)
                a = act(Y[:, t, :], X[:, t, :], ACT.Square, a, accum=ss[:, t:t + 1])
                a = rstd_of(ss[:, t:t + 1], 1, 1.0 / 1024, 1e-5, a)
                a = stt(X[:, t, :], X[:, t, :], ss[:, t:t + 1], R[:, 1, :], MUL, MUL, a, t2)
                vtt(X[:, t, :], X[:, t, :], R[:, 2, :], ADD, a, t3)
            fence("residual_ln")

        def moba_gla():
            W, WO = A["ev_w_in_2"][0], A["ev_w_out_2"][0]
            QM, KM = carve(4, 256), carve(4, 256)
            VM, GV, GG = carve(2, 512), carve(2, 512), carve(2, 512)
            GQ, GKD, GK = carve(2, 256), carve(2, 256), carve(2, 256)
            LR = carve(256)
            W2 = carve(256)
            GD = carve(2, 128)
            G = carve(2, 256)
            tw2 = load(W2[0:16, :], A["ev_gk_w2_2"][0])
            tgd = load(GD, A["gdc"][:, 0:256].rearrange("p (a b) -> p a b", b=128))
            h2 = lambda k: HT[:, k, 0:256]
            for dst, c in ((QM, 0), (KM, 512)):
                i, wt, tw = wtile(W[:, c:c + 512], 8, 512)
                for m in range(4):
                    lin_col(wt, tw, 128 * m, 128, h2, 8, 256, evc(dst[:, m, :]))
                release(i)
            i, wt, tw = wtile(W[:, 1024:1536], 8, 512)
            lin_tok(wt, tw, 0, 512, ht_tok, 8, range(2), ev(lambda t: VM[:, t, :]))
            release(i)
            i, wt, tw = wtile(W[:, 1536:2048], 8, 512)
            for m in range(4):
                lin_col(wt, tw, 128 * m, 128, h2, 8, 256, evc((GQ, GKD)[m // 2][:, m % 2, :]))
            lin_tok(wt, tw, 256, 256, ht_tok, 8, range(2), ev(lambda t: GK[:, t, :]))
            release(i)
            i, wt, tw = wtile(W[:, 2048:2560], 8, 512)
            lin_tok(wt, tw, 0, 512, ht_tok, 8, range(2), ev(lambda t: GV[:, t, :]))
            release(i)
            i, wt, tw = wtile(W[:, 2560:3072], 8, 512)
            lin_tok(wt, tw, 0, 512, ht_tok, 8, range(2), lambda t, p, tok: act(GG[:, t, :], p, ACT.Silu, tok))
            release(i)
            i, wt, tw = wtile(W[:, 3072:3088], 8, 16)
            lin_col(wt, tw, 0, 16, h2, 8, 256, lambda p, tok: vcopy(LR[0:16, :], p, tok))
            release(i)
            fence("moba_gla")
            OT = HT
            for t in range(2):
                b = bank()
                tm = mmi(ps[b][:, 0:256], LR[0:16, 128 * t:128 * t + 128], W2[0:16, :], True, True, tw2)
                vtt(G[:, t, :], ps[b][:, 0:256], row("gkb", 256), ADD, tm)
            L_ = carve(2, 256)
            fl = lambda a: a.rearrange("p a b -> p (a b)")
            t = act(fl(L_), fl(G), ACT.Abs, Q.now("v"))
            t = act(fl(L_), fl(L_), ACT.Exp, t, scale=-1.0)
            t = act(fl(L_), fl(L_), ACT.Ln, t, bias=1.0)
            t = stt(fl(G), fl(G), 0.0, fl(L_), MIN, SUB, t)
            tg = vts(fl(G), fl(G), 1.0 / 16, None, MUL, None, t)
            fence("moba_gla")
            EB, EN, QE, KE = (carve(2, 128) for _ in range(4))
            KEND = carve(256)
            AT = carve(4, 64)
            S = carve(2, 128)
            O = carve(2, 512)
            MIN_, MREV = GD[:, 0, :], GD[:, 1, :]
            for t in range(2):
                for j in range(2):
                    b = bank((0, 1))
                    tm = mmi(ps[b][:, 0:128], G[:, t, 128 * j:128 * j + 128], MIN_, True, True, free[b])
                    act(EB[:, j, :], ps[b][:, 0:128], ACT.Exp, tm, Q.now("v"), Q.now("p"))
                    free[b] = act(EN[:, j, :], ps[b][:, 0:128], ACT.Exp, scale=-1.0)
                te = Q.now("a")
                for j in range(2):
                    stt(QE[:, j, :], GQ[:, j, 128 * t:128 * t + 128], 0.125, EB[:, j, :], MUL, MUL, te, Q.now("p"))
                    tk = vtt(KE[:, j, :], GKD[:, j, 128 * t:128 * t + 128], EN[:, j, :], MUL)
                b = bank((0, 1))
                tm = mmi(ps[b][:, 0:256], MREV, G[:, t, :], True, True, free[b])
                free[b] = a = act(KEND, ps[b][:, 0:256], ACT.Exp, tm)
                tke = vtt(KEND, KEND, GK[:, t, :], MUL, a)
                for c in range(2):
                    r0 = 64 * c
                    rr = slice(r0, r0 + 64)
                    for hh in range(2):
                        for j in range(2):
                            tm = mmi(ps[2 + hh][rr, 64 * j:64 * j + 64], KE[64 * hh:64 * hh + 64, j, rr],
                                     QE[64 * hh:64 * hh + 64, j, rr], True, True, tk, free[2 + hh])
                        free[2 + hh] = ta = vtt(
                            AT[rr, :, :].rearrange("p (j w) t -> p j w t", w=2)[:, :, hh, :],
                            ps[2 + hh][rr, 0:128].rearrange("p (j t) -> p j t", t=64),
                            bc(GD[rr, 0, rr], 2, 1), MUL, tm, Q.now("p"))
                    bo = 4 + c
                    for h in range(4):
                        tm = mmi(ps[bo][rr, 128 * h:128 * h + 128], AT[rr, h, :], GV[rr, t, 128 * h:128 * h + 128],
                                 True, True, ta, free[bo])
                    free[bo] = vcopy(O[rr, t, :], ps[bo][rr, :], tm)
                    first = t == 0 and c == 0
                    if not first:
                        for hh in range(2):
                            for j in range(2):
                                tm = mmi(ps[6 + hh][rr, 128 * j:128 * j + 128], QE[64 * hh:64 * hh + 64, j, rr],
                                         S[64 * hh:64 * hh + 64, j, :], True, True, ts, free[6 + hh])
                            ov = O[rr, t, :].rearrange("p (j w d) -> p j w d", w=2, d=128)[:, :, hh, :]
                            free[6 + hh] = vtt(ov, ov, ps[6 + hh][rr, 0:256].rearrange("p (j d) -> p j d", d=128), ADD, tm)
                    if t == 0 or c == 0:
                        b = bank((0, 1))
                        for h in range(4):
                            hh, j = h % 2, h // 2
                            tm = mmi(ps[b][64 * hh:64 * hh + 64, 128 * j:128 * j + 128], KEND[rr, 64 * h:64 * h + 64],
                                     GV[rr, t, 128 * h:128 * h + 128], True, True, tke, free[b])
                        for j in range(2):
                            if first:
                                ts = vcopy(S[:, j, :], ps[b][:, 128 * j:128 * j + 128], tm)
                            else:
                                ts = stt(S[:, j, :], S[:, j, :], EB[:, j, r0 + 63:r0 + 64],
                                         ps[b][:, 128 * j:128 * j + 128], MUL, ADD, tm)
                        free[b] = ts
            readout(O, 4, GG, "evn", OT, 4, range(2))
            BI = carve(4, 512)
            attention(biased(BI, A["bias2"], 4, lambda h, qt: QM[:, h, 128 * qt:128 * qt + 128], lambda h: KM[:, h, :],
                             256, lambda h, kt: VM[:, kt, 128 * h:128 * h + 128], 128, lambda h: 0,
                             lambda h: OT[:, h, 0:256]), 128 ** -0.5)
            fence("moba_gla")
            top[0] = 0
            project_out(WO, OT, range(2))

        def readout(O, nh, G, wname, OT, c0, tiles):
            ss = cstat(nh * 2)
            SQ = carve(nh * 128)
            for t in tiles:
                tq = heads_rstd(O[:, t, :], nh, 128, 1.0 / 128, EPS, SQ, ss[:, nh * t:nh * t + nh], Q.now("v"))
                ov = O[:, t, :].rearrange("p (h d) -> p h d", d=128)
                tq = vtt(ov, ov, bc(ss[:, nh * t:nh * t + nh], 128, 2), MUL, tq)
                tq = vtt(ov, ov, bc(row(wname, 128), nh, 1), MUL, tq)
                tq = vtt(O[:, t, :], O[:, t, :], G[:, t, :], MUL, tq)
                for q in range(nh // 4):
                    b = bank()
                    for h in range(4):
                        x0 = 512 * q + 128 * h
                        t_ = tr(ps[b][:, 128 * h:128 * h + 128], O[:, t, x0:x0 + 128], tq, free[b])
                    free[b] = copy("a", OT[:, c0 + 4 * q:c0 + 4 * q + 4, 128 * t:128 * t + 128],
                                   ps[b][:, :].rearrange("p (h c) -> p h c", c=128), t_)
            fence("readout")

        def deltanet():
            W, WO = A["od_w_in_2"][0], A["od_w_out_2"][0]
            QKV = [carve(8, 256) for _ in range(3)]
            QC, KC, VC = QKV
            GATE = carve(2, 1024)
            BA = carve(2, 16)
            GD = carve(14, 128)
            tgd = load(GD, A["gdc"].rearrange("p (a b) -> p a b", b=128))
            h2 = lambda k: HT[:, k, 0:256]
            for j in range(6):
                i, wt, tw = wtile(W[:, 512 * j:512 * j + 512], 8, 512)
                for m in range(4):
                    ch = 4 * j + m

                    def e(p, tok, ch=ch):
                        d = QKV[ch // 8][:, ch % 8, :]
                        w = [col("ocw", 24 * k + ch, 1) for k in range(4)]
                        t = act(d, p, ACT.Identity, tok, scale=w[3])
                        for s in (1, 2, 3):
                            t = stt(d[:, s:256], p[:, 0:256 - s], w[3 - s], d[:, s:256], MUL, ADD, t)
                        act(d, d, ACT.Silu, t)
                        return t
                    lin_col(wt, tw, 128 * m, 128, h2, 8, 256, e)
                release(i)
            for j in range(2):
                i, wt, tw = wtile(W[:, 3072 + 512 * j:3584 + 512 * j], 8, 512)
                lin_tok(wt, tw, 0, 512, ht_tok, 8, range(2),
                        lambda t, p, tok, j=j: act(GATE[:, t, 512 * j:512 * j + 512], p, ACT.Silu, tok))
                release(i)
            i, wt, tw = wtile(W[:, 4096:4112], 8, 16)
            lin_tok(wt, tw, 0, 16, ht_tok, 8, range(2), lambda t, p, tok: vcopy(BA[:, t, :], p, tok))
            release(i)
            fence("e")
            VT = HT[:, 0:4, :].rearrange("p (t a) b -> p t (a b)", t=2)
            KT = HT[:, 4:8, :].rearrange("p (t a) b -> p t (a b)", t=2)
            O = VT
            fl = lambda a: a.rearrange("p a b -> p (a b)")
            MINC, MREV = GD[:, 0, :], GD[:, 1, :]
            BE, G, T1 = (cstat(16).rearrange("p (t h) -> p t h", h=8) for _ in range(3))
            GC, EGE, EGC, BG = (cstat(16).rearrange("p (t h) -> p t h", h=8) for _ in range(4))
            EA = cstat(8)
            t = act(BE, BA[:, :, 0:8], ACT.Exp, scale=-1.0)
            t = vts(BE, BE, 1.0, None, ADD, None, t)
            t = recip(fl(BE), fl(BE), t)
            t = vtt(G, BA[:, :, 8:16], bc(row("dtb", 8), 2, 1), ADD)
            t = act(T1, G, ACT.Abs, t)
            t = act(T1, T1, ACT.Exp, t, scale=-1.0)
            t = act(T1, T1, ACT.Ln, t, bias=1.0)
            t = stt(fl(G), fl(G), 0.0, fl(T1), MAX, ADD, t)
            t = act(EA, row("alog", 8), ACT.Exp, t)
            t = vtt(G, G, bc(EA, 2, 1), MUL, t)
            t = vts(G, G, -1.0, None, MUL, None, t)
            for tt_ in range(2):
                b = bank()
                tm = mmi(ps[b][:, 0:8], MINC, G[:, tt_, :], True, True, t)
                vcopy(GC[:, tt_, :], ps[b][:, 0:8], tm)
                act(EGC[:, tt_, :], ps[b][:, 0:8], ACT.Exp, Q.now("v"))
                b = bank()
                tm = mmi(ps[b][:, 0:8], MREV, G[:, tt_, :], True, True)
                act(EGE[:, tt_, :], ps[b][:, 0:8], ACT.Exp, tm)
            vtt(BG, BE, EGC, MUL, Q.now("a"))
            SQ, RN = carve(512), carve(512)
            for D in (QC, KC):
                for j in range(4):
                    dv = fl(D)[:, 512 * j:512 * j + 512]
                    t = act(SQ, dv, ACT.Square, Q.now("p"))
                    b = bank()
                    tm = mmi(ps[b][:, :], ones[:, :], SQ, True, True, t)
                    t = vts(RN, ps[b][:, :], EPS, None, ADD, None, tm)
                    t = act(RN, RN, ACT.Ln, t)
                    t = act(RN, RN, ACT.Exp, t, scale=-0.5)
                    vtt(dv, dv, RN, MUL, t)
            fence("e")
            for D, dst in ((KC, KT), (VC, VT)):
                for t in range(2):
                    for q in range(2):
                        b = bank()
                        for h in range(4):
                            tm = tr(ps[b][:, 128 * h:128 * h + 128], D[:, 4 * q + h, 128 * t:128 * t + 128], free[b])
                        free[b] = copy("va"[q], dst[:, t, 512 * q:512 * q + 512], ps[b][:, :], tm)
            fence("e")
            top[0] -= 1024
            vc = fl(VC)
            EGR, ET, AA, AAT = (vc[:, 512 * i:512 * i + 512].rearrange("p (h c) -> p h c", c=128) for i in range(4))
            E, T, U, W1, B_, ATT, KBG, VB, WV, KCT, QG, KEND, S = (carve(4, 128) for _ in range(13))
            scale = 128 ** -0.5
            b4 = lambda m: bc(m, 4, 1)
            v4 = lambda p: p.rearrange("p (h c) -> p h c", c=128)

            def each(l_, r_, *w, banks=range(8)):
                b = bank(banks)
                for h in range(4):
                    tm = mmi(ps[b][:, 128 * h:128 * h + 128], l_(h), r_(h), True, True, free[b], *w)
                return b, tm

            for gq in range(2):
                h0 = 4 * gq
                for t in range(2):
                    tk = slice(128 * t, 128 * t + 128)
                    ts_ = vcopy(B_, bc(G[:, t, h0:h0 + 4], 128, 2), Q.now("p"))
                    b, tm = each(lambda h: B_[:, h, :], lambda h: MINC, ts_)
                    te = act(fl(EGR), ps[b][:, :], ACT.Exp, tm, Q.now("v"))
                    for h in range(4):
                        pv = ps[b][:, 128 * h:128 * h + 128]
                        g1 = GC[:, t, h0 + h:h0 + h + 1]
                        vts(ET[:, h, :], pv, g1, 0.0, SUB, MIN, tm, te)
                        td = vts(E[:, h, :], pv, g1, 0.0, SUB, MAX)
                    free[b] = td
                    a1 = act(fl(ET), fl(ET), ACT.Exp, td)
                    a2 = act(fl(E), fl(E), ACT.Exp, scale=-1.0)
                    vtt(ET, ET, b4(MINC), MUL, a1, e="g")
                    tE = vtt(E, E, b4(MREV), MUL, a2, e="g")
                    stt(QG, QC[:, h0:h0 + 4, tk], scale, EGR, MUL, MUL, a1, Q.now("p"))
                    b, tm = each(lambda h: KC[:, h0 + h, tk], lambda h: KC[:, h0 + h, tk])
                    for h in range(4):
                        ta = stt(AA[:, h, :], ps[b][:, 128 * h:128 * h + 128], BE[:, t, h0 + h:h0 + h + 1], E[:, h, :],
                                 MUL, MUL, tm, tE)
                    free[b] = ta
                    b, tm = each(lambda h: KC[:, h0 + h, tk], lambda h: QC[:, h0 + h, tk])
                    free[b] = stt(fl(ATT), ps[b][:, :], scale, fl(ET), MUL, MUL, tm, tE)
                    b = bank()
                    for h in range(4):
                        tm = tr(ps[b][:, 128 * h:128 * h + 128], AA[:, h, :], ta, free[b])
                    free[b] = tt_ = copy("a", fl(AAT), ps[b][:, :], tm)
                    x = vtt(T, AA, b4(GD[:, 2, :]), MUL, ta)
                    x = vtt(T, b4(ident[:, :]), T, SUB, x)
                    y = vtt(U, AAT, b4(GD[:, 8, :]), MUL, tt_)
                    tU = vtt(U, b4(ident[:, :]), U, SUB, y)
                    for lv in range(1, 6):
                        z = vtt(B_, AAT, b4(GD[:, 8 + lv, :]), MUL, Q.now("p"))
                        b, tm = each(lambda h: B_[:, h, :], lambda h: T[:, h, :], z, tU)
                        free[b] = w1 = copy("a", fl(W1), ps[b][:, :], tm)
                        b2, tm2 = each(lambda h: W1[:, h, :], lambda h: U[:, h, :], w1)
                        if lv < 5:
                            b, tm = each(lambda h: U[:, h, :], lambda h: W1[:, h, :])
                            free[b] = vtt(fl(T), fl(T), ps[b][:, :], SUB, tm)
                        free[b2] = tU = vtt(fl(U), fl(U), ps[b2][:, :], SUB, tm2, Q.now("p"))
                    ktv = v4(KT[:, t, 512 * gq:512 * gq + 512])
                    vtv = v4(VT[:, t, 512 * gq:512 * gq + 512])
                    hb = lambda a: bc(a[:, t, h0:h0 + 4], 128, 2)
                    vtt(VB, vtv, hb(BE), MUL, Q.now("p"))
                    vtt(KBG, ktv, hb(BG), MUL)
                    x = vtt(KEND, ktv, hb(EGE), MUL)
                    b, tm = each(lambda h: U[:, h, :], lambda h: VB[:, h, :], x)
                    free[b] = copy("v", fl(WV), ps[b][:, :], tm)
                    b, tm = each(lambda h: KBG[:, h, :], lambda h: U[:, h, :])
                    free[b] = tw_ = copy("v", fl(KCT), ps[b][:, :], tm)
                    for c in range(2):
                        r = slice(64 * c, 64 * c + 64)
                        first = t == 0 and c == 0
                        if not first:
                            b = bank()
                            for h in range(4):
                                tm = mmi(ps[b][r, 128 * h:128 * h + 128], KCT[:, h, r], S[:, h, :], True, True, tw_, ts, free[b])
                            free[b] = tw_ = vtt(fl(WV)[r, :], fl(WV)[r, :], ps[b][r, :], SUB, tm)
                        b = bank()
                        for h in range(4):
                            o = ps[b][r, 128 * h:128 * h + 128]
                            if not first:
                                mm(o, QG[:, h, r], S[:, h, :], True, False, free[b])
                            tm = mmi(o, ATT[:, h, r], WV[:, h, :], first, True, tw_, free[b])
                        free[b] = copy("v", O[r, t, 512 * gq:512 * gq + 512], ps[b][r, :], tm)
                        if t == 0 or c == 0:
                            b = bank()
                            for h in range(4):
                                tm = mmi(ps[b][:, 128 * h:128 * h + 128], KEND[r, h, :], WV[r, h, :], True, True, tw_, free[b])
                            if first:
                                ts = copy("v", fl(S), ps[b][:, :], tm)
                            else:
                                for h in range(4):
                                    ts = stt(S[:, h, :], S[:, h, :], EGR[:, h, 64 * c + 63:64 * c + 64],
                                             ps[b][:, 128 * h:128 * h + 128], MUL, ADD, tm)
                            free[b] = ts
            fence("each")
            OT = QC
            readout(O, 8, GATE, "odn", OT, 0, range(2))
            top[0] = 2048
            project_out(WO, OT, range(2))
            return

        def moe(l):
            OVW = carve(2, 64)
            base = top[0]
            TRI, IOTA = carve(128), carve(64)
            tc = load(TRI, A["cst"][:, 128:256])
            tc = load(IOTA, A["cst"][:, 256:320])
            XG = carve(2, 8, 512)
            SEL = carve(2, 2, 512)
            SEW = carve(2, 2, 512)
            YB = carve(2, 1024)
            SGT = carve(2, 256)
            HID = carve(2, 256)
            TT = carve(2, 512)
            SG, HI = carve(512), carve(512)
            SC, SL, MS, GT, EQ, CU, RK = (carve(2, 64) for _ in range(7))
            M8 = carve(2, 64)
            GS, GM, G8 = carve(2, 8), carve(2, 8), carve(2, 8)
            sv = cstat(16)
            cscale = carve(8)
            vts(cscale, M()[:, 32:40, 0], 1.0, None, ADD, None)
            cshift = M()[:, 24:32, 0]
            fl = lambda a: a.rearrange("p a b -> p (a b)")
            h2 = lambda k: HT[:, k, 0:256]
            i, wt, tw = wtile(A["moe_router_w_2"][l], 8, 64)
            lin_tok(wt, tw, 0, 64, ht_tok, 8, range(2), lambda t, p, tok: act(SC[:, t, :], p, ACT.Exp, tok, scale=-1.0),
                    banks=(0, 1))
            release(i)
            tsc = Q.now("a")

            def choose(mask, v, k, v8, gt, eq, cu, s):
                op("v", lambda g: g.max(v8, v))
                thr = v8[:, k - 1:k]
                vts(gt, v, thr, None, ALU.is_gt, None)
                vts(eq, v, thr, None, ALU.is_equal, None)
                red(s[:, 0:1], gt, ADD)
                vts(s[:, 1:2], s[:, 0:1], -1.0, float(k), MUL, ADD)
                op("v", lambda g: g.tensor_tensor_scan(cu, ones[:, 0:v.shape[1]], eq, 0.0, MUL, ADD))
                stt(eq, cu, s[:, 1:2], eq, ALU.is_le, MUL)
                return vtt(mask, gt, eq, ADD)

            def shared():
                half = lambda i: (lambda sl: sl[:, 2048 * i:2048 * i + 2048].rearrange("p (k n) -> p k n", n=256))
                i, slot, tw = weights((half(0), A["sh_w_gate_2"][l].rearrange("(k p) n -> p k n", p=128)),
                                      (half(1), A["sh_w_up_2"][l].rearrange("(k p) n -> p k n", p=128)))
                tok = []
                for g in range(2):
                    wt = half(g)(slot)
                    for m in range(2):
                        for k in range(8):
                            f = mmi if k == 7 else mm
                            tm = f(ps[2 + g][:, 256 * m:256 * m + 256], wt[:, k, 128 * m:128 * m + 128], h2(k),
                                   k == 0, k == 7, tw, free[2 + g])
                    tok.append(tm)
                release(i)
                return tok

            def shared_down(tok):
                a = act(SG, ps[2][:, :], ACT.Silu, tok[0])
                free[2] = a
                t = free[3] = vtt(HI, SG, ps[3][:, :], MUL, a, tok[1])
                i, slot, tw = weights((lambda sl: sl[:, 0:2048].rearrange("p (k n) -> p k n", n=1024),
                                       A["sh_w_down_2"][l].rearrange("(k p) n -> p k n", p=128)))
                wt = slot.rearrange("p (k n) -> p k n", n=1024)
                hv = HI.rearrange("p (f t) -> p f t", t=256)
                for tt_ in range(2):
                    for h in range(2):
                        for f in range(2):
                            quiet("p", lambda e, o=ps[4 + 2 * tt_ + h][:, :], a=hv[:, f, 128 * tt_:128 * tt_ + 128],
                                  b=wt[:, f, 512 * h:512 * h + 512], s=f == 0:
                                  e.matmul(o, a, b, start=s, stop=False, skip_group_check=True), tw, t)
                op("p", lambda e: e.matmul(ps[0][0:32, 0:32], ident[0:32, 0:32], ident[0:32, 0:32], start=True, stop=True),
                   free[0])
                release(i)

            tok = shared()
            t_ = vts(fl(SC), fl(SC), 1.0, None, ADD, None, tsc)
            t_ = recip(fl(SC), fl(SC), t_)
            vtt(SL, SC, bc(row("rb", 64, 64 * l), 2, 1), ADD, t_)
            shared_down(tok)
            for t in range(2):
                m8 = M8[:, t, :].rearrange("p (g k) -> p g k", k=8)
                for g in range(8):
                    op("v", lambda e, t=t, g=g, m8=m8: e.max(m8[:, g, :], SL[:, t, 8 * g:8 * g + 8]))
                vtt(GS[:, t, :], m8[:, :, 0], m8[:, :, 1], ADD)
                choose(GM[:, t, :], GS[:, t, :], 4, G8[:, t, :], GT[:, t, 0:8], EQ[:, t, 0:8], CU[:, t, 0:8], sv[:, 0:2])
                e8 = lambda a: a[:, t, :].rearrange("p (g k) -> p g k", k=8)
                vtt(e8(MS), e8(SL), bc(GM[:, t, :], 8, 2), MUL)
                vts(GS[:, t, :], GM[:, t, :], -1.0, 1e30, ADD, MUL)
                vtt(e8(MS), e8(MS), bc(GS[:, t, :], 8, 2), ADD)
                tm_ = choose(SL[:, t, :], MS[:, t, :], 6, G8[:, t, :], GT[:, t, :], EQ[:, t, :], CU[:, t, :], sv[:, 0:2])
                vtt(MS[:, t, :], SL[:, t, :], SC[:, t, :], MUL)
                red(sv[:, 2:3], MS[:, t, :], ADD)
                vts(sv[:, 2:3], sv[:, 2:3], 1e-20, None, ADD, None)
                recip(sv[:, 3:4], sv[:, 2:3])
                tq = vts(MS[:, t, :], MS[:, t, :], sv[:, 3:4], 2.5, MUL, MUL)
            a = mmi(ps[1][:, 0:64], TRI, SL[:, 0, :], True, True, tm_, tc, free[1])
            mm(ps[1][:, 64:128], TRI, SL[:, 1, :], True, False)
            a = mmi(ps[1][:, 64:128], ones[:, :], SL[:, 0, :], False, True)
            a = stt(fl(RK), ps[1][:, 0:128], 1.0, fl(SL), ADD, MUL, a)
            free[1] = a
            a = vts(fl(RK), fl(RK), -1.0, None, ADD, None, a)
            a = vts(fl(GT), fl(RK), float(CAP), None, ALU.is_ge, None, a)
            b_ = vtt(fl(OVW), fl(GT), fl(MS), MUL, a, tq)
            a = mmi(ps[1][:, 0:64], ones[:, :], GT[:, 0, :], True, False, b_, free[1])
            a = mmi(ps[1][:, 0:64], ones[:, :], GT[:, 1, :], False, True)
            b_ = red(sv[:, 4:5], ps[1][:, 0:64], ADD, a)
            vcopy(flag[:, 73 * l:73 * l + 64], ps[1][:, 0:64])
            free[1] = red(GS[:, 0, :], ps[1][:, 0:64].rearrange("p (g k) -> p g k", k=8), ADD)
            vcopy(flag[:, 73 * l + 64:73 * l + 72], GS[:, 0, :])
            tflag = vcopy(flag[:, 73 * l + 72:73 * l + 73], sv[:, 4:5])

            bfree = [None, None]
            sel_t = {}
            gat = {}

            def select(q):
                r = q % 2
                for t in range(2):
                    sv_ = SEL[:, r, t, :].rearrange("p (e c) -> p e c", c=64)
                    a = vtt(sv_, bc(IOTA, 8, 1), bc(RK[:, t, 8 * q:8 * q + 8], 64, 2), ALU.is_equal, bfree[r])
                    wv = SEW[:, r, t, :].rearrange("p (e c) -> p e c", c=64)
                    a = vtt(wv, sv_, bc(MS[:, t, 8 * q:8 * q + 8], 64, 2), MUL, a, bfree[r], e="g")
                sel_t[q] = [a, Q.now("v")]

            def gather(q, k):
                r = q % 2
                b = bank((0, 1, 2, 3))
                mm(ps[b][:, :], X[:, 0, 128 * k:128 * k + 128], SEL[:, r, 0, :], True, False, free[b], sel_t[q])
                a = mmi(ps[b][:, :], X[:, 1, 128 * k:128 * k + 128], SEL[:, r, 1, :], False, True)
                free[b] = act(XG[:, r, k, :], ps[b][:, :], ACT.Identity, a, bfree[r], scale=cscale[:, k:k + 1],
                              bias=cshift[:, k:k + 1])
                gat[q] = free[b]

            hid, hfree, tts, ttfree, ys, yfree, downs = {}, [None] * 2, {}, [None] * 2, {}, [None] * 2, {}

            def up(j):
                q, r = j // 4, j % 2
                half = lambda i: (lambda sl: sl.rearrange("p (k n) -> p k n", n=512)[:, :, 256 * i:256 * i + 256])
                got = []
                for s in range(2):
                    n = 2 * j + s
                    got.append(weights((half(0), A["moe_w_gate_2"][l, n].rearrange("(k p) n -> p k n", p=128)),
                                       (half(1), A["moe_w_up_2"][l, n].rearrange("(k p) n -> p k n", p=128))))
                b = bank((0, 1, 2, 3))
                for k in range(8):
                    for s in range(2):
                        i, slot, tw = got[s]
                        x0 = 128 * (j % 4) + 64 * s
                        f = mmi if k == 7 else mm
                        tm = f(ps[b][64 * s:64 * s + 64, :], XG[:, q % 2, k, x0:x0 + 64],
                               slot.rearrange("p (k n) -> p k n", n=512)[:, k, :], k == 0, k == 7, tw, free[b], gat[q])
                release(got[0][0])
                release(got[1][0])
                if j % 4 == 3:
                    bfree_gather[q % 2] = tm
                a = act(SGT[:, r, :], ps[b][:, 0:256], ACT.Silu, tm, hid.get(j - 2))
                free[b] = hid[j] = vtt(HID[:, r, :], SGT[:, r, :], ps[b][:, 256:512], MUL, a, hfree[r])

            bfree_gather = [None, None]

            def turn(j):
                q, r = j // 4, j % 2
                b = bank((0, 1, 2, 3))
                for f in range(2):
                    tr(ps[b][:, 128 * f:128 * f + 128], HID[:, r, 128 * f:128 * f + 128], hid[j], free[b], ttfree[r])
                for t in range(2):
                    x0 = 128 * (j % 4)
                    tm = tr(ps[b][:, 256 + 128 * t:384 + 128 * t], SEW[:, q % 2, t, x0:x0 + 128])
                hfree[r] = tm
                if j % 4 == 3:
                    bfree[q % 2] = [tm, bfree_gather[q % 2]]
                free[b] = tts[j] = copy("a", TT[:, r, :], ps[b][:, :], tm, ttfree[r])

            def down(j):
                r = j % 2
                i, slot, tw = weights((lambda sl: sl.rearrange("p (k n) -> p k n", n=1024),
                                       A["moe_w_down_2"][l, 2 * j:2 * j + 2].rearrange("e (k p) n -> p (e k) n", p=128)))
                wt = slot.rearrange("p (k n) -> p k n", n=1024)
                for h in range(2):
                    b = bank((0, 1, 2, 3))
                    for f in range(2):
                        for s in range(2):
                            fn = mmi if f == 1 else mm
                            tm = fn(ps[b][64 * s:64 * s + 64, :], TT[:, r, 128 * f + 64 * s:128 * f + 64 * s + 64],
                                    wt[:, 2 * s + f, 512 * h:512 * h + 512], f == 0, f == 1, tw, tts[j], free[b])
                    free[b] = copy("v", YB[:, r, 512 * h:512 * h + 512], ps[b][:, :], tm, yfree[r])
                ys[j] = free[b]
                release(i)

            def scatter(j):
                r = j % 2
                for t in range(2):
                    for h in range(2):
                        tm = op("p", lambda e, o=ps[4 + 2 * t + h][:, :], a=TT[:, r, 256 + 128 * t:384 + 128 * t],
                                b=YB[:, r, 512 * h:512 * h + 512]:
                                e.matmul(o, a, b, start=False, stop=j == 31, skip_group_check=True), ys[j])
                yfree[r] = ttfree[r] = tm

            select(0)
            for k in range(8):
                gather(0, k)
            for j in range(32 + 3):
                q = j // 4
                if j < 32:
                    up(j)
                    if j % 4 == 1 and q < 7:
                        select(q + 1)
                if 2 <= j < 34:
                    down(j - 2)
                if j >= 3:
                    scatter(j - 3)
                if 1 <= j < 33:
                    turn(j - 1)
                if j < 32 and q < 7:
                    for k in ((), (0, 1), (2, 3, 4), (5, 6, 7))[j % 4]:
                        gather(q + 1, k)
            fence("moe")
            top[0] = base
            general(l, OVW, tflag)
            top[0] = 0
            Y = Yh[0] = carve(4, 1024)
            for t in range(2):
                for h in range(2):
                    copy("va"[h], Y[:, t, 512 * h:512 * h + 512], ps[4 + 2 * t + h][:, :])
            fence("moe")

        def general(l, OVW, tflag):
            SG, HI = carve(512), carve(512)
            WB, CW = carve(2, 128), carve(256)
            outer = Q.now("p")
            saved = Q.enter_if(flag[0:1, 73 * l + 72:73 * l + 73], tflag, f"g{l}")
            saved_jobs, saved_rel = jobs[0], dict(released)
            Q.wait_outer("s", saved, outer)
            jobs[0] = 0
            released.clear()
            h2 = lambda k: HT[:, k, 0:256]
            half = lambda i: (lambda sl: sl[:, 2048 * i:2048 * i + 2048].rearrange("p (k n) -> p k n", n=256))

            def expert(n):
                i, slot, tw = weights((half(0), A["moe_w_gate_2"][l, n].rearrange("(k p) n -> p k n", p=128)),
                                      (half(1), A["moe_w_up_2"][l, n].rearrange("(k p) n -> p k n", p=128)))
                i2, slot2, tw2 = weights((lambda sl: sl[:, 0:2048].rearrange("p (k n) -> p k n", n=1024),
                                          A["moe_w_down_2"][l, n].rearrange("(k p) n -> p k n", p=128)))
                tv = vcopy(WB, bc(OVW[:, :, n], 128, 2))
                for t in range(2):
                    tm = mmi(ps[2][:, 128 * t:128 * t + 128], WB[:, t, :], ident[:, :], True, True, tv)
                vcopy(CW, ps[2][:, 0:256], tm)
                tok = []
                for g in range(2):
                    wt = half(g)(slot)
                    for m in range(2):
                        for k in range(8):
                            f = mmi if k == 7 else mm
                            tm = f(ps[g][:, 256 * m:256 * m + 256], wt[:, k, 128 * m:128 * m + 128], h2(k),
                                   k == 0, k == 7, tw)
                    tok.append(tm)
                release(i)
                a = act(SG, ps[0][:, :], ACT.Silu, tok[0])
                t = vtt(SG, SG, ps[1][:, :], MUL, a, tok[1])
                hv = HI.rearrange("p (f t) -> p f t", t=256)
                t = vtt(hv, SG.rearrange("p (f t) -> p f t", t=256), bc(CW, 2, 1), MUL, t)
                wt = slot2[:, 0:2048].rearrange("p (k n) -> p k n", n=1024)
                for tt_ in range(2):
                    for h in range(2):
                        for f in range(2):
                            op("p", lambda e, o=ps[4 + 2 * tt_ + h][:, :], a=hv[:, f, 128 * tt_:128 * tt_ + 128],
                               b=wt[:, f, 512 * h:512 * h + 512]:
                               e.matmul(o, a, b, start=False, stop=True, skip_group_check=True), tw2, t)
                release(i2)

            def all_done():
                toks = [Q.now(e) for e in "pvag"] + [Q.now("small")]
                for e in "pvags":
                    Q.wait(e, toks)

            for n in range(NEXP):
                if n % 8 == 0:
                    group = Q.enter_branch()
                inner = Q.enter_branch()
                jobs[0] = 0
                released.clear()
                for i in range(8):
                    free[i] = None
                expert(n)
                all_done()
                Q.leave_branch(inner, flag[0:1, 73 * l + n:73 * l + n + 1])
                if n % 8 == 7:
                    Q.leave_branch(group, flag[0:1, 73 * l + 64 + n // 8:73 * l + 65 + n // 8])
            Q.leave_if(saved)
            jobs[0] = saved_jobs
            released.clear()
            released.update(saved_rel)
            for i in range(8):
                free[i] = None

        def second_layer(l):
            top[0] = 0
            cur[0] = 2 + l
            for half in range(2):
                top[0] = 0
                cs_ = cstat(8)
                t = vts(cs_, M()[:, 24 * half + 8:24 * half + 16, 0], 1.0, None, ADD, None)
                Q.wait("a", [t])
                transposed(range(2), False, lambda t: cs_, lambda t: M()[:, 24 * half:24 * half + 8, 0])
                top[0] = 0
                if half == 0:
                    (moba_gla if l == 0 else deltanet)()
                    residual_ln(2, "lmg", "lmb", l)
                else:
                    moe(l)
                    residual_ln(5, "lfg", "lfb", l)

        for l in range(2):
            top[0] = 0
            cur[0] = l
            if l == 0:
                fill["left"] = [(0, j) for j in range(12)]
                fill_rest(0)
                fence("mod")
                fill["left"] = [(m, j) for m in (1, 2, 3) for j in range(12)]
            tiles = range(4) if l == 0 else range(2)
            for half in range(2):
                top[0] = 0
                tl = range(4) if half == 0 else tiles
                cs_ = cstat(16)
                for w in range(2):
                    scaled(cs_[:, 8 * w:8 * w + 8], 3 * half + 1, w, ("npm", "npf")[half], l)
                Q.wait("v", [Q.now("v")])
                Q.wait("a", [Q.now("v")])
                transposed(tl, True, lambda t: cs_[:, 8 * (t // 2):8 * (t // 2) + 8],
                           lambda t: M()[:, 24 * half:24 * half + 8, t // 2])
                top[0] = 0
                if half == 0:
                    (even_mixer if l == 0 else odd_mixer)()
                    residual_rms(2, "nqm", l, tiles)
                else:
                    conv_ffn(l, tiles)
                    residual_rms(5, "nqf", l, tiles)
            if STAGE == l + 1:
                break

        if STAGE == 0:
            for l in range(2):
                second_layer(l)

        t = Q.dma("s", "outs", out.rearrange("a (t p) d -> p (a t) d", p=128), X[:, 0:2, :], Q.now("v"), Q.now("a"))
        Q.wait("s", [t])

        block = ctx.enter_context(nc.Block())

        @block.tensor
        def _(e):
            for f in Q.q["p"]:
                f(e)

        @block.vector
        def _(e):
            for f in Q.q["v"]:
                f(e)

        @block.scalar
        def _(e):
            for f in Q.q["a"]:
                f(e)

        @block.gpsimd
        def _(e):
            for f in Q.q["g"]:
                f(e)

        @block.sync
        def _(e):
            for f in Q.q["s"]:
                f(e)


STAGE = 0
MARKS = []


def shape_constants():
    i = np.arange(128)
    c = {"cst": np.concatenate([np.eye(128), i[:, None] < i[None, :], np.broadcast_to(np.arange(64), (128, 64)),
                                i[:, None] % 32 == np.arange(4)[None, :]], 1)
         .astype(np.float32)}
    t = np.arange(256)
    inv = (np.float32(10000.0) ** (-np.arange(16, dtype=np.float32) / np.float32(16))).astype(np.float32)
    ang = np.concatenate([(t // 64).astype(np.float32)[:, None] * inv, (t % 64).astype(np.float32)[:, None] * inv], 1)
    c["rope"] = np.concatenate([np.cos(ang), np.sin(ang)], 1).astype(np.float32)
    h = np.zeros((2, 128, 17, 128), np.float32)
    i = np.arange(128)
    s, p = i[:, None], i[None, :]
    for lv in range(7):
        m = 64 >> lv
        blk, right = p // (2 * m), (p // m) % 2
        mid = blk * 2 * m + m
        h[0, :, lv] = np.where(right == 1, (s >= mid) & (s <= p), (s > p) & (s < mid))
        sb_, tb_ = s // (2 * m), p // (2 * m)
        h[0, :, 9 + lv] = (sb_ == tb_) & ((s // m) % 2 == 0) & ((p // m) % 2 == 1)
    h[0, :, 7] = s <= p
    h[0, :, 8] = s > p
    h[0, :, 16] = s == p
    h[1] = h[0][::-1, :, ::-1]
    c["hgc"] = h.reshape(2, 128, 17 * 128)
    return c


def more_constants(c):
    i = np.arange(128)
    s, p = i[:, None], i[None, :]
    g = np.zeros((128, 14, 128), np.float32)
    same = (s // 64) == (p // 64)
    g[:, 0] = same & (s <= p)
    g[:, 1] = same & (s > p)
    for lv in range(6):
        m = 1 << lv
        low = (s // (2 * m) == p // (2 * m)) & ((s // m) % 2 == 1) & ((p // m) % 2 == 0)
        g[:, 2 + lv] = low
        g[:, 8 + lv] = low.T
    c["gdc"] = g.reshape(128, 14 * 128)


def bucket_of(d):
    d = np.maximum(d, 0)
    logd = np.log(np.maximum(d, 1).astype(np.float32) / np.float32(16)).astype(np.float32)
    large = 16 + (logd / np.float32(np.log(2048 / 16)) * np.float32(16)).astype(np.int32)
    return np.where(d < 16, d, np.minimum(large, 31))


def more_arrays(A, I):
    more_constants(A)
    t = np.arange(256)
    dist = t[:, None] - t[None, :]
    own = dist >= 0
    b2 = np.full((4, 256, 256), -1e30, np.float32)
    b2[:, own] = I["rpe_bias_2"].T[:, bucket_of(dist)[own]]
    A["bias2"] = b2
    for name in ("ada_w_2", "ev_w_in_2", "ev_gk_w2_2", "ev_w_out_2", "od_w_in_2", "od_w_out_2", "moe_router_w_2",
                 "moe_w_gate_2", "moe_w_up_2", "moe_w_down_2", "sh_w_gate_2", "sh_w_up_2", "sh_w_down_2"):
        A[name] = I[name]


def kernel(**inputs):
    import concourse.bacc as _bacc
    from concourse.bass_utils import run_bass_kernel_spmd as _run

    I = {k: np.asarray(v) for k, v in inputs.items()}
    A = shape_constants()

    def cols(a):
        a = np.asarray(a, np.float32).reshape(-1, 128)
        return a.T

    A["colp"] = np.ascontiguousarray(np.concatenate([
        cols(I["c"]), cols(I["c_ctx"]), cols(I["c_2"]), cols(I["norm_pre_mix"]), cols(I["norm_post_mix"]),
        cols(I["norm_pre_ffn"]), cols(I["norm_post_ffn"]), cols(I["b_mod"]), cols(I["ada_b_2"]),
        cols(I["ln_mix_g_2"]), cols(I["ln_mix_b_2"]), cols(I["ln_ffn_g_2"]), cols(I["ln_ffn_b_2"]),
        cols(I["ffn_conv_w"]), cols(I["ffn_conv_b"]), cols(I["od_conv_w_2"])], 1))
    A["rowp"] = np.concatenate([I[k].reshape(1, -1) for k in (
        "even_q_norm", "even_k_norm", "hgrn_out_norm", "ev_gk_b_2", "ev_norm_2", "od_norm_2",
        "od_a_log_2", "od_dt_bias_2", "moe_router_b_2")], 1)
    t = np.arange(256)
    r, cc = t // 64, t % 64
    dy = r[None, :] - r[:, None] + 7
    dx = cc[None, :] - cc[:, None] + 15
    c0 = np.clip(cc - 8, 0, 48)[:, None]
    inside = (cc[None, :] >= c0) & (cc[None, :] < c0 + 16)
    b1 = np.full((16, 256, 256), -1e30, np.float32)
    b1[:, inside] = I["odd_rpb"][0][:, dy[inside], dx[inside]]
    A["bias1"] = b1
    for name in ("x", "ctx", "w_mod", "even_w_in", "even_w_out", "odd_w_qkv", "odd_w_out", "ffn_w_up", "ffn_w_down"):
        A[name] = I[name]
    if STAGE == 0:
        more_arrays(A, I)

    nc = _bacc.Bacc("TRN2", target_bir_lowering=False, num_devices=1)
    arrays, aps = {}, {}
    for name, a in A.items():
        a = np.ascontiguousarray(a)
        arrays[f"in_{name}"] = a
        aps[name] = nc.dram_tensor(f"in_{name}", a.shape, mybir.dt.from_np(a.dtype), kind="ExternalInput").ap()
    o = nc.dram_tensor("out_0", [1, 256, 1024], F32, kind="ExternalOutput").ap()
    program(nc, aps, o)
    r = _run(nc, [arrays], core_ids=[0])
    return r.results[0]["out_0"]
```

```python
from contextlib import ExitStack

import numpy as np
import concourse.bass as bass
from concourse import mybir

F32 = mybir.dt.float32
ALU = mybir.AluOpType
ACT = mybir.ActivationFunctionType
AX = mybir.AxisListType.X
MUL, ADD, SUB, MAX, MIN = ALU.mult, ALU.add, ALU.subtract, ALU.max, ALU.min

RING = 5
SLOT = 4096
ARENA = 21000
CAP = 64
EPS = 1e-6
ALPHA = float(4 ** 0.25)
NEXP = 64

COLS = {}
_n = 0
for _name, _w in (("c", 8), ("c_ctx", 8), ("c_2", 8), ("npm", 16), ("nqm", 16), ("npf", 16), ("nqf", 16),
                  ("bmod", 96), ("adab", 96), ("lmg", 16), ("lmb", 16), ("lfg", 16), ("lfb", 16),
                  ("cw", 2 * 3 * 44), ("cb", 2 * 44), ("ocw", 4 * 24)):
    COLS[_name] = _n
    _n += _w
NCOL = _n
ROWS = {}
_n = 0
for _name, _w in (("qn", 64), ("kn", 64), ("on", 128), ("gkb", 256), ("evn", 128), ("odn", 128),
                  ("alog", 8), ("dtb", 8), ("rb", 128)):
    ROWS[_name] = _n
    _n += _w
NROW = _n


class Queues:

    def __init__(self, nc, ctx):
        self.nc, self.ctx = nc, ctx
        self.q = {e: [] for e in "pvags"}
        self.sem = {e: ctx.enter_context(nc.semaphore("done_" + e)) for e in "pvag"}
        self.n = {e: 0 for e in "pvag"}
        self.seen = {e: {} for e in "pvags"}
        self.chained = "vag"
        self.strand = None
        self.last = {}

    def new_sem(self, name):
        self.sem[name] = self.ctx.enter_context(self.nc.semaphore(name))
        self.n[name] = 0
        return name

    def wait(self, e, toks):
        for t in toks:
            if t is None:
                continue
            if isinstance(t, list):
                self.wait(e, t)
                continue
            s, v = t
            if v == 0:
                continue
            if self.seen[e].get(s, 0) >= v:
                continue
            self.seen[e][s] = v
            self.q[e].append(lambda eng, s=self.sem[s], v=v: eng.wait_ge(s, v))

    def op(self, e, f, *w):
        self.wait(e, w)
        if e in self.chained:
            self.wait(e, [(e, self.n[e]) if self.strand is None else self.last[self.strand]])
        self.n[e] += 1
        self.q[e].append(lambda eng, s=self.sem[e]: f(eng).then_inc(s, 1))
        if e != "p" and self.strand is not None:
            self.last[self.strand] = (e, self.n[e])
        return (e, self.n[e])

    def together(self, gens):
        gens = dict(enumerate(gens))
        self.last = {i: [self.now(e) for e in "vag"] for i in gens}
        while gens:
            for i in list(gens):
                self.strand = i
                if next(gens[i], "end") == "end":
                    del gens[i]
        self.strand = None

    def loose(self, on):
        self.chained = "" if on else "vag"
        if on:
            for e in "vag":
                self.wait(e, [self.now(e)])

    def quiet(self, e, f, *w):
        self.wait(e, w)
        self.q[e].append(lambda eng: f(eng))

    def dma(self, e, sem, out, in_, *w):
        self.wait(e, w)
        self.n[sem] += 16
        self.q[e].append(lambda eng, s=self.sem[sem]: eng.dma_start(out, in_).then_inc(s, 16))
        return (sem, self.n[sem])

    def now(self, e):
        return (e, self.n[e])

    def enter_if(self, flag, tok, name):
        self.wait("s", [tok])
        saved = (self.q, self.sem, self.n, self.seen)
        self.q = {e: [] for e in "pvags"}
        self.sem = {k: self.ctx.enter_context(self.nc.semaphore(f"{name}_{k}")) for k in self.sem}
        self.n = {k: 0 for k in self.sem}
        self.seen = {e: {} for e in "pvags"}
        self.flag = flag
        return saved

    def wait_outer(self, e, saved, tok):
        s, v = saved[1][tok[0]], tok[1]
        self.q[e].append(lambda eng: eng.wait_ge(s, v))

    def leave_if(self, saved):
        body, flag = self.q, self.flag
        self.q, self.sem, self.n, self.seen = saved

        def run(eng, inner):
            v = eng.value_load(flag, min_val=0, max_val=1 << 20)
            with eng.If(v > 0):
                for f in inner:
                    f(eng)

        for e in "pvags":
            self.q[e].append(lambda eng, inner=body[e]: run(eng, inner))

    def enter_branch(self):
        saved = (self.q, dict(self.n), {e: dict(x) for e, x in self.seen.items()})
        self.q = {e: [] for e in "pvags"}
        return saved

    def leave_branch(self, saved, flag):
        body = self.q
        self.q, before, self.seen = saved
        more = {e: [] for e in "pvags"}
        for k, v in self.n.items():
            if v > before[k]:
                more[k if k in "pvag" else "s"].append((self.sem[k], v - before[k]))

        def run(eng, inner, adds):
            v = eng.value_load(flag, min_val=0, max_val=1 << 20)
            with eng.If(v > 0):
                for f in inner:
                    f(eng)
            with eng.Else():
                for s, n in adds:
                    eng.sem_inc(s, n)

        for e in "pvags":
            self.q[e].append(lambda eng, inner=body[e], adds=more[e]: run(eng, inner, adds))


def program(nc, A, out):
    with ExitStack() as ctx:
        Q = Queues(nc, ctx)
        op, quiet = Q.op, Q.quiet

        def sb(name, shape):
            return ctx.enter_context(nc.sbuf_tensor(name, shape, F32))

        ring = sb("ring", [128, RING, SLOT])
        X = sb("X", [128, 4, 1024])
        HT = sb("HT", [128, 8, 512])
        arena = sb("arena", [128, ARENA])
        ident = sb("ident", [128, 128])
        ones = sb("ones", [128, 128])
        colp = sb("colp", [128, NCOL])
        rowp = sb("rowp", [128, NROW])
        mods = sb("mods", [128, 4, 96])
        RF = sb("RF", [128, 512])
        sel4 = sb("sel4", [128, 4])
        flag = ctx.enter_context(nc.sbuf_tensor("flag", [128, 146], mybir.dt.int32))
        csil = sb("csil", [128, 8, 32])
        st = sb("st", [128, 256])
        ps = [ctx.enter_context(nc.psum_tensor(f"ps{i}", [128, 512], F32)) for i in range(8)]
        free = [None] * 8
        bank_at = [0]

        for i in range(RING):
            Q.new_sem(f"w{i}")
        for i in range(4):
            Q.new_sem(f"b{i}")
        Q.new_sem("small")
        Q.new_sem("outs")

        top = [0]

        def carve(*shape):
            n = int(np.prod(shape))
            a = top[0]
            top[0] += n
            assert top[0] <= ARENA, top[0]
            v = arena[:, a:a + n]
            if len(shape) == 2:
                return v.rearrange("p (a b) -> p a b", b=shape[1])
            if len(shape) == 3:
                return v.rearrange("p (a b c) -> p a b c", b=shape[1], c=shape[2])
            return v

        st_top = [0]

        def cstat(n):
            a = st_top[0]
            st_top[0] += n
            assert st_top[0] <= 256
            return st[:, a:a + n]

        small_open = [None]

        def fence():
            toks = [Q.now(e) for e in "pvag"] + [Q.now("small")]
            for e in "pvag":
                Q.wait(e, toks)
            st_top[0] = 0
            for i in range(8):
                free[i] = None

        def load(dst, src, *w):
            return Q.dma("g", "small", dst, src, *w)

        jobs = [0]
        released = {}

        def weights(*parts):
            i = jobs[0]
            jobs[0] += 1
            s = i % RING
            if i - RING in released:
                Q.wait("s", [released.pop(i - RING)])
            tok = None
            for dst, src in parts:
                tok = Q.dma("s", f"w{s}", dst(ring[:, s, :]), src)
            return i, ring[:, s, :], tok

        def wtile(src, kc, n):
            i, slot, tok = weights((lambda sl: sl[:, 0:kc * n].rearrange("p (k n) -> p k n", n=n),
                                    src.rearrange("(k p) n -> p k n", p=128)))
            return i, slot[:, 0:kc * n].rearrange("p (k n) -> p k n", n=n), tok

        def release(i):
            released[i] = Q.now("p")

        def bank(banks=range(8)):
            banks = list(banks)
            b = banks[bank_at[0] % len(banks)]
            bank_at[0] += 1
            return b

        def mm(o, l, r, start, stop, *w):
            quiet("p", lambda e: e.matmul(o, l, r, start=start, stop=stop), *w)

        def mmi(o, l, r, start, stop, *w):
            return op("p", lambda e: e.matmul(o, l, r, start=start, stop=stop), *w)

        def tr(o, i, *w):
            k = i.shape[0]
            return op("p", lambda e: e.transpose(o, i, ident[0:k, 0:k]), *w)

        def vtt(o, a, b, f, *w, e="v"):
            return op(e, lambda g: g.tensor_tensor(o, a, b, f), *w)

        def vts(o, a, s1, s2, f1, f2, *w, e="v"):
            if f2 is None:
                return op(e, lambda g: g.tensor_scalar(o, a, s1, None, f1), *w)
            return op(e, lambda g: g.tensor_scalar(o, a, s1, s2, f1, f2), *w)

        def stt(o, a, s, b, f1, f2, *w):
            return op("v", lambda g: g.scalar_tensor_tensor(out=o, in0=a, scalar=s, in1=b, op0=f1, op1=f2), *w)

        def red(o, a, f, *w):
            return op("v", lambda g: g.tensor_reduce(o, a, AX, f), *w)

        def recip(o, a, *w):
            return op("v", lambda g: g.reciprocal(o, a), *w)

        def vcopy(o, a, *w, e="v"):
            return op(e, lambda g: g.tensor_copy(o, a), *w)

        def act(o, a, f, *w, scale=1.0, bias=0.0, accum=None):
            if accum is None:
                return op("a", lambda g: g.activation(o, a, f, scale=scale, bias=bias), *w)
            return op("a", lambda g: g.activation(o, a, f, scale=scale, bias=bias, accum_out=accum), *w)

        def copy(e, o, a, *w):
            if e == "a":
                return act(o, a, ACT.Copy, *w)
            return vcopy(o, a, *w, e=e)

        def bc(ap, n, at):
            shape = list(ap.shape)
            return ap.unsqueeze(at).broadcast_to(shape[:at] + [n] + shape[at:])

        def col(name, i, n):
            return colp[:, COLS[name] + i:COLS[name] + i + n]

        def row(name, n, i=0):
            return rowp[:, ROWS[name] + i:ROWS[name] + i + n]

        def rstd_of(ss, n, scale, eps, *w):
            t = vts(ss, ss, scale, eps, MUL, ADD, *w)
            t = act(ss, ss, ACT.Ln, t)
            return act(ss, ss, ACT.Exp, t, scale=-0.5)

        Q.new_sem("first")
        tF = Q.dma("s", "first", colp[:, :], A["colp"])
        tF = Q.dma("s", "first", sel4[:, :], A["cst"][:, 320:324])
        tI = load(ident[:, :], A["cst"][:, 0:128])
        load(rowp[:, :], A["rowp"][0:1, :].broadcast_to([128, NROW]))
        xv = A["x"].rearrange("a (t p) d -> p (a t) d", p=128)
        cv = A["ctx"].rearrange("a (t p) d -> p (a t) d", p=128)
        load(X[:, 0:2, :], xv)
        tI = load(X[:, 2:4, :], cv)
        op("v", lambda g: g.memset(ones[:, :], 1.0))
        tZ = [tF, op("v", lambda g: g.memset(csil[:, :, :], 0.0))]
        for i, nm in enumerate(("c", "c_ctx", "c_2", "c_2")):
            act(csil[:, :, i], col(nm, 0, 8), ACT.Silu, tZ)
        for e in "pv":
            Q.wait(e, [tF, Q.now("a"), Q.now("v")])

        def mod_of(m):
            return mods[:, m, :].rearrange("p (a b) -> p a b", b=2)

        cur = [0]

        def M():
            return mod_of(cur[0])

        fill = {"left": [], "open": None, "rfree": None}

        def fill_start(m, j, b):
            src = A["w_mod"][m] if m < 2 else A["ada_w_2"][m - 2]
            i, wt, tw = wtile(src[:, 512 * j:512 * j + 512], 8, 512)
            for k in range(8):
                g = k % 4
                f = mmi if k == 7 else mm
                t = f(ps[b][32 * g:32 * g + 32, :], csil[:, k, :], wt[:, k, :], k < 4, k >= 4, tw, free[b])
            release(i)
            t = copy("a", RF[:, :], ps[b][:, :], t, fill["rfree"])
            free[b] = t
            fill["open"] = (m, j, b, t)

        def fill_end():
            m, j, b, t = fill["open"]
            w0 = 0 if m < 2 else 2
            for q in range(4):
                tm = mmi(ps[b][:, 2 * q:2 * q + 2], RF[:, 128 * q:128 * q + 128], sel4[:, w0:w0 + 2], True, True, t, free[b])
            fill["rfree"] = tm
            bias = col(("bmod", "adab")[m // 2], 48 * (m % 2) + 4 * j, 4)
            free[b] = vtt(mod_of(m)[:, 4 * j:4 * j + 4, :], ps[b][:, 0:8].rearrange("p (a b) -> p a b", b=2),
                          bc(bias, 2, 2), ADD, tm)
            fill["open"] = None

        def filler(b):
            if fill["open"]:
                fill_end()
            elif fill["left"]:
                fill_start(*fill["left"].pop(0), b)

        def fill_rest(b):
            while fill["left"] or fill["open"]:
                filler(b)

        def scaled(dst, j, which, wname, l):
            return stt(dst, M()[:, 8 * j:8 * j + 8, which], 1.0, col(wname, 8 * l, 8), ADD, MUL)

        def spread(dst, c, dg, *w):
            t = vtt(dg, bc(ident[:, :], 8, 1), bc(c, 128, 2), MUL, *w)
            for h in range(2):
                b = bank()
                tm = mmi(ps[b][:, :], ones[:, :], dg[:, 4 * h:4 * h + 4, :], True, True, t, free[b])
                t2 = free[b] = copy("va"[h], dst[:, 512 * h:512 * h + 512], ps[b][:, :], tm)
                if h == 0:
                    t0 = t2
            return [t0, t2]

        next_ss = sb("next_ss", [128, 4])
        summed = [False]

        def transposed(tiles, norm, sc, sh):
            tmp = carve(2, 1024)
            sq = carve(2, 1024)
            ss = cstat(4)
            used = [None, None]
            tn, n = {}, len(tiles)
            if norm and summed[0]:
                ss = next_ss
                summed[0] = False
            elif norm:
                Q.loose(True)
                sqt = {}
                for i, t in enumerate(tiles):
                    sqt[i] = act(sq[:, i % 2, :], X[:, t, :], ACT.Square, sqt.get(i - 2), accum=ss[:, t:t + 1])
                Q.loose(False)
            if norm:
                tr_ = rstd_of(ss[:, tiles[0]:tiles[-1] + 1], n, 1.0 / 1024, EPS, Q.now("a"))
            Q.loose(True)

            def scale_(i):
                if norm and i < n:
                    t = tiles[i]
                    tn[i] = vts(tmp[:, i % 2, :], X[:, t, :], ss[:, t:t + 1], None, MUL, None, tr_, used[i % 2])

            scale_(0)
            for i, t in enumerate(tiles):
                if i == 0:
                    scale_(1)
                src = tmp[:, i % 2, :] if norm else X[:, t, :]
                bs, tts_ = [], []
                for h in range(2):
                    b = bank()
                    for c in range(4):
                        k = 4 * h + c
                        tt_ = tr(ps[b][:, 128 * c:128 * c + 128], src[:, 128 * k:128 * k + 128], tn.get(i), free[b])
                    bs.append(b)
                    tts_.append(tt_)
                used[i % 2] = tt_
                for h in range(2):
                    b, tt_ = bs[h], tts_[h]
                    for c in range(4):
                        k = 4 * h + c
                        o, a = HT[:, k, 128 * t:128 * t + 128], ps[b][:, 128 * c:128 * c + 128]
                        if h == 0:
                            z = vts(o, a, sc(t)[:, k:k + 1], sh(t)[:, k:k + 1], MUL, ADD, tt_)
                        else:
                            z = act(o, a, ACT.Identity, tt_, scale=sc(t)[:, k:k + 1], bias=sh(t)[:, k:k + 1])
                    free[b] = z
                scale_(i + 2)
            Q.loose(False)
            fence()

        def lin_tok(wt, tw, c0, n, lhs, kc, tiles, evac, banks=range(8)):
            for t in tiles:
                b = bank(banks)
                for k in range(kc):
                    f = mmi if k == kc - 1 else mm
                    tm = f(ps[b][:, 0:n], lhs(k, t), wt[:, k, c0:c0 + n], k == 0, k == kc - 1, tw, free[b])
                free[b] = evac(t, ps[b][:, 0:n], tm)

        def lin_col(wt, tw, c0, m, rhs, kc, ntok, evac, banks=range(8)):
            b = bank(banks)
            for k in range(kc):
                f = mmi if k == kc - 1 else mm
                tm = f(ps[b][0:m, 0:ntok], wt[:, k, c0:c0 + m], rhs(k), k == 0, k == kc - 1, tw, free[b])
            free[b] = evac(ps[b][0:m, 0:ntok], tm)

        ht_tok = lambda k, t: HT[:, k, 128 * t:128 * t + 128]
        flip = [0]

        def ev(dst):
            def f(t, p, tok):
                flip[0] ^= 1
                return copy("va"[flip[0]], dst(t), p, tok)
            return f

        def evc(dst):
            def f(p, tok):
                flip[0] ^= 1
                return copy("va"[flip[0]], dst, p, tok)
            return f

        def attention(items, scale, nbuf=4):
            P = carve(nbuf, 512)
            PT = carve(2, 4 * 256)
            mx, nm, sm, ri = (cstat(nbuf) for _ in range(4))
            pfree = [None] * nbuf
            ptfree = [None, None]
            S = {}
            seq = [(i, qt) for i in range(len(items)) for qt in range(2)]

            def first(n):
                i, qt = seq[n]
                it = items[i]
                r = n % nbuf
                b = bank((0, 1))
                nk = it["nk"]
                o = ps[b][:, 0:nk]
                t = mmi(o, it["q"](qt), it["k"], True, True, free[b])
                src = o
                tb = []
                if it["bias"] is not None:
                    bv, btok, lo, hi = it["bias"](qt)
                    t = stt(P[:, r, lo:hi], o[:, lo:hi], scale, bv, MUL, ADD, t, btok, pfree[r])
                    if hi < nk:
                        t2 = vts(P[:, r, hi:nk], o[:, hi:nk], scale, None, MUL, None)
                        t = [t, t2]
                    free[b] = t[1] if isinstance(t, list) else t
                    it["bias_done"](t)
                    src = P[:, r, 0:nk]
                t = red(mx[:, r:r + 1], src, MAX, t, pfree[r])
                sc = 1.0 if it["bias"] is not None else scale
                t = vts(nm[:, r:r + 1], mx[:, r:r + 1], -sc, None, MUL, None, t)
                t = act(P[:, r, 0:nk], src, ACT.Exp, t, pfree[r], scale=sc, bias=nm[:, r:r + 1], accum=sm[:, r:r + 1])
                if it["bias"] is None:
                    free[b] = t
                S[n] = t

            def second(n):
                i, qt = seq[n]
                it = items[i]
                r = n % nbuf
                nk = it["nk"]
                t = recip(ri[:, r:r + 1], sm[:, r:r + 1], S[n])
                t = vts(P[:, r, 0:nk], P[:, r, 0:nk], ri[:, r:r + 1], None, MUL, None, t)
                b = bank((2, 3, 4))
                for kt in range(nk // 128):
                    tt_ = tr(ps[b][:, 128 * kt:128 * kt + 128], P[:, r, 128 * kt:128 * kt + 128], t, free[b])
                pfree[r] = tt_
                ptv = PT[:, i % 2, 0:nk * 2].rearrange("p (k q c) -> p k q c", q=2, c=128)
                t = copy("a", ptv[:, :, qt, :], ps[b][:, 0:nk].rearrange("p (k c) -> p k c", c=128), tt_, ptfree[i % 2])
                free[b] = t
                if qt == 1:
                    S["pt", i] = t

            def third(i):
                it = items[i]
                nkt = it["nk"] // 128
                nd, base = it["nd"], it["base"]
                ptv = PT[:, i % 2, 0:nkt * 256].rearrange("p (k q) -> p k q", q=256)
                b = bank((6, 7))
                o = ps[b][base:base + nd, 0:256]
                for kt in range(nkt):
                    f = mmi if kt == nkt - 1 else mm
                    t = f(o, it["v"](kt), ptv[:, kt, :], kt == 0, kt == nkt - 1, S["pt", i], free[b])
                ptfree[i % 2] = t
                free[b] = copy("v", it["out"], o, t)

            N = len(seq)
            Q.loose(True)
            for n in range(N + 4):
                if n < N:
                    first(n)
                filler(5)
                if 2 <= n < N + 2:
                    second(n - 2)
                if n >= 4 and (n - 4) % 2 == 1:
                    third((n - 4) // 2)
            Q.loose(False)

        def heads_steps(src, nh, hd, scale, eps, tmp, ss, *w):
            yield act(tmp, src, ACT.Square, *w)
            yield red(ss, tmp.rearrange("p (h d) -> p h d", d=hd), ADD)
            yield vts(ss, ss, scale, eps, MUL, ADD)
            yield act(ss, ss, ACT.Ln)
            yield act(ss, ss, ACT.Exp, scale=-0.5)

        def even_mixer():
            W, WO = A["even_w_in"][0], A["even_w_out"][0]
            G_ = carve(4, 512)
            V = carve(4, 512)
            Z = [carve(4, 512), carve(4, 512)]
            QB = carve(4, 512)
            keep = top[0]
            AA = carve(4, 768)
            hcol = lambda k: HT[:, k, :]
            i, wt, tw = wtile(W[:, 0:512], 8, 512)
            lin_tok(wt, tw, 0, 512, ht_tok, 8, range(4), lambda t, p, tok: copy(
                "va"[t % 2], AA[:, t, 0:512].rearrange("p (h w d) -> p w h d", w=2, d=64),
                p.rearrange("p (w h d) -> p w h d", w=2, d=64), tok))
            release(i)
            i, wt, tw = wtile(W[:, 512:768], 8, 256)
            lin_tok(wt, tw, 0, 256, ht_tok, 8, range(4), ev(lambda t: AA[:, t, 512:768]))
            release(i)
            i, wt, tw = wtile(W[:, 768:1280], 8, 512)
            for h in range(4):
                def e(p, tok, h=h):
                    t = act(QB[:, h, :], p, ACT.Silu, tok)
                    vts(QB[:, h, :], QB[:, h, :], 128 ** -0.5, None, MUL, None, t)
                    return t
                lin_col(wt, tw, 128 * h, 128, hcol, 8, 512, e)
            release(i)
            for dst, c in ((Z[0], 1280), (Z[1], 1792), (V, 2304), (G_, 2816)):
                i, wt, tw = wtile(W[:, c:c + 512], 8, 512)
                if dst is G_:
                    lin_tok(wt, tw, 0, 512, ht_tok, 8, range(4), lambda t, p, tok: act(G_[:, t, :], p, ACT.Silu, tok))
                else:
                    lin_tok(wt, tw, 0, 512, ht_tok, 8, range(4), ev(lambda t, dst=dst: dst[:, t, :]))
                release(i)
            fence()
            OT = HT
            QT = carve(4, 512)
            KT = carve(512)
            work = top[0]
            SQ = carve(4, 640)
            ROT = carve(4, 320)
            cs = carve(2, 64)
            ss = cstat(40)
            tcs = load(cs, A["rope"].rearrange("(t p) c -> p t c", p=128))

            def rotary(t):
                sst = ss[:, 10 * t:10 * t + 10]
                yield from heads_steps(AA[:, t, 0:640], 10, 64, 1.0 / 64, EPS, SQ[:, t, :], sst)
                hv = AA[:, t, 0:640].rearrange("p (h d) -> p h d", d=64)
                yield vtt(hv, hv, bc(sst, 64, 2), MUL)
                yield vtt(hv[:, 0:8, :], hv[:, 0:8, :], bc(row("qn", 64), 8, 1), MUL)
                yield vtt(hv[:, 8:10, :], hv[:, 8:10, :], bc(row("kn", 64), 2, 1), MUL)
                if t < 2:
                    x1, x2 = hv[:, :, 0:32], hv[:, :, 32:64]
                    c_, s_ = bc(cs[:, t, 0:32], 10, 1), bc(cs[:, t, 32:64], 10, 1)
                    r0, r1 = (ROT[:, 2 * t + j, :].rearrange("p (h d) -> p h d", d=32) for j in range(2))
                    yield vtt(r0, x1, s_, MUL, tcs)
                    yield vtt(r1, x2, s_, MUL)
                    yield vtt(x1, x1, c_, MUL)
                    yield vtt(x1, x1, r1, SUB)
                    yield vtt(x2, x2, c_, MUL)
                    yield vtt(x2, x2, r0, ADD)

            Q.together([rotary(t) for t in range(4)])
            for t in range(4):
                b = bank()
                for h in range(4):
                    t_ = tr(ps[b][:, 128 * h:128 * h + 128], AA[:, t, 128 * h:128 * h + 128], Q.now("v"), free[b])
                free[b] = copy("v", QT[:, :, 128 * t:128 * t + 128], ps[b][:, :].rearrange("p (h c) -> p h c", c=128), t_)
                b = bank()
                t_ = tr(ps[b][:, 0:128], AA[:, t, 512:640], free[b])
                free[b] = copy("a", KT[:, 128 * t:128 * t + 128], ps[b][:, 0:128], t_)
            fence()
            top[0] = work
            items = []
            for h in range(8):
                kv, pr = h // 4, h % 4
                B0 = 64 * kv
                for grp in range(2):
                    k0 = 0 if grp == 0 else 256
                    t0 = 2 * grp
                    items.append(dict(
                        q=lambda qt, B0=B0, pr=pr, t0=t0: QT[B0:B0 + 64, pr, 128 * (t0 + qt):128 * (t0 + qt) + 128],
                        k=KT[B0:B0 + 64, k0:512], nk=512 - k0, bias=None,
                        v=lambda kt, k0=k0, kv=kv: AA[:, k0 // 128 + kt, 640 + 64 * kv:704 + 64 * kv],
                        nd=64, base=64 * (h % 2),
                        out=OT[64 * (h % 2):64 * (h % 2) + 64, h // 2, 256 * grp:256 * grp + 256]))
            attention(items, 0.125)
            fence()
            top[0] = keep
            GG = carve(4, 512)
            KTT = carve(4, 512)
            O = carve(4, 512)
            CM = carve(9, 128)
            CK = carve(8, 128)
            E = HT[:, 4:8, :].rearrange("p (h j) (l c) -> p h (j l) c", h=2, c=128)
            QF = carve(2, 128)
            S = carve(512)
            KL = carve(512)
            DL = carve(2)
            AT = carve(2, 128)
            for d in range(2):
                z = Z[d]
                fl = lambda a: a.rearrange("p a b -> p (a b)")
                tc = load(CM, A["hgc"][d, :, 0:1152].rearrange("p (a b) -> p a b", b=128))
                tc = load(CK, A["hgc"][d, :, 1152:2176].rearrange("p (a b) -> p a b", b=128))
                t = act(fl(GG), fl(z), ACT.Abs)
                t = act(fl(GG), fl(GG), ACT.Exp, t, scale=-1.0)
                t = act(fl(GG), fl(GG), ACT.Ln, t, bias=1.0)
                t = stt(fl(GG), fl(z), 0.0, fl(GG), MIN, SUB, t)
                t = vtt(fl(z), fl(GG), fl(z), SUB, t)
                t = act(fl(z), fl(z), ACT.Exp, t)
                for c in range(4):
                    b = bank()
                    for h in range(4):
                        t_ = tr(ps[b][:, 128 * h:128 * h + 128], z[:, c, 128 * h:128 * h + 128], t, free[b])
                    free[b] = copy("a", KTT[:, :, 128 * c:128 * c + 128],
                                   ps[b][:, :].rearrange("p (h c) -> p h c", c=128), t_)
                tkt = Q.now("a")
                qtwo, ktwo, last = (1, 0, 127) if d == 0 else (0, 1, 0)
                order = (2, 3, 0, 1) if d == 0 else (3, 2, 1, 0)
                units = [(n, order[n], h) for n in range(4) for h in range(4)]
                te, tx, tat, tqf = {}, {}, {}, {}
                spent, read = [None, None], [None, None]
                st_ = {"kl": None, "klr": None, "s": None}

                def decays(u):
                    n, c, h = units[u]
                    for j in range(2):
                        b = 2 + j
                        t = mmi(ps[b][:, :], GG[:, c, 128 * h:128 * h + 128], CM[:, 4 * j:4 * j + 4, :], True, True, tc,
                                Q.now("v") if u == 0 else None, free[b])
                        te[u] = free[b] = act(E[:, u % 2, 4 * j:4 * j + 4, :],
                                              ps[b][:, :].rearrange("p (a b) -> p a b", b=128), ACT.Exp, t, spent[u % 2])

                def factors(u):
                    n, c, h = units[u]
                    r = u % 2
                    qv, kv = QB[:, h, 128 * c:128 * c + 128], KTT[:, h, 128 * c:128 * c + 128]
                    vcopy(DL[:, r:r + 1], E[:, r, 7, last:last + 1], te[u])
                    tqf[u] = vtt(QF[:, r, :], E[:, r, 7, :], qv, MUL, te[u], tkt, read[r])
                    for lv in range(7):
                        m = 64 >> lv
                        w3 = lambda a: a.rearrange("p (b w m) -> p b w m", w=2, m=m)
                        e3 = w3(E[:, r, lv, :])
                        vtt(e3[:, :, qtwo, :], e3[:, :, qtwo, :], w3(qv)[:, :, qtwo, :], MUL)
                        tx[u] = vtt(e3[:, :, ktwo, :], e3[:, :, ktwo, :], w3(kv)[:, :, ktwo, :], MUL)

                def scores(u):
                    n, c, h = units[u]
                    r = u % 2
                    qv, kv = QB[:, h, 128 * c:128 * c + 128], KTT[:, h, 128 * c:128 * c + 128]
                    for j in range(2):
                        b = 4 + j
                        for a in range(4):
                            lv = 4 * j + a
                            l_, r_ = (E[:, r, lv, :], E[:, r, lv, :]) if lv < 7 else (kv, qv)
                            t = mmi(ps[b][:, 128 * a:128 * a + 128], l_, r_, True, True, tx[u], free[b])
                        t = free[b] = vtt(E[:, r, 4 * j:4 * j + 4, :], ps[b][:, :].rearrange("p (a b) -> p a b", b=128),
                                          CK[:, 4 * j:4 * j + 4, :], MUL, t)
                    tat[u] = spent[r] = red(AT[:, r, :], E[:, r, :, :].rearrange("p l t -> p t l"), ADD, t, read[r])

                def outputs(u):
                    n, c, h = units[u]
                    r = u % 2
                    bo = 6 + n % 2
                    if h == 0 and n < 3:
                        t = mmi(ps[0][:, :], CM[:, 8, :], GG[:, c, :], True, True, tc, free[0])
                        t = free[0] = act(KL, ps[0][:, :], ACT.Exp, t, st_["klr"])
                        st_["kl"] = vtt(KL, KL, z[:, c, :], MUL, t)
                    oo = ps[bo][:, 128 * h:128 * h + 128]
                    vv = V[:, c, 128 * h:128 * h + 128]
                    sl = S[:, 128 * h:128 * h + 128]
                    if n == 0:
                        t1 = mmi(oo, AT[:, r, :], vv, True, True, tat[u], free[bo])
                    else:
                        mm(oo, AT[:, r, :], vv, True, False, tat[u], free[bo])
                        t1 = mmi(oo, QF[:, r, :], sl, False, True, tqf[u], st_["s"])
                    read[r] = t1
                    if n < 3:
                        t = mmi(ps[0][:, 0:128], KL[:, 128 * h:128 * h + 128], vv, True, True, st_["kl"], free[0])
                        st_["klr"] = t
                        if n == 0:
                            free[0] = copy("v", sl, ps[0][:, 0:128], t, t1)
                        else:
                            free[0] = stt(sl, sl, DL[:, r:r + 1], ps[0][:, 0:128], MUL, ADD, t, t1)
                        st_["s"] = free[0]
                    if h == 3:
                        if d == 0:
                            free[bo] = copy("v", O[:, c, :], ps[bo][:, :], t1)
                        else:
                            free[bo] = vtt(O[:, c, :], O[:, c, :], ps[bo][:, :], ADD, t1)

                Q.loose(True)
                decays(0)
                for u in range(16):
                    if u < 15:
                        decays(u + 1)
                    factors(u)
                    filler(1)
                    if u >= 1:
                        outputs(u - 1)
                    filler(1)
                    scores(u)
                outputs(15)
                Q.loose(False)
                fence()
            fill_rest(1)
            fence()
            ss = cstat(16)
            SQ = GG

            def normed(t):
                sst = ss[:, 4 * t:4 * t + 4]
                yield from heads_steps(O[:, t, :], 4, 128, 1.0 / 128, EPS, SQ[:, t, :], sst)
                ov = O[:, t, :].rearrange("p (h d) -> p h d", d=128)
                yield vtt(ov, ov, bc(sst, 128, 2), MUL)
                yield vtt(ov, ov, bc(row("on", 128), 4, 1), MUL)
                tq = vtt(O[:, t, :], O[:, t, :], G_[:, t, :], MUL)
                yield tq
                b = bank()
                for h in range(4):
                    t_ = tr(ps[b][:, 128 * h:128 * h + 128], O[:, t, 128 * h:128 * h + 128], tq, free[b])
                free[b] = copy("a", OT[:, 4:8, 128 * t:128 * t + 128], ps[b][:, :].rearrange("p (h c) -> p h c", c=128), t_)
                yield free[b]

            Q.together([normed(t) for t in range(4)])
            fence()
            top[0] = 0
            project_out(WO, OT, range(4))

        Yh = [None]

        def project_out(WO, OT, tiles):
            Y = Yh[0] = carve(4, 1024)
            for h in range(2):
                i, wt, tw = wtile(WO[:, 512 * h:512 * h + 512], 8, 512)
                lin_tok(wt, tw, 0, 512, lambda k, t: OT[:, k, 128 * t:128 * t + 128], 8, tiles,
                        ev(lambda t: Y[:, t, 512 * h:512 * h + 512]))
                release(i)
            fence()

        def residual_rms(j, wname, l, tiles):
            Y = Yh[0]
            R = carve(2, 1024)
            DG = carve(8, 128)
            SQ = carve(1024)
            cc = cstat(16)
            ss = cstat(4)
            tg = []
            for w in range(2 if len(tiles) == 4 else 1):
                t = vtt(cc[:, 8 * w:8 * w + 8], M()[:, 8 * j:8 * j + 8, w], col(wname, 8 * l, 8), MUL)
                tg += spread(R[:, w, :], cc[:, 8 * w:8 * w + 8], DG, t, Q.now("p"))
            for t in tiles:
                act(SQ, Y[:, t, :], ACT.Square, Q.now("a"), accum=ss[:, t:t + 1])
            tq = rstd_of(ss[:, 0:len(tiles)], len(tiles), 1.0 / 1024, EPS, Q.now("a"))
            Q.loose(True)
            for t in tiles:
                stt(Y[:, t, :], Y[:, t, :], ss[:, t:t + 1], R[:, t // 2, :], MUL, MUL, tq, tg)
            a = Q.now("v")
            summed[0] = l == 0 or j == 2
            for t in tiles:
                z = vtt(X[:, t, :], X[:, t, :], Y[:, t, :], ADD, a)
                if summed[0]:
                    act(Y[:, t, :], X[:, t, :], ACT.Square, z, accum=next_ss[:, t:t + 1])
            Q.loose(False)
            fence()

        def conv_ffn(l, tiles):
            NT = 128 * len(tiles)
            ns = len(tiles) // 2
            WU, WD = A["ffn_w_up"][l], A["ffn_w_down"][l]
            HID = carve(22, NT)
            CB = carve(4, NT)
            cbf = [None] * 4
            for j in range(11):
                c = 256 * j
                i, slot, tw = weights(
                    (lambda sl: sl.rearrange("p (k n) -> p k n", n=512)[:, :, 0:256],
                     WU[:, c:c + 256].rearrange("(k p) n -> p k n", p=128)),
                    (lambda sl: sl.rearrange("p (k n) -> p k n", n=512)[:, :, 256:512],
                     WU[:, 2816 + c:2816 + c + 256].rearrange("(k p) n -> p k n", p=128)))
                wt = slot.rearrange("p (k n) -> p k n", n=512)
                for s in range(2):
                    m = 2 * j + s
                    done = []
                    for g in range(2):
                        ch = 22 * g + m
                        r = 2 * (m % 2) + g

                        def e(p, tok, ch=ch, r=r):
                            w0, w1, w2 = (col("cw", (3 * l + k) * 44 + ch, 1) for k in range(3))
                            cb = CB[:, r, :]
                            t = act(cb, p, ACT.Identity, tok, cbf[r], scale=w1, bias=col("cb", 44 * l + ch, 1))
                            cv = cb.rearrange("p (s t) -> p s t", s=ns)
                            pv = p.rearrange("p (s t) -> p s t", s=ns)
                            t = stt(cv[:, :, 1:256], pv[:, :, 0:255], w0, cv[:, :, 1:256], MUL, ADD, t)
                            t = stt(cv[:, :, 0:255], pv[:, :, 1:256], w2, cv[:, :, 0:255], MUL, ADD, t)
                            done.append(t)
                            return t
                        lin_col(wt, tw, 256 * g + 128 * s, 128, lambda k: HT[:, k, 0:NT], 8, NT, e)
                    ra, rg = 2 * (m % 2), 2 * (m % 2) + 1
                    t = act(CB[:, rg, :], CB[:, rg, :], ACT.Silu, done[1])
                    t = vtt(HID[:, m, :], CB[:, rg, :], CB[:, ra, :], MUL, t, done[0], e="g")
                    cbf[ra] = cbf[rg] = t
                release(i)
            fence()
            top[0] = 22 * NT
            Y = Yh[0] = carve(4, 1024)
            for h in range(2):
                bs = [4 * h + t for t in tiles]
                for q in range(3):
                    kc = (8, 8, 6)[q]
                    i, wt, tw = wtile(WD[1024 * q:1024 * q + 128 * kc, 512 * h:512 * h + 512], kc, 512)
                    for t in tiles:
                        for k in range(kc):
                            f = mmi if k == kc - 1 else mm
                            tm = f(ps[bs[t]][:, :], HID[:, 8 * q + k, 128 * t:128 * t + 128], wt[:, k, :],
                                   q == 0 and k == 0, q == 2 and k == kc - 1, tw)
                        if q == 2:
                            copy("va"[t % 2], Y[:, t, 512 * h:512 * h + 512], ps[bs[t]][:, :], tm)
                    release(i)
            fence()
            if len(tiles) == 4:
                top[0] = 0

        def odd_mixer():
            W, WO = A["odd_w_qkv"][0], A["odd_w_out"][0]
            QT = carve(8, 256)
            KT = carve(8, 512)
            V = carve(4, 1024)
            BI = carve(4, 512)
            for j in range(2):
                i, wt, tw = wtile(W[:, 512 * j:512 * j + 512], 8, 512)
                for m in range(4):
                    lin_col(wt, tw, 128 * m, 128, lambda k: HT[:, k, 0:256], 8, 256, evc(QT[:, 4 * j + m, :]))
                release(i)
            for j in range(2):
                i, wt, tw = wtile(W[:, 1024 + 512 * j:1536 + 512 * j], 8, 512)
                for m in range(4):
                    lin_col(wt, tw, 128 * m, 128, lambda k: HT[:, k, :], 8, 512, evc(KT[:, 4 * j + m, :]))
                release(i)
            for j in range(2):
                i, wt, tw = wtile(W[:, 2048 + 512 * j:2560 + 512 * j], 8, 512)
                lin_tok(wt, tw, 0, 512, ht_tok, 8, range(4), ev(lambda t, j=j: V[:, t, 512 * j:512 * j + 512]))
                release(i)
            fence()
            OT = HT
            attention(biased(BI, A["bias1"], 16, lambda h, qt: QT[64 * (h % 2):64 * (h % 2) + 64, h // 2, 128 * qt:128 * qt + 128],
                             lambda h: KT[64 * (h % 2):64 * (h % 2) + 64, h // 2, :], 512,
                             lambda h, kt: V[:, kt, 64 * h:64 * h + 64], 64,
                             lambda h: 64 * (h % 2), lambda h: OT[64 * (h % 2):64 * (h % 2) + 64, h // 2, 0:256]), 0.125)
            fence()
            top[0] = 0
            project_out(WO, OT, range(2))

        def biased(BI, src, nh, q, k, nk, v, nd, base, outf):
            gone = {}
            got = {}

            def fetch(h):
                got[h] = Q.dma("g", f"b{h % 4}", BI[:, h % 4, :].rearrange("p (q k) -> p q k", k=256),
                              src[h].rearrange("(q p) k -> p q k", p=128), gone.get(h - 4))

            for h in range(min(4, nh)):
                fetch(h)

            def bias(h, qt):
                if qt == 0 and 1 <= h and h + 3 < nh and h >= 1 and (h + 3) not in got:
                    fetch(h + 3)
                return BI[:, h % 4, 256 * qt:256 * qt + 256], got[h], 0, 256

            items = []
            for h in range(nh):
                items.append(dict(q=lambda qt, h=h: q(h, qt), k=k(h), nk=nk, bias=lambda qt, h=h: bias(h, qt),
                                  bias_done=lambda t, h=h: gone.__setitem__(h, t),
                                  v=lambda kt, h=h: v(h, kt), nd=nd, base=base(h), out=outf(h)))
            return items

        def residual_ln(j, gname, bname, l):
            Y = Yh[0]
            R = carve(3, 1024)
            DG = carve(3, 8, 128)
            sm, ss = cstat(4), cstat(4)
            t1 = spread(R[:, 0, :], M()[:, 8 * j:8 * j + 8, 0], DG[:, 0])
            t2 = spread(R[:, 1, :], col(gname, 8 * l, 8), DG[:, 1])
            t3 = spread(R[:, 2, :], col(bname, 8 * l, 8), DG[:, 2])

            def tile(t):
                Y_, X_ = Y[:, t, :], X[:, t, :]
                yield vtt(Y_, Y_, R[:, 0, :], MUL, t1)
                yield stt(X_, X_, ALPHA, Y_, MUL, ADD)
                yield act(Y_, X_, ACT.Identity, accum=sm[:, t:t + 1])
                yield vts(sm[:, 2 + t:3 + t], sm[:, t:t + 1], 1.0 / 1024, None, MUL, None)
                yield vts(X_, X_, sm[:, 2 + t:3 + t], None, SUB, None)
                yield act(Y_, X_, ACT.Square, accum=ss[:, t:t + 1])
                yield vts(ss[:, t:t + 1], ss[:, t:t + 1], 1.0 / 1024, 1e-5, MUL, ADD)
                yield act(ss[:, t:t + 1], ss[:, t:t + 1], ACT.Ln)
                yield act(ss[:, t:t + 1], ss[:, t:t + 1], ACT.Exp, scale=-0.5)
                yield stt(X_, X_, ss[:, t:t + 1], R[:, 1, :], MUL, MUL, t2)
                yield vtt(X_, X_, R[:, 2, :], ADD, t3)

            Q.together([tile(0), tile(1)])
            fence()

        def moba_gla():
            W, WO = A["ev_w_in_2"][0], A["ev_w_out_2"][0]
            QM, KM = carve(4, 256), carve(4, 256)
            VM, GV, GG = carve(2, 512), carve(2, 512), carve(2, 512)
            GQ, GKD, GK = carve(2, 256), carve(2, 256), carve(2, 256)
            LR = carve(256)
            W2 = carve(256)
            GD = carve(2, 128)
            G = carve(2, 256)
            tw2 = load(W2[0:16, :], A["ev_gk_w2_2"][0])
            tgd = load(GD, A["gdc"][:, 0:256].rearrange("p (a b) -> p a b", b=128))
            h2 = lambda k: HT[:, k, 0:256]
            for dst, c in ((QM, 0), (KM, 512)):
                i, wt, tw = wtile(W[:, c:c + 512], 8, 512)
                for m in range(4):
                    lin_col(wt, tw, 128 * m, 128, h2, 8, 256, evc(dst[:, m, :]))
                release(i)
            i, wt, tw = wtile(W[:, 1024:1536], 8, 512)
            lin_tok(wt, tw, 0, 512, ht_tok, 8, range(2), ev(lambda t: VM[:, t, :]))
            release(i)
            i, wt, tw = wtile(W[:, 1536:2048], 8, 512)
            for m in range(4):
                lin_col(wt, tw, 128 * m, 128, h2, 8, 256, evc((GQ, GKD)[m // 2][:, m % 2, :]))
            lin_tok(wt, tw, 256, 256, ht_tok, 8, range(2), ev(lambda t: GK[:, t, :]))
            release(i)
            i, wt, tw = wtile(W[:, 2048:2560], 8, 512)
            lin_tok(wt, tw, 0, 512, ht_tok, 8, range(2), ev(lambda t: GV[:, t, :]))
            release(i)
            i, wt, tw = wtile(W[:, 2560:3072], 8, 512)
            lin_tok(wt, tw, 0, 512, ht_tok, 8, range(2), lambda t, p, tok: act(GG[:, t, :], p, ACT.Silu, tok))
            release(i)
            i, wt, tw = wtile(W[:, 3072:3088], 8, 16)
            lin_col(wt, tw, 0, 16, h2, 8, 256, lambda p, tok: vcopy(LR[0:16, :], p, tok))
            release(i)
            fence()
            OT = HT
            for t in range(2):
                b = bank()
                tm = mmi(ps[b][:, 0:256], LR[0:16, 128 * t:128 * t + 128], W2[0:16, :], True, True, tw2)
                vtt(G[:, t, :], ps[b][:, 0:256], row("gkb", 256), ADD, tm)
            L_ = carve(2, 256)
            fl = lambda a: a.rearrange("p a b -> p (a b)")
            t = act(fl(L_), fl(G), ACT.Abs, Q.now("v"))
            t = act(fl(L_), fl(L_), ACT.Exp, t, scale=-1.0)
            t = act(fl(L_), fl(L_), ACT.Ln, t, bias=1.0)
            t = stt(fl(G), fl(G), 0.0, fl(L_), MIN, SUB, t)
            tg = vts(fl(G), fl(G), 1.0 / 16, None, MUL, None, t)
            fence()
            EB, EN, QE, KE = (carve(2, 128) for _ in range(4))
            KEND = carve(256)
            AT = carve(4, 64)
            S = carve(2, 128)
            O = carve(2, 512)
            MIN_, MREV = GD[:, 0, :], GD[:, 1, :]
            for t in range(2):
                for j in range(2):
                    b = bank((0, 1))
                    tm = mmi(ps[b][:, 0:128], G[:, t, 128 * j:128 * j + 128], MIN_, True, True, free[b])
                    act(EB[:, j, :], ps[b][:, 0:128], ACT.Exp, tm, Q.now("v"), Q.now("p"))
                    free[b] = act(EN[:, j, :], ps[b][:, 0:128], ACT.Exp, scale=-1.0)
                te = Q.now("a")
                for j in range(2):
                    stt(QE[:, j, :], GQ[:, j, 128 * t:128 * t + 128], 0.125, EB[:, j, :], MUL, MUL, te, Q.now("p"))
                    tk = vtt(KE[:, j, :], GKD[:, j, 128 * t:128 * t + 128], EN[:, j, :], MUL)
                b = bank((0, 1))
                tm = mmi(ps[b][:, 0:256], MREV, G[:, t, :], True, True, free[b])
                free[b] = a = act(KEND, ps[b][:, 0:256], ACT.Exp, tm)
                tke = vtt(KEND, KEND, GK[:, t, :], MUL, a)
                for c in range(2):
                    r0 = 64 * c
                    rr = slice(r0, r0 + 64)
                    for hh in range(2):
                        for j in range(2):
                            tm = mmi(ps[2 + hh][rr, 64 * j:64 * j + 64], KE[64 * hh:64 * hh + 64, j, rr],
                                     QE[64 * hh:64 * hh + 64, j, rr], True, True, tk, free[2 + hh])
                        free[2 + hh] = ta = vtt(
                            AT[rr, :, :].rearrange("p (j w) t -> p j w t", w=2)[:, :, hh, :],
                            ps[2 + hh][rr, 0:128].rearrange("p (j t) -> p j t", t=64),
                            bc(GD[rr, 0, rr], 2, 1), MUL, tm, Q.now("p"))
                    bo = 4 + c
                    for h in range(4):
                        tm = mmi(ps[bo][rr, 128 * h:128 * h + 128], AT[rr, h, :], GV[rr, t, 128 * h:128 * h + 128],
                                 True, True, ta, free[bo])
                    free[bo] = vcopy(O[rr, t, :], ps[bo][rr, :], tm)
                    first = t == 0 and c == 0
                    if not first:
                        for hh in range(2):
                            for j in range(2):
                                tm = mmi(ps[6 + hh][rr, 128 * j:128 * j + 128], QE[64 * hh:64 * hh + 64, j, rr],
                                         S[64 * hh:64 * hh + 64, j, :], True, True, ts, free[6 + hh])
                            ov = O[rr, t, :].rearrange("p (j w d) -> p j w d", w=2, d=128)[:, :, hh, :]
                            free[6 + hh] = vtt(ov, ov, ps[6 + hh][rr, 0:256].rearrange("p (j d) -> p j d", d=128), ADD, tm)
                    if t == 0 or c == 0:
                        b = bank((0, 1))
                        for h in range(4):
                            hh, j = h % 2, h // 2
                            tm = mmi(ps[b][64 * hh:64 * hh + 64, 128 * j:128 * j + 128], KEND[rr, 64 * h:64 * h + 64],
                                     GV[rr, t, 128 * h:128 * h + 128], True, True, tke, free[b])
                        for j in range(2):
                            if first:
                                ts = vcopy(S[:, j, :], ps[b][:, 128 * j:128 * j + 128], tm)
                            else:
                                ts = stt(S[:, j, :], S[:, j, :], EB[:, j, r0 + 63:r0 + 64],
                                         ps[b][:, 128 * j:128 * j + 128], MUL, ADD, tm)
                        free[b] = ts
            readout(O, 4, GG, "evn", OT, 4, range(2))
            BI = carve(4, 512)
            attention(biased(BI, A["bias2"], 4, lambda h, qt: QM[:, h, 128 * qt:128 * qt + 128], lambda h: KM[:, h, :],
                             256, lambda h, kt: VM[:, kt, 128 * h:128 * h + 128], 128, lambda h: 0,
                             lambda h: OT[:, h, 0:256]), 128 ** -0.5)
            fence()
            top[0] = 0
            project_out(WO, OT, range(2))

        def readout(O, nh, G, wname, OT, c0, tiles):
            ss = cstat(nh * 2)
            SQ = carve(2, nh * 128)

            def tile(t):
                sst = ss[:, nh * t:nh * t + nh]
                yield act(SQ[:, t, :], O[:, t, :], ACT.Square, Q.now("v"))
                yield red(sst, SQ[:, t, :].rearrange("p (h d) -> p h d", d=128), ADD)
                yield vts(sst, sst, 1.0 / 128, EPS, MUL, ADD)
                yield act(sst, sst, ACT.Ln)
                yield act(sst, sst, ACT.Exp, scale=-0.5)
                ov = O[:, t, :].rearrange("p (h d) -> p h d", d=128)
                yield vtt(ov, ov, bc(sst, 128, 2), MUL)
                yield vtt(ov, ov, bc(row(wname, 128), nh, 1), MUL)
                tq = vtt(O[:, t, :], O[:, t, :], G[:, t, :], MUL)
                yield tq
                for q in range(nh // 4):
                    b = bank()
                    for h in range(4):
                        x0 = 512 * q + 128 * h
                        t_ = tr(ps[b][:, 128 * h:128 * h + 128], O[:, t, x0:x0 + 128], tq, free[b])
                    free[b] = copy("a", OT[:, c0 + 4 * q:c0 + 4 * q + 4, 128 * t:128 * t + 128],
                                   ps[b][:, :].rearrange("p (h c) -> p h c", c=128), t_)
                    yield free[b]

            Q.together([tile(t) for t in tiles])
            fence()

        def deltanet():
            W, WO = A["od_w_in_2"][0], A["od_w_out_2"][0]
            QKV = [carve(8, 256) for _ in range(3)]
            QC, KC, VC = QKV
            GATE = carve(2, 1024)
            BA = carve(2, 16)
            GD = carve(14, 128)
            tgd = load(GD, A["gdc"].rearrange("p (a b) -> p a b", b=128))
            h2 = lambda k: HT[:, k, 0:256]
            for j in range(6):
                i, wt, tw = wtile(W[:, 512 * j:512 * j + 512], 8, 512)
                for m in range(4):
                    ch = 4 * j + m

                    def e(p, tok, ch=ch):
                        d = QKV[ch // 8][:, ch % 8, :]
                        w = [col("ocw", 24 * k + ch, 1) for k in range(4)]
                        t = act(d, p, ACT.Identity, tok, scale=w[3])
                        for s in (1, 2, 3):
                            t = stt(d[:, s:256], p[:, 0:256 - s], w[3 - s], d[:, s:256], MUL, ADD, t)
                        act(d, d, ACT.Silu, t)
                        return t
                    lin_col(wt, tw, 128 * m, 128, h2, 8, 256, e)
                release(i)
            for j in range(2):
                i, wt, tw = wtile(W[:, 3072 + 512 * j:3584 + 512 * j], 8, 512)
                lin_tok(wt, tw, 0, 512, ht_tok, 8, range(2),
                        lambda t, p, tok, j=j: act(GATE[:, t, 512 * j:512 * j + 512], p, ACT.Silu, tok))
                release(i)
            i, wt, tw = wtile(W[:, 4096:4112], 8, 16)
            lin_tok(wt, tw, 0, 16, ht_tok, 8, range(2), lambda t, p, tok: vcopy(BA[:, t, :], p, tok))
            release(i)
            fence()
            VT = HT[:, 0:4, :].rearrange("p (t a) b -> p t (a b)", t=2)
            KT = HT[:, 4:8, :].rearrange("p (t a) b -> p t (a b)", t=2)
            O = VT
            fl = lambda a: a.rearrange("p a b -> p (a b)")
            MINC, MREV = GD[:, 0, :], GD[:, 1, :]
            BE, G, T1 = (cstat(16).rearrange("p (t h) -> p t h", h=8) for _ in range(3))
            GC, EGE, EGC, BG = (cstat(16).rearrange("p (t h) -> p t h", h=8) for _ in range(4))
            EA = cstat(8)
            t = act(BE, BA[:, :, 0:8], ACT.Exp, scale=-1.0)
            t = vts(BE, BE, 1.0, None, ADD, None, t)
            t = recip(fl(BE), fl(BE), t)
            t = vtt(G, BA[:, :, 8:16], bc(row("dtb", 8), 2, 1), ADD)
            t = act(T1, G, ACT.Abs, t)
            t = act(T1, T1, ACT.Exp, t, scale=-1.0)
            t = act(T1, T1, ACT.Ln, t, bias=1.0)
            t = stt(fl(G), fl(G), 0.0, fl(T1), MAX, ADD, t)
            t = act(EA, row("alog", 8), ACT.Exp, t)
            t = vtt(G, G, bc(EA, 2, 1), MUL, t)
            t = vts(G, G, -1.0, None, MUL, None, t)
            for tt_ in range(2):
                b = bank()
                tm = mmi(ps[b][:, 0:8], MINC, G[:, tt_, :], True, True, t)
                vcopy(GC[:, tt_, :], ps[b][:, 0:8], tm)
                act(EGC[:, tt_, :], ps[b][:, 0:8], ACT.Exp, Q.now("v"))
                b = bank()
                tm = mmi(ps[b][:, 0:8], MREV, G[:, tt_, :], True, True)
                act(EGE[:, tt_, :], ps[b][:, 0:8], ACT.Exp, tm)
            vtt(BG, BE, EGC, MUL, Q.now("a"))
            before = top[0]

            def unit_length(D, j):
                SQ, RN = carve(512), carve(512)
                dv = fl(D)[:, 512 * j:512 * j + 512]
                t = act(SQ, dv, ACT.Square)
                yield t
                b = bank()
                tm = mmi(ps[b][:, :], ones[:, :], SQ, True, True, t, free[b])
                yield vts(RN, ps[b][:, :], EPS, None, ADD, None, tm)
                yield act(RN, RN, ACT.Ln)
                yield act(RN, RN, ACT.Exp, scale=-0.5)
                yield vtt(dv, dv, RN, MUL)

            for D in (QC, KC):
                Q.together([unit_length(D, j) for j in range(4)])
            top[0] = before
            fence()
            for D, dst in ((KC, KT), (VC, VT)):
                for t in range(2):
                    for q in range(2):
                        b = bank()
                        for h in range(4):
                            tm = tr(ps[b][:, 128 * h:128 * h + 128], D[:, 4 * q + h, 128 * t:128 * t + 128], free[b])
                        free[b] = copy("va"[q], dst[:, t, 512 * q:512 * q + 512], ps[b][:, :], tm)
            fence()
            places = [fl(VC), fl(X[:, 2:4, :])]
            scale = 128 ** -0.5
            b4 = lambda m: bc(m, 4, 1)
            v4 = lambda p: p.rearrange("p (h c) -> p h c", c=128)

            def heads(gq):
                EGR, ET, AA, AAT = (places[gq][:, 512 * i:512 * i + 512].rearrange("p (h c) -> p h c", c=128)
                                    for i in range(4))
                E, T, U, W1, B_, ATT, QG, S = (carve(4, 128) for _ in range(8))
                VB, KBG, KEND, WV, KCT = ET, AA, AAT, T, E
                at = [0]
                h0 = 4 * gq
                tp = None
                ts = None

                def nextb():
                    at[0] += 1
                    return 4 * gq + at[0] % 4

                def each(l_, r_, *w):
                    b = nextb()
                    for h in range(4):
                        tm = mmi(ps[b][:, 128 * h:128 * h + 128], l_(h), r_(h), True, True, free[b], *w)
                    return b, tm

                for t in range(2):
                    tk = slice(128 * t, 128 * t + 128)
                    ts_ = vcopy(B_, bc(G[:, t, h0:h0 + 4], 128, 2), tp)
                    b, tm = each(lambda h: B_[:, h, :], lambda h: MINC, ts_)
                    yield
                    te = act(fl(EGR), ps[b][:, :], ACT.Exp, tm)
                    yield
                    for h in range(4):
                        pv = ps[b][:, 128 * h:128 * h + 128]
                        g1 = GC[:, t, h0 + h:h0 + h + 1]
                        vts(ET[:, h, :], pv, g1, 0.0, SUB, MIN)
                        yield
                        td = vts(E[:, h, :], pv, g1, 0.0, SUB, MAX)
                        yield
                    free[b] = td
                    act(fl(ET), fl(ET), ACT.Exp)
                    yield
                    act(fl(E), fl(E), ACT.Exp, scale=-1.0)
                    b, tm = each(lambda h: KC[:, h0 + h, tk], lambda h: KC[:, h0 + h, tk])
                    b2, tm2 = each(lambda h: KC[:, h0 + h, tk], lambda h: QC[:, h0 + h, tk])
                    yield
                    vtt(E, E, b4(MREV), MUL, e="g")
                    yield
                    for h in range(4):
                        ta = stt(AA[:, h, :], ps[b][:, 128 * h:128 * h + 128], BE[:, t, h0 + h:h0 + h + 1], E[:, h, :],
                                 MUL, MUL, tm)
                        yield
                    free[b] = ta
                    b = nextb()
                    for h in range(4):
                        tm = tr(ps[b][:, 128 * h:128 * h + 128], AA[:, h, :], ta, free[b])
                    vtt(T, AA, b4(GD[:, 2, :]), MUL)
                    yield
                    vtt(T, b4(ident[:, :]), T, SUB)
                    yield
                    free[b] = copy("a", fl(AAT), ps[b][:, :], tm)
                    yield
                    vtt(ET, ET, b4(MINC), MUL, e="g")
                    free[b2] = stt(fl(ATT), ps[b2][:, :], scale, fl(ET), MUL, MUL, tm2)
                    yield
                    stt(QG, QC[:, h0:h0 + 4, tk], scale, EGR, MUL, MUL)
                    yield
                    vtt(U, AAT, b4(GD[:, 8, :]), MUL)
                    yield
                    tU = vtt(U, b4(ident[:, :]), U, SUB)
                    z = vtt(B_, AAT, b4(GD[:, 9, :]), MUL)
                    for lv in range(1, 6):
                        b, tm = each(lambda h: B_[:, h, :], lambda h: T[:, h, :], z, tU)
                        yield
                        free[b] = w1 = copy("a", fl(W1), ps[b][:, :], tm)
                        if lv < 5:
                            b1, tm1 = each(lambda h: U[:, h, :], lambda h: W1[:, h, :], w1)
                        b3, tm3 = each(lambda h: W1[:, h, :], lambda h: U[:, h, :], w1)
                        yield
                        if lv < 5:
                            free[b1] = vtt(fl(T), fl(T), ps[b1][:, :], SUB, tm1)
                            yield
                            z = vtt(B_, AAT, b4(GD[:, 9 + lv, :]), MUL, tm)
                            yield
                        free[b3] = tU = vtt(fl(U), fl(U), ps[b3][:, :], SUB, tm3)
                        yield
                    ktv = v4(KT[:, t, 512 * gq:512 * gq + 512])
                    vtv = v4(VT[:, t, 512 * gq:512 * gq + 512])
                    hb = lambda a: bc(a[:, t, h0:h0 + 4], 128, 2)
                    x = vtt(VB, vtv, hb(BE), MUL)
                    b, tm = each(lambda h: U[:, h, :], lambda h: VB[:, h, :], x)
                    yield
                    x = vtt(KBG, ktv, hb(BG), MUL)
                    b2, tm2 = each(lambda h: KBG[:, h, :], lambda h: U[:, h, :], x)
                    yield
                    vtt(KEND, ktv, hb(EGE), MUL)
                    yield
                    free[b] = copy("v", fl(WV), ps[b][:, :], tm)
                    yield
                    free[b2] = tw_ = copy("v", fl(KCT), ps[b2][:, :], tm2)
                    yield
                    for c in range(2):
                        r = slice(64 * c, 64 * c + 64)
                        first = t == 0 and c == 0
                        if not first:
                            b = nextb()
                            for h in range(4):
                                tm = mmi(ps[b][r, 128 * h:128 * h + 128], KCT[:, h, r], S[:, h, :], True, True, tw_, ts, free[b])
                            yield
                            free[b] = tw_ = vtt(fl(WV)[r, :], fl(WV)[r, :], ps[b][r, :], SUB, tm)
                        b = nextb()
                        for h in range(4):
                            o = ps[b][r, 128 * h:128 * h + 128]
                            if not first:
                                mm(o, QG[:, h, r], S[:, h, :], True, False, free[b])
                            tm = mmi(o, ATT[:, h, r], WV[:, h, :], first, True, tw_, free[b])
                        tp = tm
                        yield
                        if t == 0 or c == 0:
                            b1 = nextb()
                            for h in range(4):
                                tm1 = mmi(ps[b1][:, 128 * h:128 * h + 128], KEND[r, h, :], WV[r, h, :], True, True, tw_, free[b1])
                            tp = tm1
                        free[b] = copy("v", O[r, t, 512 * gq:512 * gq + 512], ps[b][r, :], tm)
                        yield
                        if t == 0 or c == 0:
                            if first:
                                ts = copy("v", fl(S), ps[b1][:, :], tm1)
                                yield
                            else:
                                for h in range(4):
                                    ts = stt(S[:, h, :], S[:, h, :], EGR[:, h, 64 * c + 63:64 * c + 64],
                                             ps[b1][:, 128 * h:128 * h + 128], MUL, ADD, tm1)
                                    yield
                            free[b1] = ts

            Q.together([heads(0), heads(1)])
            fence()
            OT = QC
            readout(O, 8, GATE, "odn", OT, 0, range(2))
            top[0] = 2048
            project_out(WO, OT, range(2))
            return

        def moe(l):
            OVW = carve(2, 64)
            base = top[0]
            TRI, IOTA = carve(128), carve(64)
            tc = load(TRI, A["cst"][:, 128:256])
            tc = load(IOTA, A["cst"][:, 256:320])
            XG = carve(2, 8, 512)
            SEL = carve(2, 2, 512)
            SEW = carve(2, 2, 512)
            YB = carve(2, 1024)
            SGT = carve(2, 256)
            HID = carve(2, 256)
            TT = carve(2, 512)
            SG, HI = carve(512), carve(512)
            SC, SL, MS, GT, EQ, CU, RK = (carve(2, 64) for _ in range(7))
            M8 = carve(2, 64)
            GS, GM, G8 = carve(2, 8), carve(2, 8), carve(2, 8)
            sv = cstat(16)
            cscale = carve(8)
            vts(cscale, M()[:, 32:40, 0], 1.0, None, ADD, None)
            cshift = M()[:, 24:32, 0]
            fl = lambda a: a.rearrange("p a b -> p (a b)")
            h2 = lambda k: HT[:, k, 0:256]
            i, wt, tw = wtile(A["moe_router_w_2"][l], 8, 64)
            lin_tok(wt, tw, 0, 64, ht_tok, 8, range(2), lambda t, p, tok: act(SC[:, t, :], p, ACT.Exp, tok, scale=-1.0),
                    banks=(0, 1))
            release(i)
            tsc = Q.now("a")

            def choose(mask, v, k, v8, gt, eq, cu, s):
                yield op("v", lambda g: g.max(v8, v))
                thr = v8[:, k - 1:k]
                yield vts(gt, v, thr, None, ALU.is_gt, None)
                yield vts(eq, v, thr, None, ALU.is_equal, None)
                yield red(s[:, 0:1], gt, ADD)
                yield vts(s[:, 1:2], s[:, 0:1], -1.0, float(k), MUL, ADD)
                yield op("v", lambda g: g.tensor_tensor_scan(cu, ones[:, 0:v.shape[1]], eq, 0.0, MUL, ADD))
                yield stt(eq, cu, s[:, 1:2], eq, ALU.is_le, MUL)
                yield vtt(mask, gt, eq, ADD)

            def shared():
                half = lambda i: (lambda sl: sl[:, 2048 * i:2048 * i + 2048].rearrange("p (k n) -> p k n", n=256))
                i, slot, tw = weights((half(0), A["sh_w_gate_2"][l].rearrange("(k p) n -> p k n", p=128)),
                                      (half(1), A["sh_w_up_2"][l].rearrange("(k p) n -> p k n", p=128)))
                tok = []
                for g in range(2):
                    wt = half(g)(slot)
                    for m in range(2):
                        for k in range(8):
                            f = mmi if k == 7 else mm
                            tm = f(ps[2 + g][:, 256 * m:256 * m + 256], wt[:, k, 128 * m:128 * m + 128], h2(k),
                                   k == 0, k == 7, tw, free[2 + g])
                    tok.append(tm)
                release(i)
                return tok

            def shared_down(tok):
                a = act(SG, ps[2][:, :], ACT.Silu, tok[0])
                free[2] = a
                t = free[3] = vtt(HI, SG, ps[3][:, :], MUL, a, tok[1])
                i, slot, tw = weights((lambda sl: sl[:, 0:2048].rearrange("p (k n) -> p k n", n=1024),
                                       A["sh_w_down_2"][l].rearrange("(k p) n -> p k n", p=128)))
                wt = slot.rearrange("p (k n) -> p k n", n=1024)
                hv = HI.rearrange("p (f t) -> p f t", t=256)
                for tt_ in range(2):
                    for h in range(2):
                        for f in range(2):
                            quiet("p", lambda e, o=ps[4 + 2 * tt_ + h][:, :], a=hv[:, f, 128 * tt_:128 * tt_ + 128],
                                  b=wt[:, f, 512 * h:512 * h + 512], s=f == 0:
                                  e.matmul(o, a, b, start=s, stop=False, skip_group_check=True), tw, t)
                op("p", lambda e: e.matmul(ps[0][0:32, 0:32], ident[0:32, 0:32], ident[0:32, 0:32], start=True, stop=True),
                   free[0])
                release(i)

            tok = shared()
            t_ = vts(fl(SC), fl(SC), 1.0, None, ADD, None, tsc)
            t_ = recip(fl(SC), fl(SC), t_)
            vtt(SL, SC, bc(row("rb", 64, 64 * l), 2, 1), ADD, t_)
            shared_down(tok)

            def routed(t):
                m8 = M8[:, t, :].rearrange("p (g k) -> p g k", k=8)
                s_ = sv[:, 8 * t:8 * t + 4]
                e8 = lambda a: a[:, t, :].rearrange("p (g k) -> p g k", k=8)
                for g in range(8):
                    yield op("v", lambda e, g=g: e.max(m8[:, g, :], SL[:, t, 8 * g:8 * g + 8]))
                yield vtt(GS[:, t, :], m8[:, :, 0], m8[:, :, 1], ADD)
                yield from choose(GM[:, t, :], GS[:, t, :], 4, G8[:, t, :], GT[:, t, 0:8], EQ[:, t, 0:8], CU[:, t, 0:8], s_)
                yield vtt(e8(MS), e8(SL), bc(GM[:, t, :], 8, 2), MUL)
                yield vts(GS[:, t, :], GM[:, t, :], -1.0, 1e30, ADD, MUL)
                yield vtt(e8(MS), e8(MS), bc(GS[:, t, :], 8, 2), ADD)
                yield from choose(SL[:, t, :], MS[:, t, :], 6, G8[:, t, :], GT[:, t, :], EQ[:, t, :], CU[:, t, :], s_)
                yield vtt(MS[:, t, :], SL[:, t, :], SC[:, t, :], MUL)
                yield red(s_[:, 2:3], MS[:, t, :], ADD)
                yield vts(s_[:, 2:3], s_[:, 2:3], 1e-20, None, ADD, None)
                yield recip(s_[:, 3:4], s_[:, 2:3])
                yield vts(MS[:, t, :], MS[:, t, :], s_[:, 3:4], 2.5, MUL, MUL)

            Q.together([routed(0), routed(1)])
            tm_ = tq = Q.now("v")
            a = mmi(ps[1][:, 0:64], TRI, SL[:, 0, :], True, True, tm_, tc, free[1])
            mm(ps[1][:, 64:128], TRI, SL[:, 1, :], True, False)
            a = mmi(ps[1][:, 64:128], ones[:, :], SL[:, 0, :], False, True)
            a = stt(fl(RK), ps[1][:, 0:128], 1.0, fl(SL), ADD, MUL, a)
            free[1] = a
            a = vts(fl(RK), fl(RK), -1.0, None, ADD, None, a)
            a = vts(fl(GT), fl(RK), float(CAP), None, ALU.is_ge, None, a)
            b_ = vtt(fl(OVW), fl(GT), fl(MS), MUL, a, tq)
            a = mmi(ps[1][:, 0:64], ones[:, :], GT[:, 0, :], True, False, b_, free[1])
            a = mmi(ps[1][:, 0:64], ones[:, :], GT[:, 1, :], False, True)
            b_ = red(sv[:, 4:5], ps[1][:, 0:64], ADD, a)
            vcopy(flag[:, 73 * l:73 * l + 64], ps[1][:, 0:64])
            free[1] = red(GS[:, 0, :], ps[1][:, 0:64].rearrange("p (g k) -> p g k", k=8), ADD)
            vcopy(flag[:, 73 * l + 64:73 * l + 72], GS[:, 0, :])
            tflag = vcopy(flag[:, 73 * l + 72:73 * l + 73], sv[:, 4:5])

            bfree = [None, None]
            sel_t = {}
            gat = {}

            def select(q):
                r = q % 2
                for t in range(2):
                    sv_ = SEL[:, r, t, :].rearrange("p (e c) -> p e c", c=64)
                    a = vtt(sv_, bc(IOTA, 8, 1), bc(RK[:, t, 8 * q:8 * q + 8], 64, 2), ALU.is_equal, bfree[r])
                    wv = SEW[:, r, t, :].rearrange("p (e c) -> p e c", c=64)
                    a = vtt(wv, sv_, bc(MS[:, t, 8 * q:8 * q + 8], 64, 2), MUL, a, bfree[r], e="g")
                sel_t[q] = [a, Q.now("v")]

            def gather(q, k):
                r = q % 2
                b = bank((0, 1, 2, 3))
                mm(ps[b][:, :], X[:, 0, 128 * k:128 * k + 128], SEL[:, r, 0, :], True, False, free[b], sel_t[q])
                a = mmi(ps[b][:, :], X[:, 1, 128 * k:128 * k + 128], SEL[:, r, 1, :], False, True)
                free[b] = act(XG[:, r, k, :], ps[b][:, :], ACT.Identity, a, bfree[r], scale=cscale[:, k:k + 1],
                              bias=cshift[:, k:k + 1])
                gat[q] = free[b]

            hid, hfree, tts, ttfree, ys, yfree, downs = {}, [None] * 2, {}, [None] * 2, {}, [None] * 2, {}

            def up(j):
                q, r = j // 4, j % 2
                half = lambda i: (lambda sl: sl.rearrange("p (k n) -> p k n", n=512)[:, :, 256 * i:256 * i + 256])
                got = []
                for s in range(2):
                    n = 2 * j + s
                    got.append(weights((half(0), A["moe_w_gate_2"][l, n].rearrange("(k p) n -> p k n", p=128)),
                                       (half(1), A["moe_w_up_2"][l, n].rearrange("(k p) n -> p k n", p=128))))
                b = bank((0, 1, 2, 3))
                for k in range(8):
                    for s in range(2):
                        i, slot, tw = got[s]
                        x0 = 128 * (j % 4) + 64 * s
                        f = mmi if k == 7 else mm
                        tm = f(ps[b][64 * s:64 * s + 64, :], XG[:, q % 2, k, x0:x0 + 64],
                               slot.rearrange("p (k n) -> p k n", n=512)[:, k, :], k == 0, k == 7, tw, free[b], gat[q])
                release(got[0][0])
                release(got[1][0])
                if j % 4 == 3:
                    bfree_gather[q % 2] = tm
                a = act(SGT[:, r, :], ps[b][:, 0:256], ACT.Silu, tm, hid.get(j - 2))
                free[b] = hid[j] = vtt(HID[:, r, :], SGT[:, r, :], ps[b][:, 256:512], MUL, a, hfree[r])

            bfree_gather = [None, None]

            def turn(j):
                q, r = j // 4, j % 2
                b = bank((0, 1, 2, 3))
                for f in range(2):
                    tr(ps[b][:, 128 * f:128 * f + 128], HID[:, r, 128 * f:128 * f + 128], hid[j], free[b], ttfree[r])
                for t in range(2):
                    x0 = 128 * (j % 4)
                    tm = tr(ps[b][:, 256 + 128 * t:384 + 128 * t], SEW[:, q % 2, t, x0:x0 + 128])
                hfree[r] = tm
                if j % 4 == 3:
                    bfree[q % 2] = [tm, bfree_gather[q % 2]]
                free[b] = tts[j] = copy("a", TT[:, r, :], ps[b][:, :], tm, ttfree[r])

            def down(j):
                r = j % 2
                i, slot, tw = weights((lambda sl: sl.rearrange("p (k n) -> p k n", n=1024),
                                       A["moe_w_down_2"][l, 2 * j:2 * j + 2].rearrange("e (k p) n -> p (e k) n", p=128)))
                wt = slot.rearrange("p (k n) -> p k n", n=1024)
                for h in range(2):
                    b = bank((0, 1, 2, 3))
                    for f in range(2):
                        for s in range(2):
                            fn = mmi if f == 1 else mm
                            tm = fn(ps[b][64 * s:64 * s + 64, :], TT[:, r, 128 * f + 64 * s:128 * f + 64 * s + 64],
                                    wt[:, 2 * s + f, 512 * h:512 * h + 512], f == 0, f == 1, tw, tts[j], free[b])
                    free[b] = copy("v", YB[:, r, 512 * h:512 * h + 512], ps[b][:, :], tm, yfree[r])
                ys[j] = free[b]
                release(i)

            def scatter(j):
                r = j % 2
                for t in range(2):
                    for h in range(2):
                        tm = op("p", lambda e, o=ps[4 + 2 * t + h][:, :], a=TT[:, r, 256 + 128 * t:384 + 128 * t],
                                b=YB[:, r, 512 * h:512 * h + 512]:
                                e.matmul(o, a, b, start=False, stop=j == 31, skip_group_check=True), ys[j])
                yfree[r] = ttfree[r] = tm

            select(0)
            for k in range(8):
                gather(0, k)
            for j in range(32 + 3):
                q = j // 4
                if j < 32:
                    up(j)
                    if j % 4 == 1 and q < 7:
                        select(q + 1)
                if 2 <= j < 34:
                    down(j - 2)
                if j >= 3:
                    scatter(j - 3)
                if 1 <= j < 33:
                    turn(j - 1)
                if j < 32 and q < 7:
                    for k in ((), (0, 1), (2, 3, 4), (5, 6, 7))[j % 4]:
                        gather(q + 1, k)
            fence()
            top[0] = base
            general(l, OVW, tflag)
            top[0] = 0
            Y = Yh[0] = carve(4, 1024)
            for t in range(2):
                for h in range(2):
                    copy("va"[h], Y[:, t, 512 * h:512 * h + 512], ps[4 + 2 * t + h][:, :])
            fence()

        def general(l, OVW, tflag):
            SG, HI = carve(512), carve(512)
            WB, CW = carve(2, 128), carve(256)
            outer = Q.now("p")
            saved = Q.enter_if(flag[0:1, 73 * l + 72:73 * l + 73], tflag, f"g{l}")
            saved_jobs, saved_rel = jobs[0], dict(released)
            Q.wait_outer("s", saved, outer)
            jobs[0] = 0
            released.clear()
            h2 = lambda k: HT[:, k, 0:256]
            half = lambda i: (lambda sl: sl[:, 2048 * i:2048 * i + 2048].rearrange("p (k n) -> p k n", n=256))

            def expert(n):
                i, slot, tw = weights((half(0), A["moe_w_gate_2"][l, n].rearrange("(k p) n -> p k n", p=128)),
                                      (half(1), A["moe_w_up_2"][l, n].rearrange("(k p) n -> p k n", p=128)))
                i2, slot2, tw2 = weights((lambda sl: sl[:, 0:2048].rearrange("p (k n) -> p k n", n=1024),
                                          A["moe_w_down_2"][l, n].rearrange("(k p) n -> p k n", p=128)))
                tv = vcopy(WB, bc(OVW[:, :, n], 128, 2))
                for t in range(2):
                    tm = mmi(ps[2][:, 128 * t:128 * t + 128], WB[:, t, :], ident[:, :], True, True, tv)
                vcopy(CW, ps[2][:, 0:256], tm)
                tok = []
                for g in range(2):
                    wt = half(g)(slot)
                    for m in range(2):
                        for k in range(8):
                            f = mmi if k == 7 else mm
                            tm = f(ps[g][:, 256 * m:256 * m + 256], wt[:, k, 128 * m:128 * m + 128], h2(k),
                                   k == 0, k == 7, tw)
                    tok.append(tm)
                release(i)
                a = act(SG, ps[0][:, :], ACT.Silu, tok[0])
                t = vtt(SG, SG, ps[1][:, :], MUL, a, tok[1])
                hv = HI.rearrange("p (f t) -> p f t", t=256)
                t = vtt(hv, SG.rearrange("p (f t) -> p f t", t=256), bc(CW, 2, 1), MUL, t)
                wt = slot2[:, 0:2048].rearrange("p (k n) -> p k n", n=1024)
                for tt_ in range(2):
                    for h in range(2):
                        for f in range(2):
                            op("p", lambda e, o=ps[4 + 2 * tt_ + h][:, :], a=hv[:, f, 128 * tt_:128 * tt_ + 128],
                               b=wt[:, f, 512 * h:512 * h + 512]:
                               e.matmul(o, a, b, start=False, stop=True, skip_group_check=True), tw2, t)
                release(i2)

            def all_done():
                toks = [Q.now(e) for e in "pvag"] + [Q.now("small")]
                for e in "pvags":
                    Q.wait(e, toks)

            for n in range(NEXP):
                if n % 8 == 0:
                    group = Q.enter_branch()
                inner = Q.enter_branch()
                jobs[0] = 0
                released.clear()
                for i in range(8):
                    free[i] = None
                expert(n)
                all_done()
                Q.leave_branch(inner, flag[0:1, 73 * l + n:73 * l + n + 1])
                if n % 8 == 7:
                    Q.leave_branch(group, flag[0:1, 73 * l + 64 + n // 8:73 * l + 65 + n // 8])
            Q.leave_if(saved)
            jobs[0] = saved_jobs
            released.clear()
            released.update(saved_rel)
            for i in range(8):
                free[i] = None

        def second_layer(l):
            top[0] = 0
            cur[0] = 2 + l
            for half in range(2):
                top[0] = 0
                cs_ = cstat(8)
                t = vts(cs_, M()[:, 24 * half + 8:24 * half + 16, 0], 1.0, None, ADD, None)
                Q.wait("a", [t])
                transposed(range(2), False, lambda t: cs_, lambda t: M()[:, 24 * half:24 * half + 8, 0])
                top[0] = 0
                if half == 0:
                    (moba_gla if l == 0 else deltanet)()
                    residual_ln(2, "lmg", "lmb", l)
                else:
                    moe(l)
                    residual_ln(5, "lfg", "lfb", l)

        for l in range(2):
            top[0] = 0
            cur[0] = l
            if l == 0:
                fill["left"] = [(0, j) for j in range(12)]
                fill_rest(0)
                fence()
                fill["left"] = [(m, j) for m in (1, 2, 3) for j in range(12)]
            tiles = range(4) if l == 0 else range(2)
            for half in range(2):
                top[0] = 0
                tl = range(4) if half == 0 else tiles
                cs_ = cstat(16)
                for w in range(2):
                    scaled(cs_[:, 8 * w:8 * w + 8], 3 * half + 1, w, ("npm", "npf")[half], l)
                Q.wait("v", [Q.now("v")])
                Q.wait("a", [Q.now("v")])
                transposed(tl, True, lambda t: cs_[:, 8 * (t // 2):8 * (t // 2) + 8],
                           lambda t: M()[:, 24 * half:24 * half + 8, t // 2])
                top[0] = 0
                if half == 0:
                    (even_mixer if l == 0 else odd_mixer)()
                    residual_rms(2, "nqm", l, tiles)
                else:
                    conv_ffn(l, tiles)
                    residual_rms(5, "nqf", l, tiles)

        for l in range(2):
            second_layer(l)

        t = Q.dma("s", "outs", out.rearrange("a (t p) d -> p (a t) d", p=128), X[:, 0:2, :], Q.now("v"), Q.now("a"))
        Q.wait("s", [t])

        block = ctx.enter_context(nc.Block())

        @block.tensor
        def _(e):
            for f in Q.q["p"]:
                f(e)

        @block.vector
        def _(e):
            for f in Q.q["v"]:
                f(e)

        @block.scalar
        def _(e):
            for f in Q.q["a"]:
                f(e)

        @block.gpsimd
        def _(e):
            for f in Q.q["g"]:
                f(e)

        @block.sync
        def _(e):
            for f in Q.q["s"]:
                f(e)


def shape_constants():
    i = np.arange(128)
    c = {"cst": np.concatenate([np.eye(128), i[:, None] < i[None, :], np.broadcast_to(np.arange(64), (128, 64)),
                                i[:, None] % 32 == np.arange(4)[None, :]], 1)
         .astype(np.float32)}
    t = np.arange(256)
    inv = (np.float32(10000.0) ** (-np.arange(16, dtype=np.float32) / np.float32(16))).astype(np.float32)
    ang = np.concatenate([(t // 64).astype(np.float32)[:, None] * inv, (t % 64).astype(np.float32)[:, None] * inv], 1)
    c["rope"] = np.concatenate([np.cos(ang), np.sin(ang)], 1).astype(np.float32)
    h = np.zeros((2, 128, 17, 128), np.float32)
    i = np.arange(128)
    s, p = i[:, None], i[None, :]
    for lv in range(7):
        m = 64 >> lv
        blk, right = p // (2 * m), (p // m) % 2
        mid = blk * 2 * m + m
        h[0, :, lv] = np.where(right == 1, (s >= mid) & (s <= p), (s > p) & (s < mid))
        sb_, tb_ = s // (2 * m), p // (2 * m)
        h[0, :, 9 + lv] = (sb_ == tb_) & ((s // m) % 2 == 0) & ((p // m) % 2 == 1)
    h[0, :, 7] = s <= p
    h[0, :, 8] = s > p
    h[0, :, 16] = s == p
    h[1] = h[0][::-1, :, ::-1]
    c["hgc"] = h.reshape(2, 128, 17 * 128)
    return c


def more_constants(c):
    i = np.arange(128)
    s, p = i[:, None], i[None, :]
    g = np.zeros((128, 14, 128), np.float32)
    same = (s // 64) == (p // 64)
    g[:, 0] = same & (s <= p)
    g[:, 1] = same & (s > p)
    for lv in range(6):
        m = 1 << lv
        low = (s // (2 * m) == p // (2 * m)) & ((s // m) % 2 == 1) & ((p // m) % 2 == 0)
        g[:, 2 + lv] = low
        g[:, 8 + lv] = low.T
    c["gdc"] = g.reshape(128, 14 * 128)


def bucket_of(d):
    d = np.maximum(d, 0)
    logd = np.log(np.maximum(d, 1).astype(np.float32) / np.float32(16)).astype(np.float32)
    large = 16 + (logd / np.float32(np.log(2048 / 16)) * np.float32(16)).astype(np.int32)
    return np.where(d < 16, d, np.minimum(large, 31))


def more_arrays(A, I):
    more_constants(A)
    t = np.arange(256)
    dist = t[:, None] - t[None, :]
    own = dist >= 0
    b2 = np.full((4, 256, 256), -1e30, np.float32)
    b2[:, own] = I["rpe_bias_2"].T[:, bucket_of(dist)[own]]
    A["bias2"] = b2
    for name in ("ada_w_2", "ev_w_in_2", "ev_gk_w2_2", "ev_w_out_2", "od_w_in_2", "od_w_out_2", "moe_router_w_2",
                 "moe_w_gate_2", "moe_w_up_2", "moe_w_down_2", "sh_w_gate_2", "sh_w_up_2", "sh_w_down_2"):
        A[name] = I[name]


def kernel(**inputs):
    import concourse.bacc as _bacc
    from concourse.bass_utils import run_bass_kernel_spmd as _run

    I = {k: np.asarray(v) for k, v in inputs.items()}
    A = shape_constants()

    def cols(a):
        a = np.asarray(a, np.float32).reshape(-1, 128)
        return a.T

    A["colp"] = np.ascontiguousarray(np.concatenate([
        cols(I["c"]), cols(I["c_ctx"]), cols(I["c_2"]), cols(I["norm_pre_mix"]), cols(I["norm_post_mix"]),
        cols(I["norm_pre_ffn"]), cols(I["norm_post_ffn"]), cols(I["b_mod"]), cols(I["ada_b_2"]),
        cols(I["ln_mix_g_2"]), cols(I["ln_mix_b_2"]), cols(I["ln_ffn_g_2"]), cols(I["ln_ffn_b_2"]),
        cols(I["ffn_conv_w"]), cols(I["ffn_conv_b"]), cols(I["od_conv_w_2"])], 1))
    A["rowp"] = np.concatenate([I[k].reshape(1, -1) for k in (
        "even_q_norm", "even_k_norm", "hgrn_out_norm", "ev_gk_b_2", "ev_norm_2", "od_norm_2",
        "od_a_log_2", "od_dt_bias_2", "moe_router_b_2")], 1)
    t = np.arange(256)
    r, cc = t // 64, t % 64
    dy = r[None, :] - r[:, None] + 7
    dx = cc[None, :] - cc[:, None] + 15
    c0 = np.clip(cc - 8, 0, 48)[:, None]
    inside = (cc[None, :] >= c0) & (cc[None, :] < c0 + 16)
    b1 = np.full((16, 256, 256), -1e30, np.float32)
    b1[:, inside] = I["odd_rpb"][0][:, dy[inside], dx[inside]]
    A["bias1"] = b1
    for name in ("x", "ctx", "w_mod", "even_w_in", "even_w_out", "odd_w_qkv", "odd_w_out", "ffn_w_up", "ffn_w_down"):
        A[name] = I[name]
    more_arrays(A, I)

    nc = _bacc.Bacc("TRN2", target_bir_lowering=False, num_devices=1)
    arrays, aps = {}, {}
    for name, a in A.items():
        a = np.ascontiguousarray(a)
        arrays[f"in_{name}"] = a
        aps[name] = nc.dram_tensor(f"in_{name}", a.shape, mybir.dt.from_np(a.dtype), kind="ExternalInput").ap()
    o = nc.dram_tensor("out_0", [1, 256, 1024], F32, kind="ExternalOutput").ap()
    program(nc, aps, o)
    r = _run(nc, [arrays], core_ids=[0])
    return r.results[0]["out_0"]
```
